# Optimizing a Trainium2 kernel written in Bass

```python
import math
import jax, jax.numpy as jnp
from jax import lax
import numpy as np

D_MODEL = 2048
BATCH = 1
SEQ = 256
DEPTH = 2

CHUNK = 64
Q_BLOCK = 128
EPS = 1e-6

DA_HEADS = 6
DA_QK = 64
DA_V = 128
MLA_HEADS = 6
MLA_Q_RANK = 512
MLA_KV_RANK = 256
MLA_NOPE = 128
MLA_ROPE = 64
MLA_V = 128
ROPE_THETA = 10000.0
SG_GROUPS = 4
SG_CH = 128
SG_LEN = 128
D_FF = 5632
CONV_W = 3

DA_WIDTH = DA_HEADS * DA_V
MLA_WIDTH = MLA_HEADS * MLA_V
SG_WIDTH = SG_GROUPS * SG_CH
D_MIX = DA_WIDTH + MLA_WIDTH + SG_WIDTH

SPLITS = (DA_HEADS * 2 * DA_QK, DA_HEADS * 2 * DA_QK, DA_WIDTH,
          MLA_Q_RANK, MLA_KV_RANK, MLA_ROPE, SG_WIDTH, SG_WIDTH)
IN_COLS = sum(SPLITS)
SPLIT_IDX = tuple(int(i) for i in np.cumsum(SPLITS)[:-1])
ALIBI_SLOPES = tuple(2.0 ** (-8.0 * (h + 1) / DA_HEADS) for h in range(DA_HEADS))

kernel_name = 'hymba_style_diffattn_mla_sgu_convffn_adaln'

def rms_norm(x, gain=None):
    xf = x.astype(jnp.float32)
    y = xf * lax.rsqrt(jnp.mean(xf * xf, axis=-1, keepdims=True) + EPS)
    if gain is not None:
        y = y * gain.astype(jnp.float32)
    return y.astype(x.dtype)

def rope_cos_sin(pos):
    half = MLA_ROPE // 2
    inv = ROPE_THETA ** (-jnp.arange(half, dtype=jnp.float32) / half)
    ang = pos.astype(jnp.float32)[..., None] * inv
    return jnp.cos(ang)[:, :, None, :], jnp.sin(ang)[:, :, None, :]

def apply_rope(x, cos, sin):
    xf = x.astype(jnp.float32)
    x1, x2 = jnp.split(xf, 2, axis=-1)
    return jnp.concatenate([x1 * cos - x2 * sin, x2 * cos + x1 * sin], axis=-1).astype(x.dtype)

def to_heads(t):
    return t.transpose(0, 2, 1, 3)

def chunk_causal_attention(qs, ks, v, coefs, alibi=None):
    B, H, S, _ = v.shape
    nb = S // Q_BLOCK
    scale = qs[0].shape[-1] ** -0.5
    key_chunk = jnp.arange(S) // CHUNK
    blocks = lambda t: t.reshape(B, H, nb, Q_BLOCK, t.shape[-1]).transpose(2, 0, 1, 3, 4)
    q_blocks = tuple(blocks(q) for q in qs)
    if alibi is not None:
        slopes, pos = alibi
        posf = pos.astype(jnp.float32)
        pos_blocks = posf.reshape(B, nb, Q_BLOCK).transpose(1, 0, 2)
    else:
        pos_blocks = jnp.zeros((nb, B, Q_BLOCK), jnp.float32)

    def step(args):
        qb, pb, ib = args
        q_chunk = (ib * Q_BLOCK + jnp.arange(Q_BLOCK)) // CHUNK
        mask = key_chunk[None, :] <= q_chunk[:, None]
        bias = 0.0
        if alibi is not None:
            dist = jnp.abs(pb[:, :, None] - posf[:, None, :])
            bias = -slopes[None, :, None, None] * dist[:, None]
        probs = 0.0
        for q_i, k_i, c_i in zip(qb, ks, coefs):
            s = jnp.einsum('bhqd,bhkd->bhqk', q_i, k_i).astype(jnp.float32) * scale + bias
            s = jnp.where(mask, s, -jnp.inf)
            probs = probs + c_i * jax.nn.softmax(s, axis=-1)
        return jnp.einsum('bhqk,bhkd->bhqd', probs.astype(v.dtype), v)

    out = lax.map(step, (q_blocks, pos_blocks, jnp.arange(nb)))
    return out.transpose(1, 2, 0, 3, 4).reshape(B, H, S, v.shape[-1])

def diff_attention(q, k, v, pos, slopes, q_gain, k_gain, lq1, lk1, lq2, lk2, head_gain, lam_init):
    B, S, _ = q.shape
    q = rms_norm(q.reshape(B, S, DA_HEADS, 2, DA_QK), q_gain)
    k = rms_norm(k.reshape(B, S, DA_HEADS, 2, DA_QK), k_gain)
    v = v.reshape(B, S, DA_HEADS, DA_V)
    lam = (jnp.exp(jnp.sum(lq1 * lk1)) - jnp.exp(jnp.sum(lq2 * lk2)) + lam_init).astype(jnp.float32)
    o = chunk_causal_attention(
        (to_heads(q[..., 0, :]), to_heads(q[..., 1, :])),
        (to_heads(k[..., 0, :]), to_heads(k[..., 1, :])),
        to_heads(v), (1.0, -lam), alibi=(slopes, pos))
    o = rms_norm(o, head_gain[:, None, :]) * (1.0 - lam_init)
    return o.transpose(0, 2, 1, 3).reshape(B, S, DA_WIDTH)

def latent_attention(q_a, kv_a, k_rope, cos, sin, q_a_gain, w_uq, kv_a_gain, w_ukv, q_gain, k_gain):
    B, S, _ = q_a.shape
    q = (rms_norm(q_a, q_a_gain) @ w_uq).reshape(B, S, MLA_HEADS, MLA_NOPE + MLA_ROPE)
    kv = (rms_norm(kv_a, kv_a_gain) @ w_ukv).reshape(B, S, MLA_HEADS, MLA_NOPE + MLA_V)
    k_nope, v = kv[..., :MLA_NOPE], kv[..., MLA_NOPE:]
    k_r = jnp.broadcast_to(k_rope[:, :, None, :], (B, S, MLA_HEADS, MLA_ROPE))
    k = jnp.concatenate([k_nope, k_r], axis=-1)
    q = rms_norm(q, q_gain)
    k = rms_norm(k, k_gain)
    q = jnp.concatenate([q[..., :MLA_NOPE], apply_rope(q[..., MLA_NOPE:], cos, sin)], axis=-1)
    k = jnp.concatenate([k[..., :MLA_NOPE], apply_rope(k[..., MLA_NOPE:], cos, sin)], axis=-1)
    o = chunk_causal_attention((to_heads(q),), (to_heads(k),), to_heads(v), (1.0,))
    return o.transpose(0, 2, 1, 3).reshape(B, S, MLA_WIDTH)

def spatial_gating(u, v, v_gain, w_s, b_s):
    B, S, _ = u.shape
    u = jax.nn.gelu(u).reshape(B, S, SG_GROUPS, SG_CH)
    v = rms_norm(jax.nn.gelu(v).reshape(B, S, SG_GROUPS, SG_CH), v_gain)
    v = v.reshape(B, S // SG_LEN, SG_LEN, SG_GROUPS, SG_CH)
    w = w_s * jnp.tril(jnp.ones((SG_LEN, SG_LEN), w_s.dtype))
    s = jnp.einsum('gts,bnsgc->bntgc', w, v) + b_s.T[None, None, :, :, None]
    return (u * s.reshape(B, S, SG_GROUPS, SG_CH)).reshape(B, S, SG_WIDTH)

def conv_ffn(h, w_up, conv_w, conv_b, w_down):
    a = h @ w_up
    S = a.shape[1]
    ap = jnp.pad(a, ((0, 0), (CONV_W - 1, 0), (0, 0)))
    y = conv_b + a * conv_w[CONV_W - 1]
    for j in range(CONV_W - 1):
        y = y + ap[:, j:j + S] * conv_w[j]
    g, val = jnp.split(y, 2, axis=-1)
    return (jax.nn.silu(g) * val) @ w_down

def setup_inputs(seed: int = 0) -> dict:
    key = jax.random.key(seed)
    keys = jax.random.split(key, 32)
    counter = [0]

    def nxt():
        k = keys[counter[0]]
        counter[0] += 1
        return k

    def nrm(shape, scale):
        return jax.random.normal(nxt(), shape, jnp.float32) * scale

    def gain(shape):
        return 1.0 + nrm(shape, 0.02)

    L, D = DEPTH, D_MODEL
    x = nrm((BATCH, SEQ, D), 1.0)
    c = nrm((BATCH, D), 1.0)
    offset = jax.random.randint(nxt(), (BATCH, 1), 0, 1024, jnp.int32)
    positions = offset + jnp.arange(SEQ, dtype=jnp.int32)[None, :]
    return {
        'x': x,
        'c': c,
        'positions': positions,
        'w_ada': nrm((L, D, 6 * D), 0.01),
        'b_ada': nrm((L, 6 * D), 0.01),
        'w_in': nrm((L, D, IN_COLS), D ** -0.5),
        'da_q_gain': gain((L, DA_QK)),
        'da_k_gain': gain((L, DA_QK)),
        'da_lq1': nrm((L, DA_QK), 0.1),
        'da_lk1': nrm((L, DA_QK), 0.1),
        'da_lq2': nrm((L, DA_QK), 0.1),
        'da_lk2': nrm((L, DA_QK), 0.1),
        'da_head_gain': gain((L, DA_HEADS, DA_V)),
        'mla_q_a_gain': gain((L, MLA_Q_RANK)),
        'mla_w_uq': nrm((L, MLA_Q_RANK, MLA_HEADS * (MLA_NOPE + MLA_ROPE)), MLA_Q_RANK ** -0.5),
        'mla_kv_a_gain': gain((L, MLA_KV_RANK)),
        'mla_w_ukv': nrm((L, MLA_KV_RANK, MLA_HEADS * (MLA_NOPE + MLA_V)), MLA_KV_RANK ** -0.5),
        'mla_q_gain': gain((L, MLA_NOPE + MLA_ROPE)),
        'mla_k_gain': gain((L, MLA_NOPE + MLA_ROPE)),
        'sg_v_gain': gain((L, SG_GROUPS, SG_CH)),
        'sg_w': nrm((L, SG_GROUPS, SG_LEN, SG_LEN), SG_LEN ** -0.5),
        'sg_b': gain((L, SG_GROUPS, SG_LEN)),
        'w_out': nrm((L, D_MIX, D), D_MIX ** -0.5),
        'ffn_w_up': nrm((L, D, 2 * D_FF), D ** -0.5),
        'ffn_conv_w': nrm((L, CONV_W, 2 * D_FF), CONV_W ** -0.5),
        'ffn_conv_b': nrm((L, 2 * D_FF), 0.01),
        'ffn_w_down': nrm((L, D_FF, D), D_FF ** -0.5),
    }

def reference(x, c, positions, w_ada, b_ada, w_in, da_q_gain, da_k_gain, da_lq1, da_lk1,
              da_lq2, da_lk2, da_head_gain, mla_q_a_gain, mla_w_uq, mla_kv_a_gain, mla_w_ukv,
              mla_q_gain, mla_k_gain, sg_v_gain, sg_w, sg_b, w_out, ffn_w_up, ffn_conv_w,
              ffn_conv_b, ffn_w_down):
    cond = jax.nn.silu(c)
    slopes = jnp.asarray(ALIBI_SLOPES, jnp.float32)
    cos, sin = rope_cos_sin(positions)
    for l in range(DEPTH):
        mod = (cond @ w_ada[l] + b_ada[l])[:, None, :]
        sh1, sc1, g1, sh2, sc2, g2 = jnp.split(mod, 6, axis=-1)
        h = rms_norm(x) * (1.0 + sc1) + sh1
        z = h @ w_in[l]
        da_q, da_k, da_v, q_a, kv_a, k_rope, sg_u, sg_v = jnp.split(z, SPLIT_IDX, axis=-1)
        lam_init = 0.8 - 0.6 * math.exp(-0.3 * l)
        out_a = diff_attention(da_q, da_k, da_v, positions, slopes, da_q_gain[l], da_k_gain[l],
                               da_lq1[l], da_lk1[l], da_lq2[l], da_lk2[l], da_head_gain[l], lam_init)
        out_b = latent_attention(q_a, kv_a, k_rope, cos, sin, mla_q_a_gain[l], mla_w_uq[l],
                                 mla_kv_a_gain[l], mla_w_ukv[l], mla_q_gain[l], mla_k_gain[l])
        out_c = spatial_gating(sg_u, sg_v, sg_v_gain[l], sg_w[l], sg_b[l])
        mix = jnp.concatenate([out_a, out_b, out_c], axis=-1) @ w_out[l]
        x = x + g1 * mix
        h = rms_norm(x) * (1.0 + sc2) + sh2
        x = x + g2 * conv_ffn(h, ffn_w_up[l], ffn_conv_w[l], ffn_conv_b[l], ffn_w_down[l])
    return x


_drawn_inputs = setup_inputs


def setup_inputs(seed=0):
    import zlib

    import numpy as np

    out = dict(_drawn_inputs(seed))
    spreads = {}
    factors = {'b_ada': 3.642,
     'da_q_gain': 8.0,
     'da_k_gain': 8.0,
     'da_lq1': 8.0,
     'da_lk1': 6.446,
     'da_lq2': 6.615,
     'da_lk2': 8.0,
     'da_head_gain': 8.0,
     'mla_q_a_gain': 8.0,
     'mla_kv_a_gain': 8.0,
     'mla_q_gain': 8.0,
     'mla_k_gain': 8.0,
     'sg_v_gain': 8.0,
     'sg_b': 8.0,
     'ffn_conv_b': 8.0}
    for name, (base, spread) in spreads.items():
        noise = np.random.default_rng([zlib.crc32(name.encode()), seed]).standard_normal(out[name].shape)
        drawn = base * np.exp(spread * noise) if base else spread * noise
        out[name] = __import__('jax').numpy.asarray(drawn.astype(out[name].dtype))
    for name, factor in factors.items():
        out[name] = (out[name] * factor).astype(out[name].dtype)
    return out
```

```python
from contextlib import ExitStack

import numpy as np
import concourse.bass as bass
from concourse import mybir

ALU = mybir.AluOpType
ACT = mybir.ActivationFunctionType
AX_X = mybir.AxisListType.X
F32 = mybir.dt.float32
F32R = mybir.dt.float32r
I32 = mybir.dt.int32

P = 128
D = 2048
S = 256
L = 2
KC = D // P
NH = 6
DA_QK = 64
SGG = 4
D_FF = 5632
IN_COLS = 4160
EPS = 1e-6
ROPE_COL = 3072
LAM_INIT = [0.8 - 0.6 * float(np.exp(-0.3 * l)) for l in range(L)]
SLOPES = [2.0 ** (-8.0 * (h + 1) / NH) for h in range(NH)]
DA_SCALE = DA_QK ** -0.5
MLA_SCALE = 192 ** -0.5
KEYS = 384

C_ID, C_ONE, C_BLK, C_H0, C_H1, C_ROT, C_TRIL, C_MASK = (P * i for i in range(8))
C_SEL = C_MASK + KEYS
C_INV = C_SEL + 1
C_EPS = C_INV + 1
C_N = C_EPS + 1

G_C = 0
G_LAYER = 22


def gcol(l, what, i=0):
    at = {"qg": 0, "kg": 1, "hg": 2, "qa": 8, "kva": 12, "mqn": 14, "mqr": 15, "mkn": 16, "mkr": 17, "sgv": 18}
    return KC + G_LAYER * l + at[what] + i


COL_BADA = KC + G_LAYER * L
COL_CONV = COL_BADA + 96 * L
FFC = 2 * D_FF // P
N_COLS = COL_CONV + 4 * FFC * L

U_WIN, U_SMALL, U_WOUT = 32, 6, 16
PASS_BLOCKS = (8, 8, 6)
U_LAYER = U_WIN + U_SMALL + U_WOUT + sum(4 * b + 16 for b in PASS_BLOCKS)
B_LAYER = 16 + 8 + sum(2 * b + 8 for b in PASS_BLOCKS)
UNIT = 2048

A_LAYER = 24
A_PRO = 8
A_ALL = A_LAYER * L


def make_phases():
    g = A_PRO
    out = []
    for l in range(L):
        rows = []
        u, b = l * U_LAYER, l * B_LAYER

        def add(kind, p, first, n):
            nonlocal g, u, b
            i = 0
            while i < n:
                with_ada = g < A_ALL
                m = n - i
                if with_ada:
                    m = min(m, A_LAYER - g % A_LAYER)
                rows.append((kind, p, first + i, m, u, b, g if with_ada else None))
                if with_ada:
                    g += m
                u += 4 * m
                b += 2 * m
                i += m

        add("win", 0, 0, 6)
        add("win", 0, 6, 2)
        rows.append(("small", 0, 0, 1, u, b, None))
        u += U_SMALL
        add("wout", 0, 0, 4)
        pb = 0
        for p, nb in enumerate(PASS_BLOCKS):
            add("up", p, 0, nb)
            add("down", p, 0, 4)
            pb += nb
        assert u == (l + 1) * U_LAYER and b == (l + 1) * B_LAYER
        out.append(rows)
    assert g == A_ALL
    return out


J_N1, J_QA, J_KVA, J_SGV, J_DAQK, J_MQ, J_MK, J_O, J_N2 = 0, 1, 2, 3, 5, 11, 14, 17, 20
J_LAYER = 21
SUBS = [16, 2, 1, 1, 1] + [1] * 6 + [2] * 3 + [1] * 3 + [1] * 3 + [16]
SUB_LAYER = sum(SUBS)
T_N1, T_QA, T_KVA, T_SG, T_DA, T_N2 = 0, 16, 20, 22, 26, 32
T_LAYER = 48
E_KR, E_V, E_UKV, E_UQ, E_VT, E_SG, E_KROT, E_QROT = 0, 1, 4, 14, 23, 25, 27, 28
E_ACT, E_DVE = 25, 6


N_SMALL = 2 + L * (8 + 6 + 1 + 4 + 1 + 1 + 4) + 2
TURN = 2 * float(np.pi)
ROUND = 1.5 * 2.0 ** 23
TURN_PARTS = (6.28125, round((TURN - 6.28125) * 2 ** 21) / 2 ** 21, TURN - 6.28125 - round((TURN - 6.28125) * 2 ** 21) / 2 ** 21)
PI_ = 3.1415925


def bass_trunk(nc, consts, x, c, positions, w_ada, b_ada, w_in, da_q_gain, da_k_gain, da_lq1, da_lk1,
               da_lq2, da_lk2, da_head_gain, mla_q_a_gain, mla_w_uq, mla_kv_a_gain, mla_w_ukv,
               mla_q_gain, mla_k_gain, sg_v_gain, sg_w, sg_b, w_out, ffn_w_up, ffn_conv_w,
               ffn_conv_b, ffn_w_down, out):
    phases = make_phases()
    with ExitStack() as ctx:
        def sb(name, cols, dt=F32):
            return ctx.enter_context(nc.sbuf_tensor(name, [P, cols], dt))

        def sem(name):
            return ctx.enter_context(nc.semaphore(name))

        base = nc.sbuf_base
        arena = ctx.enter_context(nc.sbuf_tensor("arena", [P, 52 * 1024 - 256], F32))
        at = [(base + 31) // 32 * 32]
        end = at[0] + (52 * 1024 - 256) * 4

        def place(name, cols, dt=F32, offset=None):
            if offset is None:
                offset = at[0]
                at[0] += (cols * 4 + 31) // 32 * 32
                assert at[0] <= end, (name, at[0], end)
            return nc.alloc_sbuf_tensor_at(name, [P, cols], dt, offset=offset), offset

        raw, _ = place("raw", 4 * UNIT)
        whi, _ = place("whi", 2 * UNIT, F32R)
        wlo, _ = place("wlo", 2 * UNIT, F32R)
        ada, o_ada = place("ada", 2 * 1024)
        xT, _ = place("xT", KC * S)
        hhi, o_h = place("hhi", KC * S, F32R)
        hlo, _ = place("hlo", KC * S, F32R)
        mhi, o_m = place("mhi", KC * S, F32R)
        mlo, _ = place("mlo", KC * S, F32R)
        z, _ = place("z", 32 * S, offset=o_m)
        apro, _ = place("apro", 8 * 1024, offset=o_m)
        xs, _ = place("xs", 2 * D, offset=o_h)
        rows, _ = place("rows", 11 * P, offset=o_h + 4 * 2 * D)
        wsr, _ = place("wsr", L * 512, offset=o_h + 4 * (2 * D + 11 * P))
        posi, _ = place("posi", S + 2, I32, offset=o_h + 4 * (2 * D + 11 * P + L * 512))
        lamr, _ = place("lamr", L * 4 * DA_QK, offset=o_h + 4 * (2 * D + 11 * P + L * 512 + 264))
        ang, _ = place("ang", 2 * S, offset=o_h + 4 * (2 * D + 11 * P + L * 512 + 264 + 512))
        vda, _ = place("vda", NH * S, offset=o_h)
        mq, _ = place("mq", NH * S, offset=o_h + 4 * 1536)
        mk, _ = place("mk", NH * S, offset=o_h + 4 * 3072)
        mv, _ = place("mv", NH * S, offset=o_h + 4 * 4608)
        mqr, _ = place("mqr", 3 * S, offset=o_h + 4 * 6144)
        mkr, _ = place("mkr", 3 * S, offset=o_h + 4 * 6912)
        kr, _ = place("kr", S, offset=o_h + 4 * 7680)
        sqkr, _ = place("sqkr", S, offset=o_h + 4 * 7936)
        o_s = at[0]
        sc_s, _ = place("sc_s", 2 * 2 * KEYS)
        pr, _ = place("pr", 2 * KEYS)
        pt, _ = place("pt", 2 * KEYS)
        qahi, _ = place("qahi", 6 * S, F32R, offset=o_s)
        qalo, _ = place("qalo", 6 * S, F32R, offset=o_s + 4 * 6 * S)
        yg, _ = place("yg", 2 * S, offset=o_s)
        yv, _ = place("yv", 2 * S, offset=o_s + 4 * 2 * S)
        vt, _ = place("vt", 4 * S)
        con, _ = place("con", C_N)
        cols, _ = place("cols", N_COLS)
        mod, _ = place("mod", 96 * L)
        condr, _ = place("condr", KC * 32)
        bs, _ = place("bs", L * 512)
        wt, _ = place("wt", L * 512)
        dist, _ = place("dist", KEYS)
        cos, _ = place("cos", S)
        sin, _ = place("sin", S)
        sq, _ = place("sq", 2 * 512)
        r, _ = place("r", 2 * 512)
        T, _ = place("T", 4 * S)
        ya, _ = place("ya", 512)
        stat, _ = place("stat", 2 * 16)
        sml, _ = place("sml", 64)
        rt_tmp, _ = place("rt_tmp", S)

        bank = [ctx.enter_context(nc.psum_tensor(f"bank{i}", [P, 512], F32)) for i in range(8)]
        B_ADA, B_MOD, B_O, B_PT = bank[4], bank[5], bank[3], bank[2]

        def col(t, i, n=1):
            return t[:, i:i + n]

        def ch(t, k, n=1):
            return t[:, bass.ds(k * S, n * S)] if not isinstance(k, int) else t[:, k * S:(k + n) * S]

        ident, ones, blk = con[:, C_ID:C_ID + P], con[:, C_ONE:C_ONE + P], con[:, C_BLK:C_BLK + P]
        half = [con[:, C_H0:C_H0 + P], con[:, C_H1:C_H1 + P]]
        rot, tril = con[:, C_ROT:C_ROT + P], con[:, C_TRIL:C_TRIL + P]
        mask = con[:, C_MASK:C_MASK + KEYS]

        w_loaded = [sem(f"w_loaded{i}") for i in range(4)]
        ada_loaded = [sem(f"ada_loaded{i}") for i in range(8)]
        x_loaded, small_loaded, stored = sem("x_loaded"), sem("small_loaded"), sem("stored")
        unit_done, chunk0_done = sem("unit_done"), sem("chunk0_done")
        ada_used, mod_turned = sem("ada_used"), sem("mod_turned")
        sub_done, ring_full = sem("sub_done"), sem("ring_full")
        pro_full = sem("pro_full")
        sc_full, pt_full, o_full, fin_full = sem("sc_full"), sem("pt_full"), sem("o_full"), sem("fin_full")
        hi_ready, sq_ready, root_ready, t_high = sem("hi_ready"), sem("sq_ready"), sem("root_ready"), sem("t_high")
        ya_ready, ring_act, gelu_done, exp_done = sem("ya_ready"), sem("ring_act"), sem("gelu_done"), sem("exp_done")
        pt_ready, mh_ready, tap_ready, silu_done, a_high = (
            sem("pt_ready"), sem("mh_ready"), sem("tap_ready"), sem("silu_done"), sem("a_high"))
        lam_exp, cond_silu, trig_done = sem("lam_exp"), sem("cond_silu"), sem("trig_done")
        lo_ready, acc_free, t_ready, t_low = sem("lo_ready"), sem("acc_free"), sem("t_ready"), sem("t_low")
        mod_ready, applied, ring_dve, pro_free = sem("mod_ready"), sem("applied"), sem("ring_dve"), sem("pro_free")
        cond_ready, dve_order, sc_free, max_ready = sem("cond_ready"), sem("dve_order"), sem("sc_free"), sem("max_ready")
        p_ready, mh_low, a_ready, a_low = sem("p_ready"), sem("mh_low"), sem("a_ready"), sem("a_low")
        rope_in, mla_q_ready, fin_free = sem("rope_in"), sem("mla_q_ready"), sem("fin_free")
        lam_sum, ang_ready = sem("lam_sum"), sem("ang_ready")


        def job(l, j):
            return l * J_LAYER + j

        def sub(l, j):
            return l * SUB_LAYER + sum(SUBS[:j])

        def dropped(l, kind):
            return U_SMALL * (l + (kind != "win"))

        def residual_final(l, which, k):
            return 2 * (l * B_LAYER + (16 if which else -8)) + k + 1

        def first_of(l, row):
            same = [x_ for x_ in phases[l] if x_[:2] == row[:2]]
            return same[0] is row

        UQ_UNITS = range(U_WIN + 3, U_WIN + 6)

        def uq_views(u, t):
            src = raw[:, (u % 4) * UNIT:(u % 4) * UNIT + 8 * 192].rearrange("p (a n) -> p a n", n=192)
            o = (u % 2) * UNIT
            return ((src[:, :, 0:P], t[:, o:o + 8 * P].rearrange("p (a n) -> p a n", n=P)),
                    (src[:, :, P:192], t[:, o + 8 * P:o + 12 * P].rearrange("p (a n) -> p a n", n=64)))

        class Order:

            def __init__(self, eng, s):
                self.eng, self.s, self.n, self.plus = eng, s, 0, 0

            def after(self, ins):
                self.n += 1
                ins.then_inc(self.s, 1)
                self.eng.wait_ge(self.s, self.plus + self.n)

        JOB_SQ = {J_QA: [(z, 18 * S, 512), (z, 20 * S, 512)], J_KVA: [(z, 22 * S, 512)]}
        for v_ in range(2):
            JOB_SQ[J_SGV + v_] = [(z, (28 + 2 * v_) * S, 512)]
        for v_ in range(6):
            JOB_SQ[J_DAQK + v_] = [(z, 2 * v_ * S, 512)]
        for v_ in range(3):
            JOB_SQ[J_MQ + v_] = [(mq, 2 * v_ * S, 512), (mqr, v_ * S, S)]
            JOB_SQ[J_MK + v_] = [(mk, 2 * v_ * S, 512)]
            JOB_SQ[J_O + v_] = [(B_O, 0, 512)]
        JOB_W = {J_N1: (S, D), J_N2: (S, D), J_QA: (S, 512), J_KVA: (S, 256)}
        for v_ in range(2):
            JOB_W[J_SGV + v_] = (512, P)
        for v_ in range(6):
            JOB_W[J_DAQK + v_] = (512, DA_QK)
        for v_ in range(3):
            JOB_W[J_MQ + v_] = JOB_W[J_MK + v_] = (512, 192)
            JOB_W[J_O + v_] = (512, P)

        block = ctx.enter_context(nc.Block())

        @block.sync
        def _(sp):
            def load_unit(u, slot, kt, width, src):
                if not isinstance(u, int) or u >= 4:
                    sp.wait_ge(lo_ready, u - 3)
                dst = raw[:, slot * UNIT:slot * UNIT + kt * width].rearrange("p (k n) -> p k n", k=kt)
                sp.dma_start(dst, src).then_inc(w_loaded[slot], 16)

            def rows_of(w, k0, kt, c0, width):
                return w[k0:k0 + kt * P, bass.ds(c0, width)].rearrange("(k p) n -> p k n", p=P)

            sp.dma_start(xs[:, 0:2 * D].rearrange("p (t d) -> p t d", t=2),
                         x.rearrange("(t p) d -> p t d", p=P)).then_inc(x_loaded, 16)
            for l in range(L):
                for kind, p, first, n, u0, b0, g0 in phases[l]:
                    if kind == "small":
                        load_unit(u0, u0 % 4, 16, 64, rows_of(w_in[l], 0, 16, ROPE_COL, 64))
                        for v in range(2):
                            load_unit(u0 + 1 + v, (u0 + 1 + v) % 4, 2, 768, rows_of(mla_w_ukv[l], 0, 2, v * 768, 768))
                        for v in range(3):
                            load_unit(u0 + 3 + v, (u0 + 3 + v) % 4, 4, 384, rows_of(mla_w_uq[l], 0, 4, v * 384, 384))
                        continue

                    def body(i):
                        pb = sum(PASS_BLOCKS[:p])
                        for v in range(4):
                            b2, s = v // 2, v % 2
                            if kind == "win":
                                w, k0, kt, c0 = w_in[l], 8 * s * P, 8, (2 * (first + i) + b2) * 256 + 64 * (first >= 6)
                            elif kind == "wout":
                                w, k0, kt, c0 = w_out[l], 8 * s * P, 8, (2 * (first + i) + b2) * 256
                            elif kind == "up":
                                w, k0, kt, c0 = ffn_w_up[l], 8 * s * P, 8, (pb + first + i) * 256 + b2 * D_FF
                            else:
                                kt = PASS_BLOCKS[p]
                                w, k0, c0 = ffn_w_down[l], (2 * pb + s * kt) * P, (2 * (first + i) + b2) * 256
                            load_unit(u0 + 4 * i + v, (u0 + v) % 4, kt, 256, rows_of(w, k0, kt, c0, 256))

                    start = 0
                    if l == 0 and u0 == 0:
                        body(0)
                        start = 1
                    with sp.Fori(start, n) as i:
                        body(i)
            sp.wait_ge(fin_free, 8)
            sp.dma_start(out.rearrange("(t p) d -> p t d", p=P),
                         xs[:, 0:2 * D].rearrange("p (t d) -> p t d", t=2)).then_inc(stored, 16)
            sp.wait_ge(stored, 16)

        @block.gpsimd
        def _(pool):
            def part_of(l, q, c0):
                return w_ada[l, 2 * q * P:(2 * q + 2) * P, bass.ds(c0, 512)].rearrange("(k p) n -> p k n", p=P)

            for g in range(A_PRO):
                for q in range(8):
                    if g >= 1:
                        pool.wait_ge(ada_used, 8 * (g - 1) + q + 1)
                    pool.dma_start(apro[:, q * 1024:(q + 1) * 1024].rearrange("p (k n) -> p k n", k=2),
                                   part_of(0, q, g * 512)).then_inc(ada_loaded[q], 16)
            for l in range(L):
                for kind, p, first, n, u0, b0, g0 in phases[l]:
                    if g0 is None:
                        continue
                    with pool.Fori(0, n) as i:
                        for q in range(8):
                            pool.wait_ge(ada_used, 8 * (g0 + i) + q - 1)
                            pool.dma_start(ada[:, (q % 2) * 1024:(q % 2 + 1) * 1024].rearrange("p (k n) -> p k n", k=2),
                                           part_of(g0 // A_LAYER, q, (g0 % A_LAYER + i) * 512)).then_inc(
                                               ada_loaded[q % 2], 16)

        @block.tensor
        def _(pe):
            def mm(out_, lhsT, rhs, start, stop):
                return pe.matmul(out_, lhsT, rhs, start=start, stop=stop, skip_group_check=True)

            def three(out_, wh, wl, ah, al, start, stop):
                mm(out_, wh, ah, start, False)
                mm(out_, wh, al, False, False)
                return mm(out_, wl, ah, False, stop)

            pe.wait_ge(small_loaded, 16 * N_SMALL)
            pro = [0]

            def pro_bank():
                if pro[0] >= 4:
                    pe.wait_ge(pro_free, pro[0] - 3)
                pro[0] += 1
                return bank[(pro[0] - 1) % 4]

            b = pro_bank()
            last = pe.transpose(b[:, 0:60], rows[0:60, 0:P], ident[0:60, 0:60])
            for l in range(L):
                last = pe.transpose(b[:, 60 + 96 * l:156 + 96 * l], rows[0:96, (1 + l) * P:(2 + l) * P],
                                    ident[0:96, 0:96])
            last.then_inc(pro_full, 1)
            for l in range(L):
                b = pro_bank()
                for v in range(4):
                    t_ = 3 + 4 * l + v
                    last = pe.transpose(b[:, v * FFC:(v + 1) * FFC], rows[0:FFC, t_ * P:(t_ + 1) * P],
                                        ident[0:FFC, 0:FFC])
                last.then_inc(pro_full, 1)
            for l in range(L):
                b = pro_bank()
                for g in range(SGG):
                    last = pe.transpose(b[:, g * P:(g + 1) * P], wsr[:, l * 512 + g * P:l * 512 + (g + 1) * P], ident)
                last.then_inc(pro_full, 1)
            pe.wait_ge(x_loaded, 16)
            for k2 in range(KC // 2):
                b = pro_bank()
                for y in range(4):
                    k, t_ = 2 * k2 + y // 2, y % 2
                    last = pe.transpose(b[:, y * P:(y + 1) * P], xs[:, t_ * D + k * P:t_ * D + (k + 1) * P], ident)
                last.then_inc(pro_full, 1)

            def ada_part(g, q, slot, buf, lap):
                if q == 0 and not (isinstance(g, int) and g == 0):
                    pe.wait_ge(ya_ready, g)
                pe.wait_ge(ada_loaded[slot], lap)
                for j in range(2):
                    k = 2 * q + j
                    cg = k % 4
                    i_ = mm(B_ADA[32 * cg:32 * cg + 32, :], condr[:, k * 32:(k + 1) * 32],
                            buf[:, slot * 1024 + j * 512:slot * 1024 + (j + 1) * 512], k < 4, k >= KC - 4)
                i_.then_inc(ada_used, 1)

            def ada_turn(g):
                pe.wait_ge(ya_ready, g + 1)
                if not (isinstance(g, int) and g == 0):
                    pe.wait_ge(mod_ready, g)
                for v in range(4):
                    i_ = mm(B_MOD[:, v:v + 1], ya[:, v * P:(v + 1) * P], con[:, C_SEL:C_SEL + 1], True, True)
                i_.then_inc(mod_turned, 1)

            pe.wait_ge(cond_ready, 1)
            for g in range(A_PRO):
                for q in range(8):
                    ada_part(g, q, q, apro, 16 * (g + 1))
                    if q == 2 and g >= 1:
                        ada_turn(g - 1)
            ada_turn(A_PRO - 1)

            def ms(l, j, subs):
                g, n, total = job(l, j), 0, sum(len(x_) for x_ in subs)
                if g >= 2:
                    pe.wait_ge(root_ready, g - 1)
                for v, products in enumerate(subs):
                    pe.wait_ge(sq_ready, sub(l, j) + v + 1)
                    for m_, sq_, (o0, o1) in products:
                        i_ = mm(bank[6 + g % 2][:, o0:o1], m_, sq_, n == 0, n == total - 1)
                        n += 1
                    i_.then_inc(sub_done, 1)

            def sqr(l, j, v, w0, w1):
                o = ((sub(l, j) + v) % 2) * 512
                return sq[:, o + w0:o + w1]

            def ms_all(l, j):
                n = 1 if j in (J_N1, J_N2) else 2
                ms(l, j, [[(ones, sqr(l, j, v, y * S, (y + 1) * S), (0, S)) for y in range(n)] for v in range(SUBS[j])])

            def ms_each(l, j, m_):
                ms(l, j, [[(m_, sqr(l, j, 0, 0, 512), (0, 512))]])

            def ms_mq(l, v):
                ms(l, J_MQ + v, [[(ones, sqr(l, J_MQ + v, 0, 0, 512), (0, 512))],
                                 [(half[y], sqr(l, J_MQ + v, 1, 0, S), (y * S, (y + 1) * S)) for y in range(2)]])

            def ms_mk(l, v):
                ms(l, J_MK + v, [[(ones, sqr(l, J_MK + v, 0, 0, 512), (0, 512))]
                                 + [(half[0], sqkr[:, 0:S], (y * S, (y + 1) * S)) for y in range(2)]])

            def ring(l, e, b0):
                if e < 4:
                    pe.wait_ge(acc_free, 2 * b0)
                elif e - 4 < E_ACT:
                    pe.wait_ge(ring_act, l * E_ACT + e - 3)
                else:
                    pe.wait_ge(ring_dve, l * E_DVE + e - 4 - E_ACT + 1)
                return bank[e % 4]

            def attention_inputs(l, u0, b0):
                item = l * T_LAYER
                b = ring(l, E_KR, b0)
                pe.wait_ge(lo_ready, u0 + 1)
                o = (u0 % 2) * UNIT
                for k in range(KC):
                    i_ = three(b[:, 0:S], whi[:, o + k * 64:o + k * 64 + P], wlo[:, o + k * 64:o + k * 64 + P],
                               ch(hhi, k), ch(hlo, k), k == 0, k == KC - 1)
                i_.then_inc(ring_full, 1)
                ms_all(l, J_QA)
                ms_all(l, J_KVA)
                for v in range(3):
                    b = ring(l, E_V + v, b0)
                    for y in range(4):
                        k, t_ = 12 + 2 * v + y // 2, y % 2
                        i_ = pe.transpose(b[:, y * P:(y + 1) * P], z[:, k * S + t_ * P:k * S + (t_ + 1) * P], ident)
                    i_.then_inc(ring_full, 1)
                pe.wait_ge(t_low, item + T_KVA + 2)
                for v in range(2):
                    u = u0 + 1 + v
                    pe.wait_ge(lo_ready, u + 1)
                    o = (u % 2) * UNIT
                    for y in range(3):
                        b = ring(l, E_UKV + 5 * v + y, b0)
                        for k in range(2):
                            a = o + k * 768 + y * 256
                            i_ = three(b[:, 0:S], whi[:, a:a + P], wlo[:, a:a + P], ch(qahi, 4 + k), ch(qalo, 4 + k),
                                       k == 0, k == 1)
                        i_.then_inc(ring_full, 1)
                    for t_ in range(2):
                        b = ring(l, E_UKV + 5 * v + 3 + t_, b0)
                        for k in range(2):
                            def v_(t):
                                return t[:, o + k * 768:o + (k + 1) * 768].rearrange("p (h n) -> p h n", h=3)[:, :, P:256]
                            c0 = (4 + k) * S + t_ * P
                            i_ = three(b[:, 0:384], qahi[:, c0:c0 + P], qalo[:, c0:c0 + P], v_(whi), v_(wlo),
                                       k == 0, k == 1)
                        i_.then_inc(ring_full, 1)
                pe.wait_ge(t_low, item + T_QA + 4)
                for v in range(3):
                    u = u0 + 3 + v
                    pe.wait_ge(lo_ready, u + 1)
                    o = (u % 2) * UNIT
                    for y in range(3):
                        b = ring(l, E_UQ + 3 * v + y, b0)
                        for k in range(4):
                            a = o + ((2 * k + y) * P if y < 2 else (8 + k) * P)
                            i_ = three(b[:, 0:S], whi[:, a:a + P], wlo[:, a:a + P], ch(qahi, k), ch(qalo, k),
                                       k == 0, k == 3)
                        i_.then_inc(ring_full, 1)
                ms_each(l, J_SGV, ones)
                ms_each(l, J_SGV + 1, ones)
                ms_each(l, J_DAQK, blk)
                ms_each(l, J_DAQK + 1, blk)
                pe.wait_ge(applied, job(l, J_SGV + 1) + 1)
                for v in range(2):
                    b = ring(l, E_VT + v, b0)
                    for y in range(4):
                        k, t_ = 28 + 2 * v + y // 2, y % 2
                        i_ = pe.transpose(b[:, y * P:(y + 1) * P], z[:, k * S + t_ * P:k * S + (t_ + 1) * P], ident)
                    i_.then_inc(ring_full, 1)
                for v in range(2, 6):
                    ms_each(l, J_DAQK + v, blk)
                for v in range(2):
                    pe.wait_ge(ring_act, l * E_ACT + E_VT + v + 1)
                    b = ring(l, E_SG + v, b0)
                    for y in range(4):
                        g = 2 * v + y // 2
                        i_ = mm(b[:, y * P:(y + 1) * P], vt[:, (4 * v + y) * P:(4 * v + y + 1) * P],
                                wt[:, l * 512 + g * P:l * 512 + (g + 1) * P], True, True)
                    i_.then_inc(ring_full, 1)
                pe.wait_ge(rope_in, 4 * l + 1)
                b = ring(l, E_KROT, b0)
                mm(b[:, 0:S], rot, kr[:, 0:S], True, True).then_inc(ring_full, 1)

                def q_rot(v):
                    pe.wait_ge(rope_in, 4 * l + 2 + v)
                    b = ring(l, E_QROT + v, b0)
                    mm(b[:, 0:S], rot, ch(mqr, v), True, True).then_inc(ring_full, 1)

                ms_mq(l, 0)
                ms_mq(l, 1)
                q_rot(0)
                ms_mq(l, 2)
                q_rot(1)
                ms_mk(l, 0)
                q_rot(2)
                ms_mk(l, 1)
                ms_mk(l, 2)

            def score(l, i):
                h = i % NH
                if i == 0:
                    pe.wait_ge(ring_act, (l + 1) * E_ACT)
                    pe.wait_ge(ring_dve, (l + 1) * E_DVE)
                    pe.wait_ge(applied, job(l, J_DAQK + 5) + 1)
                else:
                    pe.wait_ge(sc_free, 12 * l + i)
                if i >= NH:
                    pe.wait_ge(mla_q_ready, 3 * l + h // 2 + 1)
                    pe.wait_ge(applied, job(l, J_MK + h // 2) + 1)
                for c0, c1, q0, nk in ((0, P, 0, P), (P, KEYS, P, S)):
                    if i < NH:
                        for y in range(2):
                            i_ = mm(bank[y][:, c0:c1], z[64 * y:64 * y + 64, h * S + q0:h * S + q0 + P],
                                    z[64 * y:64 * y + 64, (NH + h) * S:(NH + h) * S + nk], True, True)
                    else:
                        r0, c_ = 64 * (h % 2), (h // 2) * S
                        mm(bank[0][:, c0:c1], mq[:, h * S + q0:h * S + q0 + P], mk[:, h * S:h * S + nk], True, False)
                        i_ = mm(bank[0][:, c0:c1], mqr[r0:r0 + 64, c_ + q0:c_ + q0 + P],
                                mkr[r0:r0 + 64, c_:c_ + nk], False, True)
                i_.then_inc(sc_full, 1)

            def values(l, i):
                h, o = i % NH, (i % 2) * KEYS
                pe.wait_ge(p_ready, 12 * l + i + 1)
                if i >= 1:
                    pe.wait_ge(pt_ready, 12 * l + i)
                for c0 in (0, P, 2 * P):
                    i_ = pe.transpose(B_PT[:, c0:c0 + P], pr[:, o + c0:o + c0 + P], ident)
                i_.then_inc(pt_full, 1)
                pe.wait_ge(pt_ready, 12 * l + i + 1)
                if i % 2 == 0 and 2 <= i <= NH:
                    pe.wait_ge(t_ready, l * T_LAYER + T_DA + i)
                elif i % 2 == 0 and i > NH:
                    pe.wait_ge(mh_low, l * NH + i - NH)
                v_, d0 = (vda if i < NH else mv), (i % 2) * S
                mm(B_O[:, d0:d0 + S], v_[:, h * S:h * S + P], pt[:, o:o + S], True, False)
                mm(B_O[:, d0 + P:d0 + S], v_[:, h * S + P:(h + 1) * S], pt[:, o + S:o + KEYS], False, True).then_inc(
                    o_full, 1)

            def heads(l):
                for i in range(14):
                    if i < 12:
                        score(l, i)
                    if i % 2 == 1 and 3 <= i < 9:
                        ms_each(l, J_O + (i - 3) // 2, ones)
                    if 1 <= i <= 12:
                        values(l, i - 1)

            def unit(u, slot, b2, s, kt, rhs, waits, acc_wait, after_chunk):
                pe.wait_ge(lo_ready, u + 1)
                for c_ in range(2):
                    acc = bank[2 * b2 + c_][:, 0:S]
                    if s == 0 and acc_wait is not None:
                        pe.wait_ge(acc_free, acc_wait + c_)
                    for j in range(kt):
                        if waits is not None and c_ == 0:
                            waits(s * kt + j)
                        a = slot * UNIT + j * 256 + c_ * P
                        i_ = three(acc, whi[:, a:a + P], wlo[:, a:a + P], ch(rhs[0], s * kt + j),
                                   ch(rhs[1], s * kt + j), s == 0 and j == 0, s == 1 and j == kt - 1)
                    if c_ == 1:
                        i_.then_inc(unit_done, 1)
                    elif s == 1:
                        i_.then_inc(chunk0_done, 1)
                    after_chunk(c_)

            ADA_AT = {(0, 0): (0,), (0, 1): (1,), (1, 0): (2,), (1, 1): (3,), (2, 0): (4, 5), (2, 1): (6, 7)}

            for l in range(L):
                item = l * T_LAYER
                ms_all(l, J_N1)
                for row in phases[l]:
                    kind, p, first, n, u0, b0, g0 = row
                    if kind == "small":
                        attention_inputs(l, u0, b0)
                        heads(l)
                        continue
                    begins = first_of(l, row)
                    if kind == "up" and p == 0 and begins:
                        ms_all(l, J_N2)

                    def input_ready(k):
                        if kind == "win":
                            pe.wait_ge(t_low, item + T_N1 + k + 1)
                        elif kind == "up":
                            pe.wait_ge(t_low, item + T_N2 + k + 1)
                        elif kind == "wout" and k < NH:
                            pe.wait_ge(t_low, item + T_DA + k + 1)
                        elif kind == "wout" and k < 2 * NH:
                            pe.wait_ge(mh_low, l * NH + k - NH + 1)
                        elif kind == "down" and k % 2 == 0:
                            pe.wait_ge(a_low, l * (FFC // 4) + sum(PASS_BLOCKS[:p]) + k // 2 + 1)

                    def body(i, waits):
                        for b2 in range(2):
                            acc_wait = 2 * (b0 + 2 * i + b2) - 3
                            if isinstance(acc_wait, int) and acc_wait <= 0:
                                acc_wait = None
                            for s in range(2):
                                v = 2 * b2 + s

                                def after_chunk(c_):
                                    if g0 is None:
                                        return
                                    for q in ADA_AT.get((v, c_), ()):
                                        lap = A_PRO + 4 * (g0 - A_PRO + i) + q // 2 + 1
                                        ada_part(g0 + i, q, q % 2, ada, 16 * lap)
                                    if v == 3 and c_ == 1:
                                        ada_turn(g0 + i)

                                unit(u0 + 4 * i + v, (u0 + v) % 2, b2, s, PASS_BLOCKS[p] if kind == "down" else 8,
                                     (hhi, hlo) if kind in ("win", "up") else (mhi, mlo),
                                     waits if b2 == 0 else None, acc_wait, after_chunk)

                    start = 0
                    if begins and not (kind == "up" and p > 0):
                        body(0, input_ready)
                        start = 1
                    if start < n:
                        with pe.Fori(start, n) as i:
                            body(i, None)

            for k2 in range(KC // 2):
                pe.wait_ge(acc_free, residual_final(L, 0, 2 * k2 + 1))
                if k2 >= 2:
                    pe.wait_ge(fin_free, k2 - 1)
                for y in range(4):
                    t_, k = y // 2, 2 * k2 + y % 2
                    i_ = pe.transpose(bank[6 + k2 % 2][:, y * P:(y + 1) * P],
                                      xT[:, k * S + t_ * P:k * S + (t_ + 1) * P], ident)
                i_.then_inc(fin_full, 1)

        @block.scalar
        def _(act):
            def load(dst, src):
                act.dma_start(dst, src).then_inc(small_loaded, 16)
                loads.append(1)

            loads = []
            load(con[:, 0:C_N], consts)
            load(rows[0:KC, 0:P], c.rearrange("a (k p) -> (a k) p", p=P))
            for l in range(L):
                r0 = KC + G_LAYER * l

                def vector(what, src, n, c0=0, width=P):
                    at_ = gcol(l, what)
                    load(rows[at_:at_ + n, c0:c0 + width], src.rearrange("(k p) -> k p", p=width))

                for y in range(2):
                    vector("qg", da_q_gain[l], 1, 64 * y, 64)
                    vector("kg", da_k_gain[l], 1, 64 * y, 64)
                    vector("mqr", mla_q_gain[l, P:192], 1, 64 * y, 64)
                    vector("mkr", mla_k_gain[l, P:192], 1, 64 * y, 64)
                load(rows[gcol(l, "hg"):gcol(l, "hg") + NH, 0:P], da_head_gain[l])
                vector("qa", mla_q_a_gain[l], 4)
                vector("kva", mla_kv_a_gain[l], 2)
                vector("mqn", mla_q_gain[l, 0:P], 1)
                vector("mkn", mla_k_gain[l, 0:P], 1)
                load(rows[gcol(l, "sgv"):gcol(l, "sgv") + SGG, 0:P], sg_v_gain[l])
                load(rows[0:96, (1 + l) * P:(2 + l) * P], b_ada[l].rearrange("(k p) -> k p", p=P))
                for v in range(3):
                    load(rows[0:FFC, (3 + 4 * l + v) * P:(4 + 4 * l + v) * P],
                         ffn_conv_w[l, v].rearrange("(k p) -> k p", p=P))
                load(rows[0:FFC, (6 + 4 * l) * P:(7 + 4 * l) * P], ffn_conv_b[l].rearrange("(k p) -> k p", p=P))
                load(wsr[:, l * 512:(l + 1) * 512].rearrange("p (g s) -> p g s", g=SGG),
                     sg_w[l].rearrange("g t s -> t g s"))
                load(bs[:, l * 512:(l + 1) * 512], sg_b[l:l + 1].rearrange("a g t -> a (g t)").to_broadcast([P, 512]))
                for v, t in enumerate((da_lq1, da_lk1, da_lq2, da_lk2)):
                    a = (4 * l + v) * DA_QK
                    load(lamr[:, a:a + DA_QK], t[l:l + 1, :].to_broadcast([P, DA_QK]))
            load(posi[:, 0:S], positions.to_broadcast([P, S]))
            with nc.allow_non_contiguous_dma(reason="256 positions, one per partition"):
                load(posi[:, S:S + 2], positions.rearrange("a (t p) -> p (a t)", p=P))
            assert len(loads) == N_SMALL, len(loads)

            act.wait_ge(pro_free, 1)
            act.activation(sml[:, 32:48], cols[:, 0:KC], ACT.Silu).then_inc(cond_silu, 1)
            act.wait_ge(lam_sum, 1)
            act.activation(sml[:, 4:8], sml[:, 0:4], ACT.Exp).then_inc(lam_exp, 1)
            act.wait_ge(ang_ready, 1)
            act.activation(sin[:, 0:S], ang[:, 0:S], ACT.Sin).then_inc(trig_done, 1)
            act.activation(cos[:, 0:S], ang[:, S:2 * S], ACT.Sin).then_inc(trig_done, 1)

            def copy(out_, in_):
                return act.activation(out_, in_, ACT.Copy)

            def split_hi(v4, laps):
                act.wait_ge(w_loaded[v4], 16 * (laps + 1))
                o = (v4 % 2) * UNIT
                copy(whi[:, o:o + UNIT], raw[:, v4 * UNIT:(v4 + 1) * UNIT]).then_inc(hi_ready, 1)

            def split_small(l, u0, v):
                u = u0 + v
                act.wait_ge(ring_full, l * (E_ACT + E_DVE) + (E_V, E_UKV + 5, E_UKV + 10, E_UQ + 3, E_UQ + 6,
                                                              E_UQ + 9)[v - 2])
                if v < 3 or v >= 6:
                    split_hi(u % 4, u // 4)
                    return
                act.wait_ge(w_loaded[u % 4], 16 * (u // 4 + 1))
                for src, dst in uq_views(u, whi):
                    i_ = copy(dst, src)
                i_.then_inc(hi_ready, 1)

            def ada_copy(g):
                act.wait_ge(ada_used, 8 * g + 8)
                if not (isinstance(g, int) and g == 0):
                    act.wait_ge(mod_turned, g)
                copy(ya[:, 0:512], B_ADA[:, :]).then_inc(ya_ready, 1)

            for g in range(A_PRO):
                ada_copy(g)

            def squares(l, j):
                for v, (t, c0, w) in enumerate(JOB_SQ[j]):
                    s_ = sub(l, j) + v
                    act.wait_ge(sub_done, s_ - 1)
                    if j in (J_SGV, J_SGV + 1):
                        act.wait_ge(gelu_done, 2 * l + 2)
                    act.activation(sq[:, (s_ % 2) * 512:(s_ % 2) * 512 + w], t[:, c0:c0 + w], ACT.Square).then_inc(
                        sq_ready, 1)

            def root(l, j):
                g, (w, n) = job(l, j), JOB_W[j]
                act.wait_ge(sub_done, sub(l, j) + SUBS[j])
                if g >= 2:
                    act.wait_ge(applied, g - 1)
                act.activation(r[:, (g % 2) * 512:(g % 2) * 512 + w], bank[6 + g % 2][:, 0:w], ACT.Sqrt,
                               bias=con[:, C_EPS:C_EPS + 1], scale=1.0 / n).then_inc(root_ready, 1)

            def item_hi(idx, dst):
                act.wait_ge(t_ready, idx + 1)
                copy(dst, ch(T, idx % 4)).then_inc(t_high, 1)

            def trunk(l, j, t0):
                for k in range(KC):
                    s_ = sub(l, j) + k
                    if l == 0 and j == J_N1:
                        act.wait_ge(pro_free, 5 + k // 2 + 1)
                    else:
                        act.wait_ge(acc_free, residual_final(l, j == J_N2, k))
                    if s_ >= 2:
                        act.wait_ge(sub_done, s_ - 1)
                    act.activation(sq[:, (s_ % 2) * 512:(s_ % 2) * 512 + S], ch(xT, k), ACT.Square).then_inc(
                        sq_ready, 1)
                root(l, j)
                for k in range(KC):
                    item_hi(l * T_LAYER + t0 + k, ch(hhi, k))

            def attention(l, u0, b0):
                item, e = l * T_LAYER, [0]
                act.wait_ge(acc_free, 2 * b0)
                squares(l, J_QA)
                squares_kva = True
                root(l, J_QA)
                squares(l, J_KVA)
                root(l, J_KVA)
                for k in range(6):
                    item_hi(item + T_QA + k, ch(qahi, k))

                def ring_copy(*pairs):
                    act.wait_ge(ring_full, l * (E_ACT + E_DVE) + e[0] + 1)
                    for dst, src in pairs:
                        i_ = copy(dst, src)
                    i_.then_inc(ring_act, 1)
                    e[0] += 1

                def rb():
                    return bank[e[0] % 4]

                split_small(l, u0, 2)
                act.wait_ge(ring_full, l * (E_ACT + E_DVE) + e[0] + 1)
                b = rb()
                copy(kr[0:64, 0:S], b[0:64, 0:S])
                act.activation(sqkr[:, 0:S], b[:, 0:S], ACT.Square)
                copy(kr[64:P, 0:S], b[0:64, 0:S]).then_inc(ring_act, 1)
                e[0] += 1
                for v in range(3):
                    ring_copy((vda[:, v * 512:(v + 1) * 512], rb()[:, :]))
                act.activation(ch(z, 24, 4), ch(z, 24, 4), ACT.Gelu_apprx_tanh).then_inc(gelu_done, 1)
                act.activation(ch(z, 28, 4), ch(z, 28, 4), ACT.Gelu_apprx_tanh).then_inc(gelu_done, 1)
                for v in range(2):
                    for y in range(3):
                        ring_copy((ch(mk, 3 * v + y), rb()[:, 0:S]))
                    for t_ in range(2):
                        dst = mv[:, 3 * v * S:3 * (v + 1) * S].rearrange("p (h t d) -> p h t d", h=3, t=2)[:, :, t_, :]
                        ring_copy((dst, rb()[:, 0:384].rearrange("p (h d) -> p h d", h=3)))
                    split_small(l, u0, 3 + v)
                for v in range(3):
                    ring_copy((ch(mq, 2 * v), rb()[:, 0:S]))
                    ring_copy((ch(mq, 2 * v + 1), rb()[:, 0:S]))
                    ring_copy((ch(mqr, v), rb()[:, 0:S]))
                    split_small(l, u0, 5 + v)
                jobs = list(range(J_SGV, J_O))
                squares(l, jobs[0])
                for n_, j in enumerate(jobs):
                    if n_ + 1 < len(jobs):
                        squares(l, jobs[n_ + 1])
                    root(l, j)
                    if j == J_DAQK + 1:
                        for v in range(2):
                            ring_copy((vt[:, v * 512:(v + 1) * 512], rb()[:, :]))
                    if j == J_DAQK + 5:
                        for g in range(SGG):
                            item_hi(item + T_SG + g, ch(mhi, 12 + g))
                assert e[0] == E_ACT
                for i in range(14):
                    if i < 12:
                        o, st = (i % 2) * 2 * KEYS, (i % 2) * 16
                        act.wait_ge(max_ready, 12 * l + i + 1)
                        for s_ in range(2 if i < NH else 1):
                            for qb, (c0, c1) in enumerate(((0, P), (P, KEYS))):
                                v = 2 * s_ + qb
                                a = sc_s[:, o + s_ * KEYS + c0:o + s_ * KEYS + c1]
                                i_ = act.activation(a, a, ACT.Exp, bias=stat[:, st + 4 + v:st + 5 + v],
                                                    accum_out=stat[:, st + 8 + v:st + 9 + v])
                        i_.then_inc(exp_done, 1)
                    if i % 2 == 1 and i >= 3:
                        pair = (i - 3) // 2
                        if pair < 3:
                            root(l, J_O + pair)
                            for y in range(2):
                                item_hi(item + T_DA + 2 * pair + y, ch(mhi, 2 * pair + y))
                        else:
                            act.wait_ge(o_full, 12 * l + 2 * pair + 2)
                            for y in range(2):
                                h = 2 * (pair - 3) + y
                                copy(ch(mhi, NH + h), B_O[:, y * S:(y + 1) * S]).then_inc(mh_ready, 1)
                    if 1 <= i <= 12:
                        v = i - 1
                        act.wait_ge(pt_full, 12 * l + v + 1)
                        if v >= 2:
                            act.wait_ge(o_full, 12 * l + v - 1)
                        copy(pt[:, (v % 2) * KEYS:(v % 2 + 1) * KEYS], B_PT[:, 0:KEYS]).then_inc(pt_ready, 1)
                        if v % 2 == 1 and v < NH:
                            act.wait_ge(o_full, 12 * l + v + 1)
                            squares(l, J_O + v // 2)

            split_hi(0, 0)
            split_hi(1, 0)
            for l in range(L):
                trunk(l, J_N1, T_N1)
                for row in phases[l]:
                    kind, p, first, n, u0, b0, g0 = row
                    if kind == "small":
                        attention(l, u0, b0)
                        continue
                    if kind == "up" and p == 0 and first_of(l, row):
                        trunk(l, J_N2, T_N2)

                    d0 = u0 - dropped(l, kind)

                    def body(i, ending=False):
                        pb = sum(PASS_BLOCKS[:p])
                        for b2 in range(2):
                            for v in (2 * b2 + 2, 2 * b2 + 3):
                                if not (ending and b2 == 1):
                                    act.wait_ge(unit_done, d0 + 4 * i + v - 1)
                                    split_hi((u0 + v) % 4, (u0 + v) // 4 + i)
                                if v == 4 and g0 is not None:
                                    ada_copy(g0 + i)
                            if kind == "win":
                                for c_ in range(2):
                                    if c_ == 0:
                                        act.wait_ge(chunk0_done, b0 + 2 * i + b2 + 1)
                                    else:
                                        act.wait_ge(unit_done, d0 + 4 * i + 2 * b2 + 2)
                                    copy(ch(z, (first + i) * 4 + 2 * b2 + c_), bank[2 * b2 + c_][:, 0:S]).then_inc(
                                        acc_free, 1)
                            if kind == "up":
                                y_ = yv if b2 else yg
                                pair = l * (FFC // 4) + pb + first + i
                                for c_ in range(2):
                                    if c_ == 0:
                                        act.wait_ge(chunk0_done, b0 + 2 * i + b2 + 1)
                                        if not isinstance(pair, int) or pair >= 1:
                                            act.wait_ge(a_ready if b2 == 0 else a_low, pair)
                                    else:
                                        act.wait_ge(unit_done, d0 + 4 * i + 2 * b2 + 2)
                                    cc = COL_CONV + 4 * FFC * l + 2 * (pb + first + i) + (FFC // 2) * b2 + c_
                                    act.activation(ch(y_, c_), bank[2 * b2 + c_][:, 0:S], ACT.Identity,
                                                   bias=cols[:, bass.ds(cc + 3 * FFC, 1)],
                                                   scale=cols[:, bass.ds(cc + 2 * FFC, 1)]).then_inc(tap_ready, 1)
                        if kind == "up":
                            act.wait_ge(acc_free, 2 * (b0 + 2 * i) + 2)
                            act.activation(yg[:, 0:512], yg[:, 0:512], ACT.Silu).then_inc(silu_done, 1)
                            act.wait_ge(a_ready, pair + 1)
                            copy(mhi[:, bass.ds((first + i) * 512, 512)], yv[:, 0:512]).then_inc(a_high, 1)

                    ends = l == L - 1 and row is phases[l][-1]
                    if n - ends > 0:
                        with act.Fori(0, n - ends) as i:
                            body(i)
                    if ends:
                        body(n - 1, True)
            for k2 in range(0, KC // 2, 1):
                act.wait_ge(fin_full, k2 + 1)
                dst = xs[:, 0:2 * D].rearrange("p (t d) -> p t d", t=2)[:, :, k2 * S:(k2 + 1) * S]
                copy(dst, bank[6 + k2 % 2][:, :].rearrange("p (t d) -> p t d", t=2)).then_inc(fin_free, 1)

        @block.vector
        def _(dve):
            order = Order(dve, dve_order)
            stt, ts, tt = dve.scalar_tensor_tensor, dve.tensor_scalar, dve.tensor_tensor

            dve.wait_ge(pro_full, 1)
            dve.tensor_copy(cols[:, 0:252], bank[0][:, 0:252]).then_inc(pro_free, 1)
            dve.wait_ge(cond_silu, 1)
            dve.tensor_copy(condr[:, 0:KC * 32].rearrange("p (k m) -> p k m", m=32),
                            sml[:, 32:48].unsqueeze(2).to_broadcast([P, KC, 32])).then_inc(cond_ready, 1)
            for l in range(L):
                dve.wait_ge(pro_full, 2 + l)
                dve.tensor_copy(cols[:, COL_CONV + 4 * FFC * l:COL_CONV + 4 * FFC * (l + 1)],
                                bank[1 + l][:, 0:4 * FFC]).then_inc(pro_free, 1)
            for l in range(L):
                dve.wait_ge(pro_full, 4 + l)
                b = bank[(3 + l) % 4]
                dve.tensor_tensor(wt[:, l * 512:(l + 1) * 512].rearrange("p (g t) -> p g t", g=SGG),
                                  b[:, :].rearrange("p (g t) -> p g t", g=SGG),
                                  tril.unsqueeze(1).to_broadcast([P, SGG, P]), ALU.mult).then_inc(pro_free, 1)
            for k2 in range(KC // 2):
                dve.wait_ge(pro_full, 6 + k2)
                dve.tensor_copy(xT[:, k2 * 512:(k2 + 1) * 512], bank[(5 + k2) % 4][:, :]).then_inc(pro_free, 1)
            for l in range(L):
                a = cols[:, gcol(l, "hg"):gcol(l, "hg") + NH]
                order.after(ts(a, a, 1.0 - LAM_INIT[l], None, ALU.mult))
            lv = lamr[:, 0:L * 4 * DA_QK].rearrange("p (a b d) -> p a b d", b=2, d=DA_QK)
            order.after(tt(lv[:, :, 0, :], lv[:, :, 0, :], lv[:, :, 1, :], ALU.mult))
            dve.tensor_reduce(sml[:, 0:4], lv[:, :, 0, :], AX_X, ALU.add).then_inc(lam_sum, 1)
            dve.wait_ge(lam_exp, 1)
            for l in range(L):
                order.after(tt(sml[:, 8 + l:9 + l], sml[:, 5 + 2 * l:6 + 2 * l], sml[:, 4 + 2 * l:5 + 2 * l],
                               ALU.subtract))
                order.after(ts(sml[:, 8 + l:9 + l], sml[:, 8 + l:9 + l], -LAM_INIT[l], None, ALU.add))
            dve.tensor_copy(sml[:, 48:50], posi[:, S:S + 2])
            order.after(dve.tensor_copy(ang[:, 0:S], posi[:, 0:S]))
            ts(dist[:, 0:P], ang[:, 0:P], sml[:, 48:49], None, ALU.subtract)
            order.after(ts(dist[:, P:KEYS], ang[:, 0:S], sml[:, 49:50], None, ALU.subtract))
            order.after(stt(dist[:, 0:KEYS], dist[:, 0:KEYS], -1.0, dist[:, 0:KEYS], ALU.mult, ALU.max))
            order.after(ts(ang[:, 0:S], ang[:, 0:S], con[:, C_INV:C_INV + 1], None, ALU.mult))
            order.after(ts(rt_tmp[:, 0:S], ang[:, 0:S], 1.0 / TURN, ROUND, ALU.mult, ALU.add))
            order.after(ts(rt_tmp[:, 0:S], rt_tmp[:, 0:S], -ROUND, None, ALU.add))
            for part in TURN_PARTS:
                order.after(stt(ang[:, 0:S], rt_tmp[:, 0:S], -part, ang[:, 0:S], ALU.mult, ALU.add))
            order.after(ts(ang[:, 0:S], ang[:, 0:S], PI_, -PI_, ALU.min, ALU.max))
            order.after(stt(rt_tmp[:, 0:S], ang[:, 0:S], -1.0, ang[:, 0:S], ALU.mult, ALU.max))
            ts(ang[:, S:2 * S], rt_tmp[:, 0:S], -1.0, TURN / 4, ALU.mult, ALU.add).then_inc(ang_ready, 1)
            dve.wait_ge(trig_done, 2)

            def split_lo(u, v4):
                dve.wait_ge(hi_ready, u + 1)
                o = (v4 % 2) * UNIT
                tt(wlo[:, o:o + UNIT], raw[:, v4 * UNIT:(v4 + 1) * UNIT], whi[:, o:o + UNIT].bitcast(F32),
                   ALU.subtract).then_inc(lo_ready, 1)

            def split_lo_static(u):
                if u % U_LAYER in UQ_UNITS:
                    dve.wait_ge(hi_ready, u + 1)
                    for (src, dst), (_, hi) in zip(uq_views(u, wlo), uq_views(u, whi)):
                        i_ = tt(dst, src, hi.bitcast(F32), ALU.subtract)
                    i_.then_inc(lo_ready, 1)
                    return
                split_lo(u, u % 4)

            def mod_add(g):
                dve.wait_ge(mod_turned, g + 1)
                dst = mod[:, bass.ds(4 * g, 4)]
                tt(dst, B_MOD[:, 0:4], cols[:, bass.ds(COL_BADA + 4 * g, 4)], ALU.add).then_inc(mod_ready, 1)

            for g in range(A_PRO):
                mod_add(g)

            def t_free(idx):
                if idx >= 4:
                    dve.wait_ge(t_low, idx - 3)

            def item_lo(idx, hi, dst):
                dve.wait_ge(t_high, idx + 1)
                tt(dst, ch(T, idx % 4), hi.bitcast(F32), ALU.subtract).then_inc(t_low, 1)

            def inverse(l, j):
                g, w = job(l, j), JOB_W[j][0]
                dve.wait_ge(root_ready, g + 1)
                a = r[:, (g % 2) * 512:(g % 2) * 512 + w]
                order.after(dve.reciprocal(a, a))
                return a

            def trunk(l, j, t0, part):
                dve.wait_ge(mod_ready, A_LAYER * l + 4 * (part + 2))
                m0 = 96 * l + 16 * part
                order.after(ts(sml[:, 16:32], mod[:, m0 + 16:m0 + 32], 1.0, None, ALU.add))
                a = inverse(l, j)
                for k in range(KC + 1):
                    idx = l * T_LAYER + t0 + k
                    if k < KC:
                        t_free(idx)
                        t_ = ch(T, idx % 4)
                        i_ = tt(t_, ch(xT, k), a, ALU.mult)
                        if k == KC - 1:
                            i_.then_inc(applied, 1)
                            dve.wait_ge(applied, job(l, j) + 1)
                        else:
                            order.after(i_)
                        ts(t_, t_, sml[:, 16 + k:17 + k], mod[:, m0 + k:m0 + k + 1], ALU.mult, ALU.add).then_inc(
                            t_ready, 1)
                    if k >= 1:
                        item_lo(idx - 1, ch(hhi, k - 1), ch(hlo, k - 1))

            def g_(l, what, i=0):
                a = gcol(l, what, i)
                return cols[:, a:a + 1]

            def attention(l, u0, b0):
                item = l * T_LAYER
                for j, t0, n, z0, what in ((J_QA, T_QA, 4, 18, "qa"), (J_KVA, T_KVA, 2, 22, "kva")):
                    a = inverse(l, j)
                    for k in range(n + 1):
                        idx = item + t0 + k
                        if k < n:
                            t_free(idx)
                            stt(ch(T, idx % 4), ch(z, z0 + k), g_(l, what, k), a, ALU.mult, ALU.mult).then_inc(t_ready, 1)
                        if k >= 1:
                            c_ = k - 1 + (4 if j == J_KVA else 0)
                            item_lo(idx - 1, ch(qahi, c_), ch(qalo, c_))
                    dve.engine_nop().then_inc(applied, 1)
                for v in range(2, 8):
                    split_lo_static(u0 + v)
                for v in range(2):
                    a = inverse(l, J_SGV + v)
                    for y in range(2):
                        k = 2 * v + y
                        i_ = stt(ch(z, 28 + k), ch(z, 28 + k), g_(l, "sgv", k), a[:, y * S:(y + 1) * S],
                                 ALU.mult, ALU.mult)
                    i_.then_inc(applied, 1)

                def pair(j, t, k, gain):
                    a = inverse(l, j)
                    stt(ch(t, k, 2), ch(t, k, 2), gain, a, ALU.mult, ALU.mult).then_inc(applied, 1)

                for v in range(6):
                    pair(J_DAQK + v, z, 2 * v, g_(l, "qg" if v < 3 else "kg"))
                    if v == 1:
                        ts(kr[:, 0:S], kr[:, 0:S], g_(l, "mkr"), None, ALU.mult).then_inc(rope_in, 1)

                def ring_wait(e):
                    dve.wait_ge(ring_full, l * (E_ACT + E_DVE) + e + 1)
                    return bank[e % 4]

                for v in range(2):
                    b = ring_wait(E_SG + v)
                    bias = bs[:, l * 512 + v * S:l * 512 + (v + 1) * S].rearrange("p (g t) -> p g t", g=2)
                    ts_ = [ch(T, (T_SG + 2 * v + y) % 4) for y in range(2)]
                    t_free(item + T_SG + 2 * v + 1)
                    for y in range(2):
                        i_ = tt(ts_[y].rearrange("p (n t) -> p n t", n=2),
                                b[:, y * S:(y + 1) * S].rearrange("p (n t) -> p n t", n=2),
                                bias[:, y, :].unsqueeze(1).to_broadcast([P, 2, P]), ALU.add)
                    i_.then_inc(ring_dve, 1)
                    dve.wait_ge(ring_dve, l * E_DVE + v + 1)
                    for y in range(2):
                        tt(ts_[y], ts_[y], ch(z, 24 + 2 * v + y), ALU.mult).then_inc(t_ready, 1)
                    for y in range(2):
                        k = 2 * v + y
                        item_lo(item + T_SG + k, ch(mhi, 12 + k), ch(mlo, 12 + k))

                def rotate(e, t, done=None):
                    b = ring_wait(e)
                    tt(rt_tmp[:, 0:S], b[:, 0:S], sin[:, 0:S], ALU.mult).then_inc(ring_dve, 1)
                    order.after(tt(t, t, cos[:, 0:S], ALU.mult))
                    dve.wait_ge(ring_dve, l * E_DVE + e - E_SG + 1)
                    i_ = tt(t, t, rt_tmp[:, 0:S], ALU.add)
                    if done is None:
                        order.after(i_)
                    else:
                        i_.then_inc(done, 1)

                def mla_q(v):
                    a = inverse(l, J_MQ + v)
                    for y in range(2):
                        t_ = mqr[64 * y:64 * y + 64, v * S:(v + 1) * S]
                        i_ = stt(t_, t_, g_(l, "mqr")[64 * y:64 * y + 64, :], a[64 * y:64 * y + 64, y * S:(y + 1) * S],
                                 ALU.mult, ALU.mult)
                    i_.then_inc(rope_in, 1)
                    stt(ch(mq, 2 * v, 2), ch(mq, 2 * v, 2), g_(l, "mqn"), a, ALU.mult, ALU.mult).then_inc(applied, 1)

                def mla_k(v):
                    a = inverse(l, J_MK + v)
                    for y in range(2):
                        tt(mkr[64 * y:64 * y + 64, v * S:(v + 1) * S], kr[64 * y:64 * y + 64, 0:S],
                           a[64 * y:64 * y + 64, y * S:(y + 1) * S], ALU.mult)
                    stt(ch(mk, 2 * v, 2), ch(mk, 2 * v, 2), g_(l, "mkn"), a, ALU.mult, ALU.mult).then_inc(applied, 1)

                rotate(E_KROT, kr[:, 0:S])
                mla_q(0)
                mla_q(1)
                rotate(E_QROT, ch(mqr, 0), mla_q_ready)
                mla_q(2)
                rotate(E_QROT + 1, ch(mqr, 1), mla_q_ready)
                mla_k(0)
                rotate(E_QROT + 2, ch(mqr, 2), mla_q_ready)
                mla_k(1)
                mla_k(2)

                def maxima(i):
                    ns, o, st = (2 if i < NH else 1), (i % 2) * 2 * KEYS, (i % 2) * 16
                    dve.wait_ge(sc_full, 12 * l + i + 1)
                    for s_ in range(ns):
                        i_ = stt(sc_s[:, o + s_ * KEYS:o + (s_ + 1) * KEYS], bank[s_][:, 0:KEYS],
                                 DA_SCALE if i < NH else MLA_SCALE, mask, ALU.mult, ALU.add)
                    i_.then_inc(sc_free, 1)
                    dve.wait_ge(sc_free, 12 * l + i + 1)
                    if i < NH:
                        for s_ in range(2):
                            a = sc_s[:, o + s_ * KEYS:o + (s_ + 1) * KEYS]
                            i_ = stt(a, dist[:, 0:KEYS], -SLOPES[i], a, ALU.mult, ALU.add)
                        order.after(i_)
                    for s_ in range(ns):
                        for qb, (c0, c1) in enumerate(((0, P), (P, KEYS))):
                            v = 2 * s_ + qb
                            i_ = dve.tensor_reduce(stat[:, st + v:st + v + 1],
                                                   sc_s[:, o + s_ * KEYS + c0:o + s_ * KEYS + c1], AX_X, ALU.max)
                    order.after(i_)
                    ts(stat[:, st + 4:st + 4 + 2 * ns], stat[:, st:st + 2 * ns], -1.0, None, ALU.mult).then_inc(
                        max_ready, 1)

                def probabilities(i):
                    ns, o, st = (2 if i < NH else 1), (i % 2) * 2 * KEYS, (i % 2) * 16
                    dve.wait_ge(exp_done, 12 * l + i + 1)
                    order.after(dve.reciprocal(stat[:, st + 12:st + 12 + 2 * ns], stat[:, st + 8:st + 8 + 2 * ns]))
                    if i < NH:
                        a = stat[:, st + 14:st + 16]
                        order.after(ts(a, a, sml[:, 8 + l:9 + l], None, ALU.mult))
                    if i >= 2:
                        dve.wait_ge(pt_full, 12 * l + i - 1)
                    for s_ in reversed(range(ns)):
                        for qb, (c0, c1) in enumerate(((0, P), (P, KEYS))):
                            dst = pr[:, (i % 2) * KEYS + c0:(i % 2) * KEYS + c1]
                            e_ = sc_s[:, o + s_ * KEYS + c0:o + s_ * KEYS + c1]
                            cf = stat[:, st + 12 + 2 * s_ + qb:st + 13 + 2 * s_ + qb]
                            if s_ == ns - 1:
                                i_ = ts(dst, e_, cf, None, ALU.mult)
                            else:
                                i_ = stt(dst, e_, cf, dst, ALU.mult, ALU.add)
                        if s_ == 0:
                            i_.then_inc(p_ready, 1)
                        else:
                            order.after(i_)

                for i in range(14):
                    if i < 12:
                        maxima(i)
                    if i % 2 == 1 and i >= 3:
                        v = (i - 3) // 2
                        if v < 3:
                            a = inverse(l, J_O + v)
                            for y in range(2):
                                h = 2 * v + y
                                t_free(item + T_DA + h)
                                stt(ch(T, (T_DA + h) % 4), B_O[:, y * S:(y + 1) * S], g_(l, "hg", h), a[:, y * S:(y + 1) * S],
                                    ALU.mult, ALU.mult).then_inc(t_ready, 1)
                            dve.engine_nop().then_inc(applied, 1)
                            for y in range(2):
                                item_lo(item + T_DA + 2 * v + y, ch(mhi, 2 * v + y), ch(mlo, 2 * v + y))
                        else:
                            dve.wait_ge(mh_ready, l * NH + 2 * (v - 3) + 2)
                            for y in range(2):
                                h = 2 * (v - 3) + y
                                tt(ch(mlo, NH + h), B_O[:, y * S:(y + 1) * S], ch(mhi, NH + h).bitcast(F32),
                                   ALU.subtract).then_inc(mh_low, 1)
                    if 1 <= i <= 12:
                        probabilities(i - 1)

            split_lo_static(0)
            split_lo_static(1)
            for l in range(L):
                trunk(l, J_N1, T_N1, 0)
                for row in phases[l]:
                    kind, p, first, n, u0, b0, g0 = row
                    if kind == "small":
                        attention(l, u0, b0)
                        continue
                    if kind == "up" and p == 0 and first_of(l, row):
                        trunk(l, J_N2, T_N2, 3)
                    if kind in ("wout", "down"):
                        dve.wait_ge(mod_ready, A_LAYER * l + (12 if kind == "wout" else 24))
                    pb = sum(PASS_BLOCKS[:p])
                    d0 = u0 - dropped(l, kind)
                    links = {"up": 4, "down": 0, "wout": 0, "win": 0}[kind]

                    def body(i, ending=False):
                        n0 = order.n
                        order.plus = links * i
                        for b2 in range(2):
                            for v in (2 * b2 + 2, 2 * b2 + 3):
                                if not (ending and b2 == 1):
                                    split_lo(u0 + 4 * i + v, (u0 + v) % 4)
                            if kind == "win":
                                continue
                            for c_ in range(2):
                                acc = bank[2 * b2 + c_]
                                if kind == "up":
                                    dve.wait_ge(tap_ready, tap0 + 4 * i + 2 * b2 + c_ + 1)
                                    y_ = ch(yv if b2 else yg, c_)
                                    cc = COL_CONV + 4 * FFC * l + 2 * (pb + first + i) + (FFC // 2) * b2 + c_
                                    order.after(stt(y_[:, 1:S], acc[:, 0:S - 1], cols[:, bass.ds(cc + FFC, 1)],
                                                    y_[:, 1:S], ALU.mult, ALU.add))
                                    stt(y_[:, 2:S], acc[:, 0:S - 2], cols[:, bass.ds(cc, 1)],
                                        y_[:, 2:S], ALU.mult, ALU.add).then_inc(acc_free, 1)
                                else:
                                    if c_ == 0:
                                        dve.wait_ge(chunk0_done, b0 + 2 * i + b2 + 1)
                                    else:
                                        dve.wait_ge(unit_done, d0 + 4 * i + 2 * b2 + 2)
                                    k = 4 * (first + i) + 2 * b2 + c_
                                    gate = 96 * l + 16 * (2 if kind == "wout" else 5) + k
                                    xa = xT[:, bass.ds(k * S, S)]
                                    stt(xa, acc[:, 0:S], mod[:, bass.ds(gate, 1)], xa, ALU.mult, ALU.add).then_inc(
                                        acc_free, 1)
                        if kind == "up":
                            dve.wait_ge(silu_done, pair0 + i + 1)
                            dve.wait_ge(acc_free, 2 * (b0 + 2 * i) + 4)
                            tt(yv[:, 0:512], yv[:, 0:512], yg[:, 0:512], ALU.mult).then_inc(a_ready, 1)
                            dve.wait_ge(a_high, pair0 + i + 1)
                            o = (first + i) * 512
                            tt(mlo[:, bass.ds(o, 512)], yv[:, 0:512], mhi[:, bass.ds(o, 512)].bitcast(F32),
                               ALU.subtract).then_inc(a_low, 1)
                        if g0 is not None:
                            mod_add(g0 + i)
                        assert order.n - n0 == links
                        order.plus = 0
                        return n0

                    pair0 = l * (FFC // 4) + pb + first
                    tap0 = 4 * pair0
                    ends = l == L - 1 and row is phases[l][-1]
                    m = n - ends
                    if m > 0:
                        with dve.Fori(0, m) as i:
                            n0 = body(i)
                        order.n = n0 + links * m
                    if ends:
                        body(n - 1, True)


_INS = ['x', 'c', 'positions', 'w_ada', 'b_ada', 'w_in', 'da_q_gain', 'da_k_gain', 'da_lq1', 'da_lk1', 'da_lq2',
        'da_lk2', 'da_head_gain', 'mla_q_a_gain', 'mla_w_uq', 'mla_kv_a_gain', 'mla_w_ukv', 'mla_q_gain',
        'mla_k_gain', 'sg_v_gain', 'sg_w', 'sg_b', 'w_out', 'ffn_w_up', 'ffn_conv_w', 'ffn_conv_b', 'ffn_w_down']


def shape_constants():
    a = np.zeros((P, C_N), np.float32)
    p = np.arange(P)[:, None]
    f = np.arange(P)[None, :]
    a[:, C_ID:C_ID + P] = p == f
    a[:, C_ONE:C_ONE + P] = 1.0
    a[:, C_BLK:C_BLK + P] = p // 64 == f // 64
    a[:, C_H0:C_H0 + P] = p < 64
    a[:, C_H1:C_H1 + P] = p >= 64
    a[:, C_ROT:C_ROT + P] = np.where((f % 64 < 32) & (p == f + 32), -1.0, 0.0) + np.where(
        (f % 64 >= 32) & (p == f - 32), 1.0, 0.0)
    a[:, C_TRIL:C_TRIL + P] = p <= f
    for c0, q0, n in ((0, 0, P), (P, P, S)):
        k = np.arange(n)[None, :]
        a[:, C_MASK + c0:C_MASK + c0 + n] = np.where(k // 64 <= (q0 + p) // 64, 0.0, -1e30)
    a[::32, C_SEL] = 1.0
    a[:, C_INV] = np.float32(10000.0) ** (-(np.arange(P) % 32).astype(np.float32) / np.float32(32))
    a[:, C_EPS] = EPS
    return a


def kernel(**inputs):
    import concourse.bacc as _bacc
    from concourse.bass_utils import run_bass_kernel_spmd as _run

    nc = _bacc.Bacc("TRN2", target_bir_lowering=False, num_devices=1)
    arrays, args = {}, []
    for name in ['consts'] + _INS:
        a = shape_constants() if name == 'consts' else np.ascontiguousarray(inputs[name])
        if name == 'x':
            a = a.reshape(S, D)
        arrays[f"in_{name}_dram"] = a
        args.append(nc.dram_tensor(f"in_{name}_dram", a.shape, mybir.dt.from_np(a.dtype), kind="ExternalInput").ap())
    args.append(nc.dram_tensor("out_0_dram", (S, D), F32, kind="ExternalOutput").ap())
    bass_trunk(nc, *args)
    res = _run(nc, [arrays], core_ids=[0])
    return res.results[0]["out_0_dram"].reshape(1, S, D)
```

```python
from contextlib import ExitStack

import numpy as np
import concourse.bass as bass
from concourse import mybir

ALU = mybir.AluOpType
ACT = mybir.ActivationFunctionType
AX_X = mybir.AxisListType.X
F32 = mybir.dt.float32
F32R = mybir.dt.float32r
I32 = mybir.dt.int32

P = 128
D = 2048
S = 256
L = 2
KC = D // P
NH = 6
DA_QK = 64
SGG = 4
D_FF = 5632
IN_COLS = 4160
EPS = 1e-6
ROPE_COL = 3072
LAM_INIT = [0.8 - 0.6 * float(np.exp(-0.3 * l)) for l in range(L)]
SLOPES = [2.0 ** (-8.0 * (h + 1) / NH) for h in range(NH)]
DA_SCALE = DA_QK ** -0.5
MLA_SCALE = 192 ** -0.5
KEYS = 384

C_ID, C_ONE, C_BLK, C_H0, C_H1, C_ROT, C_TRIL, C_MASK = (P * i for i in range(8))
C_SEL = C_MASK + KEYS
C_INV = C_SEL + 1
C_EPS = C_INV + 1
C_N = C_EPS + 1

G_C = 0
G_LAYER = 22


def gcol(l, what, i=0):
    at = {"qg": 0, "kg": 1, "hg": 2, "qa": 8, "kva": 12, "mqn": 14, "mqr": 15, "mkn": 16, "mkr": 17, "sgv": 18}
    return KC + G_LAYER * l + at[what] + i


COL_BADA = KC + G_LAYER * L
COL_CONV = COL_BADA + 96 * L
FFC = 2 * D_FF // P
N_COLS = COL_CONV + 4 * FFC * L

U_WIN, U_SMALL, U_WOUT = 32, 6, 16
PASS_BLOCKS = (8, 8, 6)
U_LAYER = U_WIN + U_SMALL + U_WOUT + sum(4 * b + 16 for b in PASS_BLOCKS)
B_LAYER = 16 + 8 + sum(2 * b + 8 for b in PASS_BLOCKS)
UNIT = 2048

A_LAYER = 48
A_PRO = 16
A_FILL, A_HEADS = 5, 7
A_ATT = A_FILL + A_HEADS
A_ALL = A_LAYER * L


def make_phases():
    g = A_PRO
    out = []
    for l in range(L):
        rows = []
        u, b = l * U_LAYER, l * B_LAYER

        def add(kind, p, first, n):
            nonlocal g, u, b
            i = 0
            while i < n:
                with_ada = g < A_ALL
                m = n - i
                if with_ada:
                    m = min(m, A_LAYER - g % A_LAYER)
                rows.append((kind, p, first + i, m, u, b, g if with_ada else None))
                if with_ada:
                    g += m
                u += 4 * m
                b += 2 * m
                i += m

        add("win", 0, 0, 6)
        add("win", 0, 6, 2)
        rows.append(("small", 0, 0, 1, u, b, g))
        g += A_ATT
        u += U_SMALL
        add("wout", 0, 0, 4)
        pb = 0
        for p, nb in enumerate(PASS_BLOCKS):
            add("up", p, 0, nb)
            add("down", p, 0, 4)
            pb += nb
        assert u == (l + 1) * U_LAYER and b == (l + 1) * B_LAYER
        out.append(rows)
    assert g == A_ALL, g
    return out


J_N1, J_QA, J_KVA, J_SGV, J_DAQK, J_MQ, J_MK, J_O, J_N2 = 0, 1, 2, 3, 5, 11, 14, 17, 20
J_LAYER = 21
SUBS = [16, 2, 1, 1, 1] + [1] * 6 + [2] * 3 + [1] * 3 + [1] * 3 + [16]
SUB_LAYER = sum(SUBS)
T_N1, T_QA, T_KVA, T_SG, T_DA, T_N2 = 0, 16, 20, 22, 26, 32
T_LAYER = 48
E_KR, E_V, E_UKV, E_UQ, E_VT, E_SG, E_KROT, E_QROT = 0, 1, 4, 14, 23, 25, 27, 28
E_ACT, E_DVE = 25, 6


N_FIRST = 2 + L
N_SMALL = L * (8 + 6 + 4 + 1 + 1 + 4) + 2
PRO_X, PRO_VEC = 1, 1 + KC // 2
TURN = 2 * float(np.pi)
ROUND = 1.5 * 2.0 ** 23
TURN_PARTS = (6.28125, round((TURN - 6.28125) * 2 ** 21) / 2 ** 21, TURN - 6.28125 - round((TURN - 6.28125) * 2 ** 21) / 2 ** 21)
PI_ = 3.1415925


def bass_trunk(nc, consts, x, c, positions, w_ada, b_ada, w_in, da_q_gain, da_k_gain, da_lq1, da_lk1,
               da_lq2, da_lk2, da_head_gain, mla_q_a_gain, mla_w_uq, mla_kv_a_gain, mla_w_ukv,
               mla_q_gain, mla_k_gain, sg_v_gain, sg_w, sg_b, w_out, ffn_w_up, ffn_conv_w,
               ffn_conv_b, ffn_w_down, out):
    phases = make_phases()
    with ExitStack() as ctx:
        def sb(name, cols, dt=F32):
            return ctx.enter_context(nc.sbuf_tensor(name, [P, cols], dt))

        def sem(name):
            return ctx.enter_context(nc.semaphore(name))

        base = nc.sbuf_base
        arena = ctx.enter_context(nc.sbuf_tensor("arena", [P, 52 * 1024 - 256], F32))
        at = [(base + 31) // 32 * 32]
        end = at[0] + (52 * 1024 - 256) * 4

        def place(name, cols, dt=F32, offset=None):
            if offset is None:
                offset = at[0]
                at[0] += (cols * 4 + 31) // 32 * 32
                assert at[0] <= end, (name, at[0], end)
            return nc.alloc_sbuf_tensor_at(name, [P, cols], dt, offset=offset), offset

        raw, _ = place("raw", 4 * UNIT)
        whi, _ = place("whi", 2 * UNIT, F32R)
        wlo, _ = place("wlo", 2 * UNIT, F32R)
        ada, o_ada = place("ada", 2 * 1024)
        xT, _ = place("xT", KC * S)
        hhi, o_h = place("hhi", KC * S, F32R)
        hlo, _ = place("hlo", KC * S, F32R)
        mhi, o_m = place("mhi", KC * S, F32R)
        mlo, _ = place("mlo", KC * S, F32R)
        z, _ = place("z", 32 * S, offset=o_m)
        apro, _ = place("apro", 8 * 1024, offset=o_m)
        xs, _ = place("xs", 2 * D, offset=o_h)
        rows, _ = place("rows", 11 * P, offset=o_h + 4 * 2 * D)
        wsr, _ = place("wsr", L * 512, offset=o_h + 4 * (2 * D + 11 * P))
        posi, _ = place("posi", S + 2, I32, offset=o_h + 4 * (2 * D + 11 * P + L * 512))
        lamr, _ = place("lamr", L * 4 * DA_QK, offset=o_h + 4 * (2 * D + 11 * P + L * 512 + 264))
        ang, _ = place("ang", 2 * S, offset=o_h + 4 * (2 * D + 11 * P + L * 512 + 264 + 512))
        vda, _ = place("vda", NH * S, offset=o_h)
        mq, _ = place("mq", NH * S, offset=o_h + 4 * 1536)
        mk, _ = place("mk", NH * S, offset=o_h + 4 * 3072)
        mv, _ = place("mv", NH * S, offset=o_h + 4 * 4608)
        mqr, _ = place("mqr", 3 * S, offset=o_h + 4 * 6144)
        mkr, _ = place("mkr", 3 * S, offset=o_h + 4 * 6912)
        kr, _ = place("kr", S, offset=o_h + 4 * 7680)
        sqkr, _ = place("sqkr", S, offset=o_h + 4 * 7936)
        o_s = at[0]
        sc_s, _ = place("sc_s", 2 * 2 * KEYS)
        pr, _ = place("pr", 2 * KEYS)
        pt, _ = place("pt", 2 * KEYS)
        qahi, _ = place("qahi", 6 * S, F32R, offset=o_s)
        qalo, _ = place("qalo", 6 * S, F32R, offset=o_s + 4 * 6 * S)
        yg, _ = place("yg", 2 * S, offset=o_s)
        yv, _ = place("yv", 2 * S, offset=o_s + 4 * 2 * S)
        vt, _ = place("vt", 4 * S)
        con, _ = place("con", C_N)
        cols, _ = place("cols", N_COLS)
        mod, _ = place("mod", 96 * L)
        condr, _ = place("condr", KC * 32)
        bs, _ = place("bs", L * 512)
        wt, _ = place("wt", L * 512)
        dist, _ = place("dist", KEYS)
        cos, _ = place("cos", S)
        sin, _ = place("sin", S)
        sq, _ = place("sq", 2 * 512)
        r, _ = place("r", 2 * 512)
        T, _ = place("T", 4 * S)
        ya, _ = place("ya", 256)
        stat, _ = place("stat", 2 * 16)
        sml, _ = place("sml", 64)
        rt_tmp, _ = place("rt_tmp", S)

        bank = [ctx.enter_context(nc.psum_tensor(f"bank{i}", [P, 512], F32)) for i in range(8)]
        B_ADA, B_MOD, B_O, B_PT = bank[4], bank[5], bank[3], bank[2]

        def col(t, i, n=1):
            return t[:, i:i + n]

        def ch(t, k, n=1):
            return t[:, bass.ds(k * S, n * S)] if not isinstance(k, int) else t[:, k * S:(k + n) * S]

        ident, ones, blk = con[:, C_ID:C_ID + P], con[:, C_ONE:C_ONE + P], con[:, C_BLK:C_BLK + P]
        half = [con[:, C_H0:C_H0 + P], con[:, C_H1:C_H1 + P]]
        rot, tril = con[:, C_ROT:C_ROT + P], con[:, C_TRIL:C_TRIL + P]
        mask = con[:, C_MASK:C_MASK + KEYS]

        w_loaded = [sem(f"w_loaded{i}") for i in range(4)]
        ada_loaded = [sem(f"ada_loaded{i}") for i in range(8)]
        x_loaded, first_loaded, small_loaded, stored = (
            sem("x_loaded"), sem("first_loaded"), sem("small_loaded"), sem("stored"))
        unit_done, chunk0_done = sem("unit_done"), sem("chunk0_done")
        ada_used, mod_turned = sem("ada_used"), sem("mod_turned")
        sub_done, ring_full = sem("sub_done"), sem("ring_full")
        pro_full = sem("pro_full")
        sc_full, pt_full, o_full, fin_full = sem("sc_full"), sem("pt_full"), sem("o_full"), sem("fin_full")
        hi_ready, sq_ready, root_ready, t_high = sem("hi_ready"), sem("sq_ready"), sem("root_ready"), sem("t_high")
        ya_ready, ring_act, gelu_done, exp_done = sem("ya_ready"), sem("ring_act"), sem("gelu_done"), sem("exp_done")
        pt_ready, mh_ready, tap_ready, silu_done, a_high = (
            sem("pt_ready"), sem("mh_ready"), sem("tap_ready"), sem("silu_done"), sem("a_high"))
        lam_exp, cond_silu, trig_done = sem("lam_exp"), sem("cond_silu"), sem("trig_done")
        lo_ready, acc_free, t_ready, t_low = sem("lo_ready"), sem("acc_free"), sem("t_ready"), sem("t_low")
        mod_ready, applied, ring_dve, pro_free = sem("mod_ready"), sem("applied"), sem("ring_dve"), sem("pro_free")
        cond_ready, dve_order, sc_free, max_ready = sem("cond_ready"), sem("dve_order"), sem("sc_free"), sem("max_ready")
        p_ready, mh_low, a_ready, a_low = sem("p_ready"), sem("mh_low"), sem("a_ready"), sem("a_low")
        rope_in, mla_q_ready, fin_free = sem("rope_in"), sem("mla_q_ready"), sem("fin_free")
        lam_sum, ang_ready = sem("lam_sum"), sem("ang_ready")


        def job(l, j):
            return l * J_LAYER + j

        def sub(l, j):
            return l * SUB_LAYER + sum(SUBS[:j])

        def dropped(l, kind):
            return U_SMALL * (l + (kind != "win"))

        def residual_final(l, which, k):
            return 2 * (l * B_LAYER + (16 if which else -8)) + k + 1

        def first_of(l, row):
            same = [x_ for x_ in phases[l] if x_[:2] == row[:2]]
            return same[0] is row

        UQ_UNITS = range(U_WIN + 3, U_WIN + 6)

        def uq_views(u, t):
            src = raw[:, (u % 4) * UNIT:(u % 4) * UNIT + 8 * 192].rearrange("p (a n) -> p a n", n=192)
            o = (u % 2) * UNIT
            return ((src[:, :, 0:P], t[:, o:o + 8 * P].rearrange("p (a n) -> p a n", n=P)),
                    (src[:, :, P:192], t[:, o + 8 * P:o + 12 * P].rearrange("p (a n) -> p a n", n=64)))

        class Order:

            def __init__(self, eng, s):
                self.eng, self.s, self.n, self.plus = eng, s, 0, 0

            def after(self, ins):
                self.n += 1
                ins.then_inc(self.s, 1)
                self.eng.wait_ge(self.s, self.plus + self.n)

        JOB_SQ = {J_QA: [(z, 18 * S, 512), (z, 20 * S, 512)], J_KVA: [(z, 22 * S, 512)]}
        for v_ in range(2):
            JOB_SQ[J_SGV + v_] = [(z, (28 + 2 * v_) * S, 512)]
        for v_ in range(6):
            JOB_SQ[J_DAQK + v_] = [(z, 2 * v_ * S, 512)]
        for v_ in range(3):
            JOB_SQ[J_MQ + v_] = [(mq, 2 * v_ * S, 512), (mqr, v_ * S, S)]
            JOB_SQ[J_MK + v_] = [(mk, 2 * v_ * S, 512)]
            JOB_SQ[J_O + v_] = [(B_O, 0, 512)]
        JOB_W = {J_N1: (S, D), J_N2: (S, D), J_QA: (S, 512), J_KVA: (S, 256)}
        for v_ in range(2):
            JOB_W[J_SGV + v_] = (512, P)
        for v_ in range(6):
            JOB_W[J_DAQK + v_] = (512, DA_QK)
        for v_ in range(3):
            JOB_W[J_MQ + v_] = JOB_W[J_MK + v_] = (512, 192)
            JOB_W[J_O + v_] = (512, P)

        block = ctx.enter_context(nc.Block())

        @block.sync
        def _(sp):
            def load_unit(u, slot, kt, width, src):
                if not isinstance(u, int) or u >= 4:
                    sp.wait_ge(lo_ready, u - 3)
                dst = raw[:, slot * UNIT:slot * UNIT + kt * width].rearrange("p (k n) -> p k n", k=kt)
                sp.dma_start(dst, src).then_inc(w_loaded[slot], 16)

            def rows_of(w, k0, kt, c0, width):
                return w[k0:k0 + kt * P, bass.ds(c0, width)].rearrange("(k p) n -> p k n", p=P)

            sp.dma_start(xs[:, 0:2 * D].rearrange("p (t d) -> p t d", t=2),
                         x.rearrange("(t p) d -> p t d", p=P)).then_inc(x_loaded, 16)
            for l in range(L):
                for kind, p, first, n, u0, b0, g0 in phases[l]:
                    if kind == "small":
                        load_unit(u0, u0 % 4, 16, 64, rows_of(w_in[l], 0, 16, ROPE_COL, 64))
                        for v in range(2):
                            load_unit(u0 + 1 + v, (u0 + 1 + v) % 4, 2, 768, rows_of(mla_w_ukv[l], 0, 2, v * 768, 768))
                        for v in range(3):
                            load_unit(u0 + 3 + v, (u0 + 3 + v) % 4, 4, 384, rows_of(mla_w_uq[l], 0, 4, v * 384, 384))
                        continue

                    def body(i):
                        pb = sum(PASS_BLOCKS[:p])
                        for v in range(4):
                            b2, s = v // 2, v % 2
                            if kind == "win":
                                w, k0, kt, c0 = w_in[l], 8 * s * P, 8, (2 * (first + i) + b2) * 256 + 64 * (first >= 6)
                            elif kind == "wout":
                                w, k0, kt, c0 = w_out[l], 8 * s * P, 8, (2 * (first + i) + b2) * 256
                            elif kind == "up":
                                w, k0, kt, c0 = ffn_w_up[l], 8 * s * P, 8, (pb + first + i) * 256 + b2 * D_FF
                            else:
                                kt = PASS_BLOCKS[p]
                                w, k0, c0 = ffn_w_down[l], (2 * pb + s * kt) * P, (2 * (first + i) + b2) * 256
                            load_unit(u0 + 4 * i + v, (u0 + v) % 4, kt, 256, rows_of(w, k0, kt, c0, 256))

                    start = 0
                    if l == 0 and u0 == 0:
                        sp.wait_ge(ada_used, 4 * (A_PRO - 2))
                        body(0)
                        start = 1
                    with sp.Fori(start, n) as i:
                        body(i)
            sp.wait_ge(fin_free, 8)
            sp.dma_start(out.rearrange("(t p) d -> p t d", p=P),
                         xs[:, 0:2 * D].rearrange("p (t d) -> p t d", t=2)).then_inc(stored, 16)
            sp.wait_ge(stored, 16)

        @block.gpsimd
        def _(pool):
            def part_of(l, q, c0):
                return w_ada[l, 4 * q * P:(4 * q + 4) * P, bass.ds(c0, 256)].rearrange("(k p) n -> p k n", p=P)

            def slot_of(t, v):
                return t[:, v * 1024:(v + 1) * 1024].rearrange("p (k n) -> p k n", k=4)

            for g in range(A_PRO):
                for q in range(4):
                    m = 4 * g + q
                    if m >= 8:
                        pool.wait_ge(ada_used, m - 7)
                    pool.dma_start(slot_of(apro, m % 8), part_of(0, q, g * 256)).then_inc(ada_loaded[m % 8], 16)

            def load_group(g, lg, l, parts=range(4)):
                for q in parts:
                    pool.wait_ge(ada_used, 4 * g + q - 1)
                    pool.dma_start(slot_of(ada, q % 2), part_of(l, q, lg * 256)).then_inc(ada_loaded[q % 2], 16)

            ahead = False
            for l in range(L):
                for kind, p, first, n, u0, b0, g0 in phases[l]:
                    pb = sum(PASS_BLOCKS[:p])

                    def gated(i):
                        pair = l * (FFC // 4) + pb + first + i
                        pool.wait_ge(silu_done, pair + 1)
                        pool.wait_ge(acc_free, 2 * (b0 + 2 * i) + 4)
                        pool.tensor_tensor(yv[:, 0:512], yv[:, 0:512], yg[:, 0:512], ALU.mult).then_inc(a_ready, 1)
                        pool.wait_ge(a_ready, pair + 1)
                        o = (first + i) * 512
                        pool.tensor_copy(mhi[:, bass.ds(o, 512)], yv[:, 0:512]).then_inc(a_high, 1)
                        pool.wait_ge(a_high, pair + 1)
                        pool.tensor_tensor(mlo[:, bass.ds(o, 512)], yv[:, 0:512], mhi[:, bass.ds(o, 512)].bitcast(F32),
                                           ALU.subtract).then_inc(a_low, 1)

                    def group(i, parts=range(4)):
                        load_group(g0 + i, g0 % A_LAYER + i, g0 // A_LAYER, parts)

                    ada_row = g0 is not None
                    count = A_ATT if kind == "small" else n
                    if ada_row:
                        group(0, range(2 if ahead else 0, 4))
                    if kind == "up":
                        with pool.Fori(1, n) as i:
                            if ada_row:
                                group(i, range(3))
                            gated(i - 1)
                            if ada_row:
                                group(i, (3,))
                    elif ada_row and count > 1:
                        with pool.Fori(1, count) as i:
                            group(i)
                    ahead = False
                    if kind == "up":
                        following = phases[l][phases[l].index((kind, p, first, n, u0, b0, g0)) + 1]
                        if following[6] is not None:
                            load_group(following[6], following[6] % A_LAYER, following[6] // A_LAYER, range(2))
                            ahead = True
                        gated(n - 1)

        @block.tensor
        def _(pe):
            def mm(out_, lhsT, rhs, start, stop):
                return pe.matmul(out_, lhsT, rhs, start=start, stop=stop, skip_group_check=True)

            def three(out_, wh, wl, ah, al, start, stop):
                mm(out_, wh, ah, start, False)
                mm(out_, wh, al, False, False)
                return mm(out_, wl, ah, False, stop)

            pro = [0]

            def pro_bank():
                if pro[0] >= 4:
                    pe.wait_ge(pro_free, pro[0] - 3)
                pro[0] += 1
                return bank[(pro[0] - 1) % 4]

            pe.wait_ge(first_loaded, 16 * N_FIRST)
            b = pro_bank()
            pe.transpose(b[:, 0:KC], rows[0:KC, 0:P], ident[0:KC, 0:KC])
            for l in range(L):
                last = pe.transpose(b[:, 60 + 96 * l:156 + 96 * l], rows[0:96, (1 + l) * P:(2 + l) * P],
                                    ident[0:96, 0:96])
            last.then_inc(pro_full, 1)
            pe.wait_ge(x_loaded, 16)
            for k2 in range(KC // 2):
                b = pro_bank()
                for y in range(4):
                    k, t_ = 2 * k2 + y // 2, y % 2
                    last = pe.transpose(b[:, y * P:(y + 1) * P], xs[:, t_ * D + k * P:t_ * D + (k + 1) * P], ident)
                last.then_inc(pro_full, 1)

            def turn_vectors():
                pe.wait_ge(small_loaded, 16 * N_SMALL)
                b = pro_bank()
                pe.transpose(b[:, 0:60], rows[0:60, 0:P], ident[0:60, 0:60]).then_inc(pro_full, 1)
                for l in range(L):
                    b = pro_bank()
                    for v in range(4):
                        t_ = 3 + 4 * l + v
                        last = pe.transpose(b[:, v * FFC:(v + 1) * FFC], rows[0:FFC, t_ * P:(t_ + 1) * P],
                                            ident[0:FFC, 0:FFC])
                    last.then_inc(pro_full, 1)
                for l in range(L):
                    b = pro_bank()
                    for g in range(SGG):
                        last = pe.transpose(b[:, g * P:(g + 1) * P], wsr[:, l * 512 + g * P:l * 512 + (g + 1) * P],
                                            ident)
                    last.then_inc(pro_full, 1)

            def ada_part(g, q, slot, buf, lap):
                if q == 0 and not (isinstance(g, int) and g == 0):
                    pe.wait_ge(ya_ready, g)
                pe.wait_ge(ada_loaded[slot], 16 * lap)
                for j in range(4):
                    k = 4 * q + j
                    i_ = mm(B_ADA[32 * j:32 * j + 32, 0:256], condr[:, k * 32:(k + 1) * 32],
                            buf[:, slot * 1024 + j * 256:slot * 1024 + (j + 1) * 256], q == 0, q == 3)
                i_.then_inc(ada_used, 1)

            def ada_part_later(g, q):
                ada_part(g, q, q % 2, ada, A_PRO // 2 + 2 * (g - A_PRO) + q // 2 + 1)

            def ada_turn(g):
                pe.wait_ge(ya_ready, g + 1)
                if not (isinstance(g, int) and g == 0):
                    pe.wait_ge(mod_ready, g)
                for v in range(2):
                    i_ = mm(B_MOD[:, v:v + 1], ya[:, v * P:(v + 1) * P], con[:, C_SEL:C_SEL + 1], True, True)
                i_.then_inc(mod_turned, 1)

            def ms(l, j, subs):
                g, n, total = job(l, j), 0, sum(len(x_) for x_ in subs)
                if g >= 2:
                    pe.wait_ge(root_ready, g - 1)
                for v, products in enumerate(subs):
                    pe.wait_ge(sq_ready, sub(l, j) + v + 1)
                    for m_, sq_, (o0, o1) in products:
                        i_ = mm(bank[6 + g % 2][:, o0:o1], m_, sq_, n == 0, n == total - 1)
                        n += 1
                    i_.then_inc(sub_done, 1)

            def sqr(l, j, v, w0, w1):
                o = ((sub(l, j) + v) % 2) * 512
                return sq[:, o + w0:o + w1]

            def ms_all(l, j):
                n = 1 if j in (J_N1, J_N2) else 2
                ms(l, j, [[(ones, sqr(l, j, v, y * S, (y + 1) * S), (0, S)) for y in range(n)] for v in range(SUBS[j])])

            def ms_each(l, j, m_):
                ms(l, j, [[(m_, sqr(l, j, 0, 0, 512), (0, 512))]])

            def ms_mq(l, v):
                ms(l, J_MQ + v, [[(ones, sqr(l, J_MQ + v, 0, 0, 512), (0, 512))],
                                 [(half[y], sqr(l, J_MQ + v, 1, 0, S), (y * S, (y + 1) * S)) for y in range(2)]])

            def ms_mk(l, v):
                ms(l, J_MK + v, [[(ones, sqr(l, J_MK + v, 0, 0, 512), (0, 512))]
                                 + [(half[0], sqkr[:, 0:S], (y * S, (y + 1) * S)) for y in range(2)]])

            pe.wait_ge(cond_ready, 1)
            for g in range(A_PRO):
                for q in range(4):
                    ada_part(g, q, (4 * g + q) % 8, apro, g // 2 + 1)
                    if q == 2 and g >= 1:
                        ada_turn(g - 1)
                if g == 0:
                    ms_all(0, J_N1)
                if g == 3:
                    turn_vectors()
            ada_turn(A_PRO - 1)

            class Fill:

                def __init__(self, g):
                    self.g, self.calls = g, 0

                def __call__(self):
                    v = self.calls
                    self.calls += 1
                    if v < 10:
                        for q in range(2):
                            ada_part_later(self.g + v // 2, 2 * (v % 2) + q)
                    if v % 2 == 0 and v >= 2:
                        ada_turn(self.g + v // 2 - 1)

            def ring(l, e, b0):
                if e < 4:
                    pe.wait_ge(acc_free, 2 * b0)
                elif e - 4 < E_ACT:
                    pe.wait_ge(ring_act, l * E_ACT + e - 3)
                else:
                    pe.wait_ge(ring_dve, l * E_DVE + e - 4 - E_ACT + 1)
                return bank[e % 4]

            def attention_inputs(l, u0, b0, fill):
                item = l * T_LAYER
                b = ring(l, E_KR, b0)
                pe.wait_ge(lo_ready, u0 + 1)
                o = (u0 % 2) * UNIT
                for k in range(KC):
                    i_ = three(b[:, 0:S], whi[:, o + k * 64:o + k * 64 + P], wlo[:, o + k * 64:o + k * 64 + P],
                               ch(hhi, k), ch(hlo, k), k == 0, k == KC - 1)
                i_.then_inc(ring_full, 1)
                fill()
                ms_all(l, J_QA)
                fill()
                ms_all(l, J_KVA)
                for v in range(3):
                    b = ring(l, E_V + v, b0)
                    for y in range(4):
                        k, t_ = 12 + 2 * v + y // 2, y % 2
                        i_ = pe.transpose(b[:, y * P:(y + 1) * P], z[:, k * S + t_ * P:k * S + (t_ + 1) * P], ident)
                    i_.then_inc(ring_full, 1)
                fill()
                pe.wait_ge(t_low, item + T_KVA + 2)
                for v in range(2):
                    u = u0 + 1 + v
                    pe.wait_ge(lo_ready, u + 1)
                    o = (u % 2) * UNIT
                    for y in range(3):
                        b = ring(l, E_UKV + 5 * v + y, b0)
                        for k in range(2):
                            a = o + k * 768 + y * 256
                            i_ = three(b[:, 0:S], whi[:, a:a + P], wlo[:, a:a + P], ch(qahi, 4 + k), ch(qalo, 4 + k),
                                       k == 0, k == 1)
                        i_.then_inc(ring_full, 1)
                    for t_ in range(2):
                        b = ring(l, E_UKV + 5 * v + 3 + t_, b0)
                        for k in range(2):
                            def v_(t):
                                return t[:, o + k * 768:o + (k + 1) * 768].rearrange("p (h n) -> p h n", h=3)[:, :, P:256]
                            c0 = (4 + k) * S + t_ * P
                            i_ = three(b[:, 0:384], qahi[:, c0:c0 + P], qalo[:, c0:c0 + P], v_(whi), v_(wlo),
                                       k == 0, k == 1)
                        i_.then_inc(ring_full, 1)
                fill()
                pe.wait_ge(t_low, item + T_QA + 4)
                for v in range(3):
                    u = u0 + 3 + v
                    pe.wait_ge(lo_ready, u + 1)
                    o = (u % 2) * UNIT
                    for y in range(3):
                        b = ring(l, E_UQ + 3 * v + y, b0)
                        for k in range(4):
                            a = o + ((2 * k + y) * P if y < 2 else (8 + k) * P)
                            i_ = three(b[:, 0:S], whi[:, a:a + P], wlo[:, a:a + P], ch(qahi, k), ch(qalo, k),
                                       k == 0, k == 3)
                        i_.then_inc(ring_full, 1)
                fill()
                ms_each(l, J_SGV, ones)
                ms_each(l, J_SGV + 1, ones)
                ms_each(l, J_DAQK, blk)
                fill()
                ms_each(l, J_DAQK + 1, blk)
                pe.wait_ge(applied, job(l, J_SGV + 1) + 1)
                for v in range(2):
                    b = ring(l, E_VT + v, b0)
                    for y in range(4):
                        k, t_ = 28 + 2 * v + y // 2, y % 2
                        i_ = pe.transpose(b[:, y * P:(y + 1) * P], z[:, k * S + t_ * P:k * S + (t_ + 1) * P], ident)
                    i_.then_inc(ring_full, 1)
                fill()
                for v in range(2, 6):
                    ms_each(l, J_DAQK + v, blk)
                    if v == 3:
                        fill()
                fill()
                for v in range(2):
                    pe.wait_ge(ring_act, l * E_ACT + E_VT + v + 1)
                    b = ring(l, E_SG + v, b0)
                    for y in range(4):
                        g = 2 * v + y // 2
                        i_ = mm(b[:, y * P:(y + 1) * P], vt[:, (4 * v + y) * P:(4 * v + y + 1) * P],
                                wt[:, l * 512 + g * P:l * 512 + (g + 1) * P], True, True)
                    i_.then_inc(ring_full, 1)
                pe.wait_ge(rope_in, 4 * l + 1)
                b = ring(l, E_KROT, b0)
                mm(b[:, 0:S], rot, kr[:, 0:S], True, True).then_inc(ring_full, 1)

                def q_rot(v):
                    pe.wait_ge(rope_in, 4 * l + 2 + v)
                    b = ring(l, E_QROT + v, b0)
                    mm(b[:, 0:S], rot, ch(mqr, v), True, True).then_inc(ring_full, 1)

                ms_mq(l, 0)
                fill()
                ms_mq(l, 1)
                q_rot(0)
                ms_mq(l, 2)
                q_rot(1)
                ms_mk(l, 0)
                q_rot(2)
                ms_mk(l, 1)
                fill()
                ms_mk(l, 2)

            def score(l, i):
                h = i % NH
                if i == 0:
                    pe.wait_ge(ring_act, (l + 1) * E_ACT)
                    pe.wait_ge(ring_dve, (l + 1) * E_DVE)
                    pe.wait_ge(applied, job(l, J_DAQK + 5) + 1)
                else:
                    pe.wait_ge(sc_free, 12 * l + i)
                if i >= NH:
                    pe.wait_ge(mla_q_ready, 3 * l + h // 2 + 1)
                    pe.wait_ge(applied, job(l, J_MK + h // 2) + 1)
                for c0, c1, q0, nk in ((0, P, 0, P), (P, KEYS, P, S)):
                    if i < NH:
                        for y in range(2):
                            i_ = mm(bank[y][:, c0:c1], z[64 * y:64 * y + 64, h * S + q0:h * S + q0 + P],
                                    z[64 * y:64 * y + 64, (NH + h) * S:(NH + h) * S + nk], True, True)
                    else:
                        r0, c_ = 64 * (h % 2), (h // 2) * S
                        mm(bank[0][:, c0:c1], mq[:, h * S + q0:h * S + q0 + P], mk[:, h * S:h * S + nk], True, False)
                        i_ = mm(bank[0][:, c0:c1], mqr[r0:r0 + 64, c_ + q0:c_ + q0 + P],
                                mkr[r0:r0 + 64, c_:c_ + nk], False, True)
                i_.then_inc(sc_full, 1)

            def values(l, i):
                h, o = i % NH, (i % 2) * KEYS
                pe.wait_ge(p_ready, 12 * l + i + 1)
                if i >= 1:
                    pe.wait_ge(pt_ready, 12 * l + i)
                for c0 in (0, P, 2 * P):
                    i_ = pe.transpose(B_PT[:, c0:c0 + P], pr[:, o + c0:o + c0 + P], ident)
                i_.then_inc(pt_full, 1)
                pe.wait_ge(pt_ready, 12 * l + i + 1)
                if i % 2 == 0 and 2 <= i <= NH:
                    pe.wait_ge(t_ready, l * T_LAYER + T_DA + i)
                elif i % 2 == 0 and i > NH:
                    pe.wait_ge(mh_low, l * NH + i - NH)
                v_, d0 = (vda if i < NH else mv), (i % 2) * S
                mm(B_O[:, d0:d0 + S], v_[:, h * S:h * S + P], pt[:, o:o + S], True, False)
                mm(B_O[:, d0 + P:d0 + S], v_[:, h * S + P:(h + 1) * S], pt[:, o + S:o + KEYS], False, True).then_inc(
                    o_full, 1)

            def heads(l, g):
                for i in range(15):
                    if i < 12:
                        score(l, i)
                    if i % 2 == 0 and 4 <= i < 10:
                        ms_each(l, J_O + (i - 4) // 2, ones)
                    if 2 <= i <= 13:
                        values(l, i - 2)
                    if i < 2 * A_HEADS:
                        for q in range(2):
                            ada_part_later(g + i // 2, 2 * (i % 2) + q)
                    if i % 2 == 0 and i >= 2:
                        ada_turn(g + i // 2 - 1)

            def unit(u, slot, b2, s, kt, rhs, waits, acc_wait, after_chunk):
                pe.wait_ge(lo_ready, u + 1)
                for c_ in range(2):
                    acc = bank[2 * b2 + c_][:, 0:S]
                    if s == 0 and acc_wait is not None:
                        pe.wait_ge(acc_free, acc_wait + c_)
                    for j in range(kt):
                        if waits is not None and c_ == 0:
                            waits(s * kt + j)
                        a = slot * UNIT + j * 256 + c_ * P
                        i_ = three(acc, whi[:, a:a + P], wlo[:, a:a + P], ch(rhs[0], s * kt + j),
                                   ch(rhs[1], s * kt + j), s == 0 and j == 0, s == 1 and j == kt - 1)
                    if c_ == 1:
                        i_.then_inc(unit_done, 1)
                    elif s == 1:
                        i_.then_inc(chunk0_done, 1)
                    after_chunk(c_)

            for l in range(L):
                item = l * T_LAYER
                if l > 0:
                    ms_all(l, J_N1)
                for row in phases[l]:
                    kind, p, first, n, u0, b0, g0 = row
                    if kind == "small":
                        attention_inputs(l, u0, b0, Fill(g0))
                        heads(l, g0 + A_FILL)
                        continue
                    begins = first_of(l, row)
                    if kind == "up" and p == 0 and begins:
                        ms_all(l, J_N2)

                    def input_ready(k):
                        if kind == "win":
                            pe.wait_ge(t_low, item + T_N1 + k + 1)
                        elif kind == "up":
                            pe.wait_ge(t_low, item + T_N2 + k + 1)
                        elif kind == "wout" and k < NH:
                            pe.wait_ge(t_low, item + T_DA + k + 1)
                        elif kind == "wout" and k < 2 * NH:
                            pe.wait_ge(mh_low, l * NH + k - NH + 1)
                        elif kind == "down" and k % 2 == 0:
                            pe.wait_ge(a_low, l * (FFC // 4) + sum(PASS_BLOCKS[:p]) + k // 2 + 1)

                    def body(i, waits):
                        for b2 in range(2):
                            acc_wait = 2 * (b0 + 2 * i + b2) - 3
                            if isinstance(acc_wait, int) and acc_wait <= 0:
                                acc_wait = None
                            for s in range(2):
                                v = 2 * b2 + s

                                def after_chunk(c_):
                                    if g0 is None:
                                        return
                                    if c_ == 0:
                                        ada_part_later(g0 + i, v)
                                    elif v == 3:
                                        ada_turn(g0 + i)

                                unit(u0 + 4 * i + v, (u0 + v) % 2, b2, s, PASS_BLOCKS[p] if kind == "down" else 8,
                                     (hhi, hlo) if kind in ("win", "up") else (mhi, mlo),
                                     waits if b2 == 0 else None, acc_wait, after_chunk)

                    start = 0
                    if begins and not (kind == "up" and p > 0):
                        body(0, input_ready)
                        start = 1
                    if start < n:
                        with pe.Fori(start, n) as i:
                            body(i, None)

            for k2 in range(KC // 2):
                pe.wait_ge(acc_free, residual_final(L, 0, 2 * k2 + 1))
                if k2 >= 2:
                    pe.wait_ge(fin_free, k2 - 1)
                for y in range(4):
                    t_, k = y // 2, 2 * k2 + y % 2
                    i_ = pe.transpose(bank[6 + k2 % 2][:, y * P:(y + 1) * P],
                                      xT[:, k * S + t_ * P:k * S + (t_ + 1) * P], ident)
                i_.then_inc(fin_full, 1)

        @block.scalar
        def _(act):
            act.dma_start(con[:, 0:C_N], consts).then_inc(first_loaded, 16)
            act.dma_start(rows[0:KC, 0:P], c.rearrange("a (k p) -> (a k) p", p=P)).then_inc(first_loaded, 16)
            for l in range(L):
                act.dma_start(rows[0:96, (1 + l) * P:(2 + l) * P],
                              b_ada[l].rearrange("(k p) -> k p", p=P)).then_inc(first_loaded, 16)

            def load(dst, src):
                act.dma_start(dst, src).then_inc(small_loaded, 16)
                loads.append(1)

            loads = []
            for l in range(L):
                r0 = KC + G_LAYER * l

                def vector(what, src, n, c0=0, width=P):
                    at_ = gcol(l, what)
                    load(rows[at_:at_ + n, c0:c0 + width], src.rearrange("(k p) -> k p", p=width))

                for y in range(2):
                    vector("qg", da_q_gain[l], 1, 64 * y, 64)
                    vector("kg", da_k_gain[l], 1, 64 * y, 64)
                    vector("mqr", mla_q_gain[l, P:192], 1, 64 * y, 64)
                    vector("mkr", mla_k_gain[l, P:192], 1, 64 * y, 64)
                load(rows[gcol(l, "hg"):gcol(l, "hg") + NH, 0:P], da_head_gain[l])
                vector("qa", mla_q_a_gain[l], 4)
                vector("kva", mla_kv_a_gain[l], 2)
                vector("mqn", mla_q_gain[l, 0:P], 1)
                vector("mkn", mla_k_gain[l, 0:P], 1)
                load(rows[gcol(l, "sgv"):gcol(l, "sgv") + SGG, 0:P], sg_v_gain[l])
                for v in range(3):
                    load(rows[0:FFC, (3 + 4 * l + v) * P:(4 + 4 * l + v) * P],
                         ffn_conv_w[l, v].rearrange("(k p) -> k p", p=P))
                load(rows[0:FFC, (6 + 4 * l) * P:(7 + 4 * l) * P], ffn_conv_b[l].rearrange("(k p) -> k p", p=P))
                load(wsr[:, l * 512:(l + 1) * 512].rearrange("p (g s) -> p g s", g=SGG),
                     sg_w[l].rearrange("g t s -> t g s"))
                load(bs[:, l * 512:(l + 1) * 512], sg_b[l:l + 1].rearrange("a g t -> a (g t)").to_broadcast([P, 512]))
                for v, t in enumerate((da_lq1, da_lk1, da_lq2, da_lk2)):
                    a = (4 * l + v) * DA_QK
                    load(lamr[:, a:a + DA_QK], t[l:l + 1, :].to_broadcast([P, DA_QK]))
            load(posi[:, 0:S], positions.to_broadcast([P, S]))
            with nc.allow_non_contiguous_dma(reason="256 positions, one per partition"):
                load(posi[:, S:S + 2], positions.rearrange("a (t p) -> p (a t)", p=P))
            assert len(loads) == N_SMALL, len(loads)

            act.wait_ge(pro_free, 1)
            act.activation(sml[:, 32:48], cols[:, 0:KC], ACT.Silu).then_inc(cond_silu, 1)

            def copy(out_, in_):
                return act.activation(out_, in_, ACT.Copy)

            def split_hi(v4, laps):
                act.wait_ge(w_loaded[v4], 16 * (laps + 1))
                o = (v4 % 2) * UNIT
                copy(whi[:, o:o + UNIT], raw[:, v4 * UNIT:(v4 + 1) * UNIT]).then_inc(hi_ready, 1)

            def split_small(l, u0, v):
                u = u0 + v
                act.wait_ge(ring_full, l * (E_ACT + E_DVE) + (E_V, E_UKV + 5, E_UKV + 10, E_UQ + 3, E_UQ + 6,
                                                              E_UQ + 9)[v - 2])
                if v < 3 or v >= 6:
                    split_hi(u % 4, u // 4)
                    return
                act.wait_ge(w_loaded[u % 4], 16 * (u // 4 + 1))
                for src, dst in uq_views(u, whi):
                    i_ = copy(dst, src)
                i_.then_inc(hi_ready, 1)

            def ada_copy(g):
                act.wait_ge(ada_used, 4 * g + 4)
                if not (isinstance(g, int) and g == 0):
                    act.wait_ge(mod_turned, g)
                copy(ya[:, 0:256], B_ADA[:, 0:256]).then_inc(ya_ready, 1)

            def squares(l, j):
                for v, (t, c0, w) in enumerate(JOB_SQ[j]):
                    s_ = sub(l, j) + v
                    act.wait_ge(sub_done, s_ - 1)
                    if j in (J_SGV, J_SGV + 1):
                        act.wait_ge(gelu_done, 2 * l + 2)
                    act.activation(sq[:, (s_ % 2) * 512:(s_ % 2) * 512 + w], t[:, c0:c0 + w], ACT.Square).then_inc(
                        sq_ready, 1)

            def root(l, j):
                g, (w, n) = job(l, j), JOB_W[j]
                act.wait_ge(sub_done, sub(l, j) + SUBS[j])
                if g >= 2:
                    act.wait_ge(applied, g - 1)
                act.activation(r[:, (g % 2) * 512:(g % 2) * 512 + w], bank[6 + g % 2][:, 0:w], ACT.Sqrt,
                               bias=con[:, C_EPS:C_EPS + 1], scale=1.0 / n).then_inc(root_ready, 1)

            def item_hi(idx, dst):
                act.wait_ge(t_ready, idx + 1)
                copy(dst, ch(T, idx % 4)).then_inc(t_high, 1)

            def trunk_squares(l, j):
                for k in range(KC):
                    s_ = sub(l, j) + k
                    if l == 0 and j == J_N1:
                        act.wait_ge(pro_free, PRO_X + k // 2 + 1)
                    else:
                        act.wait_ge(acc_free, residual_final(l, j == J_N2, k))
                    if s_ >= 2:
                        act.wait_ge(sub_done, s_ - 1)
                    act.activation(sq[:, (s_ % 2) * 512:(s_ % 2) * 512 + S], ch(xT, k), ACT.Square).then_inc(
                        sq_ready, 1)
                root(l, j)

            def trunk(l, j, t0):
                if l > 0 or j == J_N2:
                    trunk_squares(l, j)
                for k in range(KC):
                    idx, shift = l * T_LAYER + t0 + k, 96 * l + 48 * (j == J_N2) + k
                    act.wait_ge(t_ready, idx + 1)
                    act.activation(ch(hhi, k), ch(T, idx % 4), ACT.Identity, bias=mod[:, shift:shift + 1]).then_inc(
                        t_high, 1)

            def attention(l, u0, b0, ga):
                item, e = l * T_LAYER, [0]
                act.wait_ge(acc_free, 2 * b0)
                squares(l, J_QA)
                squares_kva = True
                root(l, J_QA)
                squares(l, J_KVA)
                root(l, J_KVA)
                for k in range(6):
                    item_hi(item + T_QA + k, ch(qahi, k))
                ada_copy(ga)

                def ring_copy(*pairs):
                    act.wait_ge(ring_full, l * (E_ACT + E_DVE) + e[0] + 1)
                    for dst, src in pairs:
                        i_ = copy(dst, src)
                    i_.then_inc(ring_act, 1)
                    e[0] += 1

                def rb():
                    return bank[e[0] % 4]

                split_small(l, u0, 2)
                act.wait_ge(ring_full, l * (E_ACT + E_DVE) + e[0] + 1)
                b = rb()
                copy(kr[0:64, 0:S], b[0:64, 0:S])
                act.activation(sqkr[:, 0:S], b[:, 0:S], ACT.Square)
                copy(kr[64:P, 0:S], b[0:64, 0:S]).then_inc(ring_act, 1)
                e[0] += 1
                for v in range(3):
                    ring_copy((vda[:, v * 512:(v + 1) * 512], rb()[:, :]))
                act.activation(ch(z, 24, 4), ch(z, 24, 4), ACT.Gelu_apprx_tanh).then_inc(gelu_done, 1)
                act.activation(ch(z, 28, 4), ch(z, 28, 4), ACT.Gelu_apprx_tanh).then_inc(gelu_done, 1)
                for v in range(2):
                    for y in range(3):
                        ring_copy((ch(mk, 3 * v + y), rb()[:, 0:S]))
                    for t_ in range(2):
                        dst = mv[:, 3 * v * S:3 * (v + 1) * S].rearrange("p (h t d) -> p h t d", h=3, t=2)[:, :, t_, :]
                        ring_copy((dst, rb()[:, 0:384].rearrange("p (h d) -> p h d", h=3)))
                    split_small(l, u0, 3 + v)
                for v in range(3):
                    ring_copy((ch(mq, 2 * v), rb()[:, 0:S]))
                    ring_copy((ch(mq, 2 * v + 1), rb()[:, 0:S]))
                    ring_copy((ch(mqr, v), rb()[:, 0:S]))
                    split_small(l, u0, 5 + v)
                    if v == 0:
                        ada_copy(ga + 1)
                jobs = list(range(J_SGV, J_O))
                squares(l, jobs[0])
                for n_, j in enumerate(jobs):
                    if n_ + 1 < len(jobs):
                        squares(l, jobs[n_ + 1])
                    root(l, j)
                    if j == J_DAQK:
                        ada_copy(ga + 2)
                    if j == J_DAQK + 3:
                        ada_copy(ga + 3)
                    if j == J_MQ:
                        ada_copy(ga + 4)
                    if j == J_DAQK + 1:
                        for v in range(2):
                            ring_copy((vt[:, v * 512:(v + 1) * 512], rb()[:, :]))
                    if j == J_DAQK + 5:
                        for g in range(SGG):
                            item_hi(item + T_SG + g, ch(mhi, 12 + g))
                assert e[0] == E_ACT
                for i in range(15):
                    if i % 2 == 0 and i >= 2:
                        ada_copy(ga + A_FILL + i // 2 - 1)
                    if i % 2 == 0 and i >= 4:
                        pair = (i - 4) // 2
                        if pair < 3:
                            root(l, J_O + pair)
                            for y in range(2):
                                item_hi(item + T_DA + 2 * pair + y, ch(mhi, 2 * pair + y))
                        else:
                            act.wait_ge(o_full, 12 * l + 2 * pair + 2)
                            for y in range(2):
                                h = 2 * (pair - 3) + y
                                copy(ch(mhi, NH + h), B_O[:, y * S:(y + 1) * S]).then_inc(mh_ready, 1)
                    if 2 <= i <= 13:
                        v = i - 2
                        act.wait_ge(pt_full, 12 * l + v + 1)
                        if v >= 2:
                            act.wait_ge(o_full, 12 * l + v - 1)
                        copy(pt[:, (v % 2) * KEYS:(v % 2 + 1) * KEYS], B_PT[:, 0:KEYS]).then_inc(pt_ready, 1)
                    if i < 12:
                        o, st = (i % 2) * 2 * KEYS, (i % 2) * 16
                        act.wait_ge(max_ready, 12 * l + i + 1)
                        for s_ in range(2 if i < NH else 1):
                            for qb, (c0, c1) in enumerate(((0, P), (P, KEYS))):
                                v = 2 * s_ + qb
                                a = sc_s[:, o + s_ * KEYS + c0:o + s_ * KEYS + c1]
                                i_ = act.activation(a, a, ACT.Exp, bias=stat[:, st + 4 + v:st + 5 + v],
                                                    accum_out=stat[:, st + 8 + v:st + 9 + v])
                        i_.then_inc(exp_done, 1)
                    if i % 2 == 1 and 3 <= i < 9:
                        act.wait_ge(o_full, 12 * l + i - 1)
                        squares(l, J_O + (i - 3) // 2)

            trunk_squares(0, J_N1)
            for g in range(A_PRO):
                ada_copy(g)
                if g == 6:
                    act.wait_ge(lam_sum, 1)
                    act.activation(sml[:, 4:8], sml[:, 0:4], ACT.Exp).then_inc(lam_exp, 1)
                if g == 9:
                    act.wait_ge(ang_ready, 1)
                    act.activation(sin[:, 0:S], ang[:, 0:S], ACT.Sin).then_inc(trig_done, 1)
                    act.activation(cos[:, 0:S], ang[:, S:2 * S], ACT.Sin).then_inc(trig_done, 1)
            split_hi(0, 0)
            split_hi(1, 0)
            for l in range(L):
                trunk(l, J_N1, T_N1)
                for row in phases[l]:
                    kind, p, first, n, u0, b0, g0 = row
                    if kind == "small":
                        attention(l, u0, b0, g0)
                        continue
                    if kind == "up" and p == 0 and first_of(l, row):
                        trunk(l, J_N2, T_N2)

                    d0 = u0 - dropped(l, kind)

                    def body(i, ending=False):
                        pb = sum(PASS_BLOCKS[:p])
                        for b2 in range(2):
                            for v in (2 * b2 + 2, 2 * b2 + 3):
                                if not (ending and b2 == 1):
                                    act.wait_ge(unit_done, d0 + 4 * i + v - 1)
                                    split_hi((u0 + v) % 4, (u0 + v) // 4 + i)
                                if v == 4 and g0 is not None:
                                    ada_copy(g0 + i)
                            if kind == "win":
                                for c_ in range(2):
                                    if c_ == 0:
                                        act.wait_ge(chunk0_done, b0 + 2 * i + b2 + 1)
                                    else:
                                        act.wait_ge(unit_done, d0 + 4 * i + 2 * b2 + 2)
                                    copy(ch(z, (first + i) * 4 + 2 * b2 + c_), bank[2 * b2 + c_][:, 0:S]).then_inc(
                                        acc_free, 1)
                            if kind == "up":
                                y_ = yv if b2 else yg
                                pair = l * (FFC // 4) + pb + first + i
                                for c_ in range(2):
                                    if c_ == 0:
                                        act.wait_ge(chunk0_done, b0 + 2 * i + b2 + 1)
                                        if not isinstance(pair, int) or pair >= 1:
                                            act.wait_ge(a_ready if b2 == 0 else a_low, pair)
                                    else:
                                        act.wait_ge(unit_done, d0 + 4 * i + 2 * b2 + 2)
                                    cc = COL_CONV + 4 * FFC * l + 2 * (pb + first + i) + (FFC // 2) * b2 + c_
                                    act.activation(ch(y_, c_), bank[2 * b2 + c_][:, 0:S], ACT.Identity,
                                                   bias=cols[:, bass.ds(cc + 3 * FFC, 1)],
                                                   scale=cols[:, bass.ds(cc + 2 * FFC, 1)]).then_inc(tap_ready, 1)
                        if kind == "up":
                            act.wait_ge(acc_free, 2 * (b0 + 2 * i) + 2)
                            act.activation(yg[:, 0:512], yg[:, 0:512], ACT.Silu).then_inc(silu_done, 1)

                    ends = l == L - 1 and row is phases[l][-1]
                    if n - ends > 0:
                        with act.Fori(0, n - ends) as i:
                            body(i)
                    if ends:
                        body(n - 1, True)
            for k2 in range(0, KC // 2, 1):
                act.wait_ge(fin_full, k2 + 1)
                dst = xs[:, 0:2 * D].rearrange("p (t d) -> p t d", t=2)[:, :, k2 * S:(k2 + 1) * S]
                copy(dst, bank[6 + k2 % 2][:, :].rearrange("p (t d) -> p t d", t=2)).then_inc(fin_free, 1)

        @block.vector
        def _(dve):
            order = Order(dve, dve_order)
            stt, ts, tt = dve.scalar_tensor_tensor, dve.tensor_scalar, dve.tensor_tensor

            dve.wait_ge(pro_full, 1)
            dve.tensor_copy(cols[:, 0:KC], bank[0][:, 0:KC])
            dve.tensor_copy(cols[:, COL_BADA:COL_CONV], bank[0][:, 60:252]).then_inc(pro_free, 1)
            dve.wait_ge(cond_silu, 1)
            dve.tensor_copy(condr[:, 0:KC * 32].rearrange("p (k m) -> p k m", m=32),
                            sml[:, 32:48].unsqueeze(2).to_broadcast([P, KC, 32])).then_inc(cond_ready, 1)
            for k2 in range(KC // 2):
                dve.wait_ge(pro_full, PRO_X + k2 + 1)
                dve.tensor_copy(xT[:, k2 * 512:(k2 + 1) * 512], bank[(PRO_X + k2) % 4][:, :]).then_inc(pro_free, 1)

            def vectors():
                e = PRO_VEC
                dve.wait_ge(pro_full, e + 1)
                dve.tensor_copy(cols[:, KC:COL_BADA], bank[e % 4][:, KC:COL_BADA]).then_inc(pro_free, 1)
                for l in range(L):
                    e += 1
                    dve.wait_ge(pro_full, e + 1)
                    dve.tensor_copy(cols[:, COL_CONV + 4 * FFC * l:COL_CONV + 4 * FFC * (l + 1)],
                                    bank[e % 4][:, 0:4 * FFC]).then_inc(pro_free, 1)
                for l in range(L):
                    e += 1
                    dve.wait_ge(pro_full, e + 1)
                    tt(wt[:, l * 512:(l + 1) * 512].rearrange("p (g t) -> p g t", g=SGG),
                       bank[e % 4][:, :].rearrange("p (g t) -> p g t", g=SGG),
                       tril.unsqueeze(1).to_broadcast([P, SGG, P]), ALU.mult).then_inc(pro_free, 1)
                dve.wait_ge(pro_free, PRO_VEC + 1)

            def lambdas():
                for l in range(L):
                    a = cols[:, gcol(l, "hg"):gcol(l, "hg") + NH]
                    order.after(ts(a, a, 1.0 - LAM_INIT[l], None, ALU.mult))
                lv = lamr[:, 0:L * 4 * DA_QK].rearrange("p (a b d) -> p a b d", b=2, d=DA_QK)
                order.after(tt(lv[:, :, 0, :], lv[:, :, 0, :], lv[:, :, 1, :], ALU.mult))
                dve.tensor_reduce(sml[:, 0:4], lv[:, :, 0, :], AX_X, ALU.add).then_inc(lam_sum, 1)
                dve.wait_ge(lam_exp, 1)
                for l in range(L):
                    order.after(tt(sml[:, 8 + l:9 + l], sml[:, 5 + 2 * l:6 + 2 * l], sml[:, 4 + 2 * l:5 + 2 * l],
                                   ALU.subtract))
                    order.after(ts(sml[:, 8 + l:9 + l], sml[:, 8 + l:9 + l], -LAM_INIT[l], None, ALU.add))

            def places():
                dve.tensor_copy(sml[:, 48:50], posi[:, S:S + 2])
                order.after(dve.tensor_copy(ang[:, 0:S], posi[:, 0:S]))
                ts(dist[:, 0:P], ang[:, 0:P], sml[:, 48:49], None, ALU.subtract)
                order.after(ts(dist[:, P:KEYS], ang[:, 0:S], sml[:, 49:50], None, ALU.subtract))
                order.after(stt(dist[:, 0:KEYS], dist[:, 0:KEYS], -1.0, dist[:, 0:KEYS], ALU.mult, ALU.max))
                order.after(ts(ang[:, 0:S], ang[:, 0:S], con[:, C_INV:C_INV + 1], None, ALU.mult))
                order.after(ts(rt_tmp[:, 0:S], ang[:, 0:S], 1.0 / TURN, ROUND, ALU.mult, ALU.add))
                order.after(ts(rt_tmp[:, 0:S], rt_tmp[:, 0:S], -ROUND, None, ALU.add))
                for part in TURN_PARTS:
                    order.after(stt(ang[:, 0:S], rt_tmp[:, 0:S], -part, ang[:, 0:S], ALU.mult, ALU.add))
                order.after(ts(ang[:, 0:S], ang[:, 0:S], PI_, -PI_, ALU.min, ALU.max))
                order.after(stt(rt_tmp[:, 0:S], ang[:, 0:S], -1.0, ang[:, 0:S], ALU.mult, ALU.max))
                ts(ang[:, S:2 * S], rt_tmp[:, 0:S], -1.0, TURN / 4, ALU.mult, ALU.add).then_inc(ang_ready, 1)

            def split_lo(u, v4):
                dve.wait_ge(hi_ready, u + 1)
                o = (v4 % 2) * UNIT
                tt(wlo[:, o:o + UNIT], raw[:, v4 * UNIT:(v4 + 1) * UNIT], whi[:, o:o + UNIT].bitcast(F32),
                   ALU.subtract).then_inc(lo_ready, 1)

            def split_lo_static(u):
                if u % U_LAYER in UQ_UNITS:
                    dve.wait_ge(hi_ready, u + 1)
                    for (src, dst), (_, hi) in zip(uq_views(u, wlo), uq_views(u, whi)):
                        i_ = tt(dst, src, hi.bitcast(F32), ALU.subtract)
                    i_.then_inc(lo_ready, 1)
                    return
                split_lo(u, u % 4)

            def mod_add(g):
                dve.wait_ge(mod_turned, g + 1)
                dst = mod[:, bass.ds(2 * g, 2)]
                tt(dst, B_MOD[:, 0:2], cols[:, bass.ds(COL_BADA + 2 * g, 2)], ALU.add).then_inc(mod_ready, 1)

            def t_free(idx):
                if idx >= 4:
                    dve.wait_ge(t_low, idx - 3)

            def item_lo(idx, hi, dst):
                dve.wait_ge(t_high, idx + 1)
                tt(dst, ch(T, idx % 4), hi.bitcast(F32), ALU.subtract).then_inc(t_low, 1)

            def inverse(l, j):
                g, w = job(l, j), JOB_W[j][0]
                dve.wait_ge(root_ready, g + 1)
                a = r[:, (g % 2) * 512:(g % 2) * 512 + w]
                order.after(dve.reciprocal(a, a))
                return a

            def trunk(l, j, t0, part):
                dve.wait_ge(mod_ready, A_LAYER * l + 8 * (part + 2))
                m0 = 96 * l + 16 * part
                order.after(ts(sml[:, 16:32], mod[:, m0 + 16:m0 + 32], 1.0, None, ALU.add))
                a = first_inverse if l == 0 and j == J_N1 else inverse(l, j)
                for k in range(KC + 1):
                    idx = l * T_LAYER + t0 + k
                    if k < KC:
                        t_free(idx)
                        i_ = stt(ch(T, idx % 4), ch(xT, k), sml[:, 16 + k:17 + k], a, ALU.mult, ALU.mult)
                        i_.then_inc(t_ready, 1)
                    if k >= 1:
                        dve.wait_ge(t_high, idx)
                        stt(ch(hlo, k - 1), ch(T, (idx - 1) % 4), mod[:, m0 + k - 1:m0 + k], ch(hhi, k - 1).bitcast(F32),
                            ALU.add, ALU.subtract).then_inc(t_low, 1)
                dve.engine_nop().then_inc(applied, 1)

            def g_(l, what, i=0):
                a = gcol(l, what, i)
                return cols[:, a:a + 1]

            def attention(l, u0, b0, ga):
                item = l * T_LAYER
                for j, t0, n, z0, what in ((J_QA, T_QA, 4, 18, "qa"), (J_KVA, T_KVA, 2, 22, "kva")):
                    a = inverse(l, j)
                    for k in range(n + 1):
                        idx = item + t0 + k
                        if k < n:
                            t_free(idx)
                            stt(ch(T, idx % 4), ch(z, z0 + k), g_(l, what, k), a, ALU.mult, ALU.mult).then_inc(t_ready, 1)
                        if k >= 1:
                            c_ = k - 1 + (4 if j == J_KVA else 0)
                            item_lo(idx - 1, ch(qahi, c_), ch(qalo, c_))
                    dve.engine_nop().then_inc(applied, 1)
                for v in range(2, 8):
                    split_lo_static(u0 + v)
                    if v == 2:
                        mod_add(ga)
                mod_add(ga + 1)
                for v in range(2):
                    a = inverse(l, J_SGV + v)
                    for y in range(2):
                        k = 2 * v + y
                        i_ = stt(ch(z, 28 + k), ch(z, 28 + k), g_(l, "sgv", k), a[:, y * S:(y + 1) * S],
                                 ALU.mult, ALU.mult)
                    i_.then_inc(applied, 1)

                def pair(j, t, k, gain):
                    a = inverse(l, j)
                    stt(ch(t, k, 2), ch(t, k, 2), gain, a, ALU.mult, ALU.mult).then_inc(applied, 1)

                for v in range(6):
                    pair(J_DAQK + v, z, 2 * v, g_(l, "qg" if v < 3 else "kg"))
                    if v == 2:
                        mod_add(ga + 2)
                    if v == 5:
                        mod_add(ga + 3)
                    if v == 1:
                        ts(kr[:, 0:S], kr[:, 0:S], g_(l, "mkr"), None, ALU.mult).then_inc(rope_in, 1)

                def ring_wait(e):
                    dve.wait_ge(ring_full, l * (E_ACT + E_DVE) + e + 1)
                    return bank[e % 4]

                for v in range(2):
                    b = ring_wait(E_SG + v)
                    bias = bs[:, l * 512 + v * S:l * 512 + (v + 1) * S].rearrange("p (g t) -> p g t", g=2)
                    ts_ = [ch(T, (T_SG + 2 * v + y) % 4) for y in range(2)]
                    t_free(item + T_SG + 2 * v + 1)
                    for y in range(2):
                        i_ = tt(ts_[y].rearrange("p (n t) -> p n t", n=2),
                                b[:, y * S:(y + 1) * S].rearrange("p (n t) -> p n t", n=2),
                                bias[:, y, :].unsqueeze(1).to_broadcast([P, 2, P]), ALU.add)
                    i_.then_inc(ring_dve, 1)
                    dve.wait_ge(ring_dve, l * E_DVE + v + 1)
                    for y in range(2):
                        tt(ts_[y], ts_[y], ch(z, 24 + 2 * v + y), ALU.mult).then_inc(t_ready, 1)
                    for y in range(2):
                        k = 2 * v + y
                        item_lo(item + T_SG + k, ch(mhi, 12 + k), ch(mlo, 12 + k))

                def rotate(e, t, done=None):
                    b = ring_wait(e)
                    tt(rt_tmp[:, 0:S], b[:, 0:S], sin[:, 0:S], ALU.mult).then_inc(ring_dve, 1)
                    order.after(tt(t, t, cos[:, 0:S], ALU.mult))
                    dve.wait_ge(ring_dve, l * E_DVE + e - E_SG + 1)
                    i_ = tt(t, t, rt_tmp[:, 0:S], ALU.add)
                    if done is None:
                        order.after(i_)
                    else:
                        i_.then_inc(done, 1)

                def mla_q(v):
                    a = inverse(l, J_MQ + v)
                    for y in range(2):
                        t_ = mqr[64 * y:64 * y + 64, v * S:(v + 1) * S]
                        i_ = stt(t_, t_, g_(l, "mqr")[64 * y:64 * y + 64, :], a[64 * y:64 * y + 64, y * S:(y + 1) * S],
                                 ALU.mult, ALU.mult)
                    i_.then_inc(rope_in, 1)
                    stt(ch(mq, 2 * v, 2), ch(mq, 2 * v, 2), g_(l, "mqn"), a, ALU.mult, ALU.mult).then_inc(applied, 1)

                def mla_k(v):
                    a = inverse(l, J_MK + v)
                    for y in range(2):
                        tt(mkr[64 * y:64 * y + 64, v * S:(v + 1) * S], kr[64 * y:64 * y + 64, 0:S],
                           a[64 * y:64 * y + 64, y * S:(y + 1) * S], ALU.mult)
                    stt(ch(mk, 2 * v, 2), ch(mk, 2 * v, 2), g_(l, "mkn"), a, ALU.mult, ALU.mult).then_inc(applied, 1)

                rotate(E_KROT, kr[:, 0:S])
                mla_q(0)
                mla_q(1)
                rotate(E_QROT, ch(mqr, 0), mla_q_ready)
                mla_q(2)
                mod_add(ga + 4)
                rotate(E_QROT + 1, ch(mqr, 1), mla_q_ready)
                mla_k(0)
                rotate(E_QROT + 2, ch(mqr, 2), mla_q_ready)
                mla_k(1)
                mla_k(2)

                def maxima(i):
                    ns, o, st = (2 if i < NH else 1), (i % 2) * 2 * KEYS, (i % 2) * 16
                    dve.wait_ge(sc_full, 12 * l + i + 1)
                    if i >= 2:
                        dve.wait_ge(p_ready, 12 * l + i - 1)
                    for s_ in range(ns):
                        i_ = stt(sc_s[:, o + s_ * KEYS:o + (s_ + 1) * KEYS], bank[s_][:, 0:KEYS],
                                 DA_SCALE if i < NH else MLA_SCALE, mask, ALU.mult, ALU.add)
                    i_.then_inc(sc_free, 1)
                    dve.wait_ge(sc_free, 12 * l + i + 1)
                    if i < NH:
                        for s_ in range(2):
                            a = sc_s[:, o + s_ * KEYS:o + (s_ + 1) * KEYS]
                            i_ = stt(a, dist[:, 0:KEYS], -SLOPES[i], a, ALU.mult, ALU.add)
                        order.after(i_)
                    for s_ in range(ns):
                        for qb, (c0, c1) in enumerate(((0, P), (P, KEYS))):
                            v = 2 * s_ + qb
                            i_ = dve.tensor_reduce(stat[:, st + v:st + v + 1],
                                                   sc_s[:, o + s_ * KEYS + c0:o + s_ * KEYS + c1], AX_X, ALU.max)
                    order.after(i_)
                    ts(stat[:, st + 4:st + 4 + 2 * ns], stat[:, st:st + 2 * ns], -1.0, None, ALU.mult).then_inc(
                        max_ready, 1)

                def probabilities(i):
                    ns, o, st = (2 if i < NH else 1), (i % 2) * 2 * KEYS, (i % 2) * 16
                    dve.wait_ge(exp_done, 12 * l + i + 1)
                    order.after(dve.reciprocal(stat[:, st + 12:st + 12 + 2 * ns], stat[:, st + 8:st + 8 + 2 * ns]))
                    if i < NH:
                        a = stat[:, st + 14:st + 16]
                        order.after(ts(a, a, sml[:, 8 + l:9 + l], None, ALU.mult))
                    if i >= 2:
                        dve.wait_ge(pt_full, 12 * l + i - 1)
                    for s_ in reversed(range(ns)):
                        for qb, (c0, c1) in enumerate(((0, P), (P, KEYS))):
                            dst = pr[:, (i % 2) * KEYS + c0:(i % 2) * KEYS + c1]
                            e_ = sc_s[:, o + s_ * KEYS + c0:o + s_ * KEYS + c1]
                            cf = stat[:, st + 12 + 2 * s_ + qb:st + 13 + 2 * s_ + qb]
                            if s_ == ns - 1:
                                i_ = ts(dst, e_, cf, None, ALU.mult)
                            else:
                                i_ = stt(dst, e_, cf, dst, ALU.mult, ALU.add)
                        if s_ == 0:
                            i_.then_inc(p_ready, 1)
                        else:
                            order.after(i_)

                for i in range(15):
                    if i < 12:
                        maxima(i)
                    if i % 2 == 0 and i >= 4:
                        v = (i - 4) // 2
                        if v < 3:
                            a = inverse(l, J_O + v)
                            for y in range(2):
                                h = 2 * v + y
                                t_free(item + T_DA + h)
                                stt(ch(T, (T_DA + h) % 4), B_O[:, y * S:(y + 1) * S], g_(l, "hg", h), a[:, y * S:(y + 1) * S],
                                    ALU.mult, ALU.mult).then_inc(t_ready, 1)
                            dve.engine_nop().then_inc(applied, 1)
                            for y in range(2):
                                item_lo(item + T_DA + 2 * v + y, ch(mhi, 2 * v + y), ch(mlo, 2 * v + y))
                        else:
                            dve.wait_ge(mh_ready, l * NH + 2 * (v - 3) + 2)
                            for y in range(2):
                                h = 2 * (v - 3) + y
                                tt(ch(mlo, NH + h), B_O[:, y * S:(y + 1) * S], ch(mhi, NH + h).bitcast(F32),
                                   ALU.subtract).then_inc(mh_low, 1)
                    if 1 <= i <= 12:
                        probabilities(i - 1)
                    if i % 2 == 0 and i >= 2:
                        mod_add(ga + A_FILL + i // 2 - 1)

            first_inverse = inverse(0, J_N1)
            for g in range(A_PRO):
                mod_add(g)
                if g == 2:
                    vectors()
                if g == 5:
                    lambdas()
                if g == 8:
                    places()
                if g == 12:
                    dve.wait_ge(trig_done, 2)
            split_lo_static(0)
            split_lo_static(1)
            for l in range(L):
                trunk(l, J_N1, T_N1, 0)
                for row in phases[l]:
                    kind, p, first, n, u0, b0, g0 = row
                    if kind == "small":
                        attention(l, u0, b0, g0)
                        continue
                    if kind == "up" and p == 0 and first_of(l, row):
                        trunk(l, J_N2, T_N2, 3)
                    if kind in ("wout", "down"):
                        dve.wait_ge(mod_ready, A_LAYER * l + (24 if kind == "wout" else 48))
                    pb = sum(PASS_BLOCKS[:p])
                    d0 = u0 - dropped(l, kind)
                    links = {"up": 4, "down": 0, "wout": 0, "win": 0}[kind]

                    def body(i, ending=False):
                        n0 = order.n
                        order.plus = links * i
                        for b2 in range(2):
                            for v in (2 * b2 + 2, 2 * b2 + 3):
                                if not (ending and b2 == 1):
                                    split_lo(u0 + 4 * i + v, (u0 + v) % 4)
                            if kind == "win":
                                continue
                            for c_ in range(2):
                                acc = bank[2 * b2 + c_]
                                if kind == "up":
                                    dve.wait_ge(tap_ready, tap0 + 4 * i + 2 * b2 + c_ + 1)
                                    y_ = ch(yv if b2 else yg, c_)
                                    cc = COL_CONV + 4 * FFC * l + 2 * (pb + first + i) + (FFC // 2) * b2 + c_
                                    order.after(stt(y_[:, 1:S], acc[:, 0:S - 1], cols[:, bass.ds(cc + FFC, 1)],
                                                    y_[:, 1:S], ALU.mult, ALU.add))
                                    stt(y_[:, 2:S], acc[:, 0:S - 2], cols[:, bass.ds(cc, 1)],
                                        y_[:, 2:S], ALU.mult, ALU.add).then_inc(acc_free, 1)
                                else:
                                    if c_ == 0:
                                        dve.wait_ge(chunk0_done, b0 + 2 * i + b2 + 1)
                                    else:
                                        dve.wait_ge(unit_done, d0 + 4 * i + 2 * b2 + 2)
                                    k = 4 * (first + i) + 2 * b2 + c_
                                    gate = 96 * l + 16 * (2 if kind == "wout" else 5) + k
                                    xa = xT[:, bass.ds(k * S, S)]
                                    stt(xa, acc[:, 0:S], mod[:, bass.ds(gate, 1)], xa, ALU.mult, ALU.add).then_inc(
                                        acc_free, 1)
                        if g0 is not None:
                            mod_add(g0 + i)
                        assert order.n - n0 == links
                        order.plus = 0
                        return n0

                    pair0 = l * (FFC // 4) + pb + first
                    tap0 = 4 * pair0
                    ends = l == L - 1 and row is phases[l][-1]
                    m = n - ends
                    if m > 0:
                        with dve.Fori(0, m) as i:
                            n0 = body(i)
                        order.n = n0 + links * m
                    if ends:
                        body(n - 1, True)


_INS = ['x', 'c', 'positions', 'w_ada', 'b_ada', 'w_in', 'da_q_gain', 'da_k_gain', 'da_lq1', 'da_lk1', 'da_lq2',
        'da_lk2', 'da_head_gain', 'mla_q_a_gain', 'mla_w_uq', 'mla_kv_a_gain', 'mla_w_ukv', 'mla_q_gain',
        'mla_k_gain', 'sg_v_gain', 'sg_w', 'sg_b', 'w_out', 'ffn_w_up', 'ffn_conv_w', 'ffn_conv_b', 'ffn_w_down']


def shape_constants():
    a = np.zeros((P, C_N), np.float32)
    p = np.arange(P)[:, None]
    f = np.arange(P)[None, :]
    a[:, C_ID:C_ID + P] = p == f
    a[:, C_ONE:C_ONE + P] = 1.0
    a[:, C_BLK:C_BLK + P] = p // 64 == f // 64
    a[:, C_H0:C_H0 + P] = p < 64
    a[:, C_H1:C_H1 + P] = p >= 64
    a[:, C_ROT:C_ROT + P] = np.where((f % 64 < 32) & (p == f + 32), -1.0, 0.0) + np.where(
        (f % 64 >= 32) & (p == f - 32), 1.0, 0.0)
    a[:, C_TRIL:C_TRIL + P] = p <= f
    for c0, q0, n in ((0, 0, P), (P, P, S)):
        k = np.arange(n)[None, :]
        a[:, C_MASK + c0:C_MASK + c0 + n] = np.where(k // 64 <= (q0 + p) // 64, 0.0, -1e30)
    a[::32, C_SEL] = 1.0
    a[:, C_INV] = np.float32(10000.0) ** (-(np.arange(P) % 32).astype(np.float32) / np.float32(32))
    a[:, C_EPS] = EPS
    return a


def kernel(**inputs):
    import concourse.bacc as _bacc
    from concourse.bass_utils import run_bass_kernel_spmd as _run

    nc = _bacc.Bacc("TRN2", target_bir_lowering=False, num_devices=1)
    arrays, args = {}, []
    for name in ['consts'] + _INS:
        a = shape_constants() if name == 'consts' else np.ascontiguousarray(inputs[name])
        if name == 'x':
            a = a.reshape(S, D)
        arrays[f"in_{name}_dram"] = a
        args.append(nc.dram_tensor(f"in_{name}_dram", a.shape, mybir.dt.from_np(a.dtype), kind="ExternalInput").ap())
    args.append(nc.dram_tensor("out_0_dram", (S, D), F32, kind="ExternalOutput").ap())
    bass_trunk(nc, *args)
    res = _run(nc, [arrays], core_ids=[0])
    return res.results[0]["out_0_dram"].reshape(1, S, D)
```

```python
from contextlib import ExitStack

import numpy as np
import concourse.bass as bass
from concourse import mybir

ALU = mybir.AluOpType
ACT = mybir.ActivationFunctionType
AX_X = mybir.AxisListType.X
F32 = mybir.dt.float32
F32R = mybir.dt.float32r
I32 = mybir.dt.int32

P = 128
D = 2048
S = 256
L = 2
KC = D // P
NH = 6
DA_QK = 64
SGG = 4
D_FF = 5632
EPS = 1e-6
ROPE_COL = 3072
LAM_INIT = [0.8 - 0.6 * float(np.exp(-0.3 * l)) for l in range(L)]
SLOPES = [2.0 ** (-8.0 * (h + 1) / NH) for h in range(NH)]
DA_SCALE = DA_QK ** -0.5
MLA_SCALE = 192 ** -0.5
KEYS = 384

C_ID, C_ONE, C_BLK, C_ROT, C_TRIL, C_MASK = (P * i for i in range(6))
C_SEL = C_MASK + KEYS
C_INV = C_SEL + 1
C_EPS = C_INV + 1
C_ROW2 = C_EPS + 1
C_ROW1 = C_ROW2 + 2 * (2 * NH - 2) + 2
C_N = C_ROW1 + 2 * (NH - 1) + 1

G_LAYER = 22


def gcol(l, what, i=0):
    at = {"qg": 0, "kg": 1, "hg": 2, "qa": 8, "kva": 12, "mqn": 14, "mqr": 15, "mkn": 16, "mkr": 17, "sgv": 18}
    return KC + G_LAYER * l + at[what] + i


COL_BADA = KC + G_LAYER * L
COL_CONV = COL_BADA + 96 * L
FFC = 2 * D_FF // P
N_COLS = COL_CONV + 4 * FFC * L

U_WIN, U_SMALL, U_WOUT = 32, 6, 16
PASS_BLOCKS = (8, 8, 6)
U_LAYER = U_WIN + U_SMALL + U_WOUT + sum(4 * b + 16 for b in PASS_BLOCKS)
B_LAYER = 16 + 8 + sum(2 * b + 8 for b in PASS_BLOCKS)
UNIT = 2048

A_LAYER = 48
A_PRO = 16
PRO_ORDER = [g // 2 + (A_PRO // 2) * (g % 2) for g in range(A_PRO)]
PRO_CHUNKS = {11: (0, 6), 12: (6, 12), 13: (12, 14), 15: (14, 16)}
A_FILL, A_HEADS = 5, 7
A_ATT = A_FILL + A_HEADS
A_ALL = A_LAYER * L


def make_phases():
    g = A_PRO
    out = []
    for l in range(L):
        rows = []
        u, b = l * U_LAYER, l * B_LAYER

        def add(kind, p, first, n):
            nonlocal g, u, b
            i = 0
            while i < n:
                with_ada = g < A_ALL
                m = n - i
                if with_ada:
                    m = min(m, A_LAYER - g % A_LAYER)
                rows.append((kind, p, first + i, m, u, b, g if with_ada else None))
                if with_ada:
                    g += m
                u += 4 * m
                b += 2 * m
                i += m

        add("win", 0, 0, 6)
        add("win", 0, 6, 2)
        rows.append(("small", 0, 0, 1, u, b, g))
        g += A_ATT
        u += U_SMALL
        add("wout", 0, 0, 4)
        pb = 0
        for p, nb in enumerate(PASS_BLOCKS):
            add("up", p, 0, nb)
            add("down", p, 0, 4)
            pb += nb
        assert u == (l + 1) * U_LAYER and b == (l + 1) * B_LAYER
        out.append(rows)
    assert g == A_ALL, g
    return out


J_N1, J_QA, J_KVA, J_DAQ, J_DAK, J_SGV, J_MK, J_MQ, J_O, J_N2 = range(10)
J_LAYER = 10
SUBS = [16, 2, 1, 3, 3, 2, 3, 6, 3, 16]
SUB_LAYER = sum(SUBS)
T_N1, T_QA, T_KVA, T_SG, T_DA, T_N2 = 0, 16, 20, 22, 26, 32
T_LAYER = 48
RING = (("kr", 1, "act"), ("v", 3, "act"), ("ukv", 10, "act"), ("krot", 1, "dve"), ("dak", 3, "dve"),
        ("uq", 9, "act"), ("vt", 2, "act"), ("mk", 3, "dve"), ("qrot", 3, "dve"), ("sg", 2, "dve"))
RING_BY = [by for _, n, by in RING for _ in range(n)]
RING_N = len(RING_BY)
RING_OF = {"act": RING_BY.count("act"), "dve": RING_BY.count("dve")}


def entry(what, i=0):
    at = 0
    for name, n, _ in RING:
        if name == what:
            return at + i
        at += n


def evacuated(l, e):
    return RING_BY[e], l * RING_OF[RING_BY[e]] + RING_BY[:e + 1].count(RING_BY[e])


R_DA, R_MQ, R_SG, R_N = 0, 24, 36, 44


N_FIRST = 2 + L
N_SMALL = L * (8 + 6 + 4 + 1 + 1 + 4) + 2
PRO_X, PRO_VEC = 1, 1 + KC // 2
TURN = 2 * float(np.pi)
ROUND = 1.5 * 2.0 ** 23
TURN_PARTS = (6.28125, round((TURN - 6.28125) * 2 ** 21) / 2 ** 21, TURN - 6.28125 - round((TURN - 6.28125) * 2 ** 21) / 2 ** 21)
PI_ = 3.1415925


def bass_trunk(nc, consts, x, c, positions, w_ada, b_ada, w_in, da_q_gain, da_k_gain, da_lq1, da_lk1,
               da_lq2, da_lk2, da_head_gain, mla_q_a_gain, mla_w_uq, mla_kv_a_gain, mla_w_ukv,
               mla_q_gain, mla_k_gain, sg_v_gain, sg_w, sg_b, w_out, ffn_w_up, ffn_conv_w,
               ffn_conv_b, ffn_w_down, out):
    phases = make_phases()
    with ExitStack() as ctx:
        def sb(name, cols, dt=F32):
            return ctx.enter_context(nc.sbuf_tensor(name, [P, cols], dt))

        def sem(name):
            return ctx.enter_context(nc.semaphore(name))

        base = nc.sbuf_base
        arena = ctx.enter_context(nc.sbuf_tensor("arena", [P, 52 * 1024 - 256], F32))
        at = [(base + 31) // 32 * 32]
        end = at[0] + (52 * 1024 - 256) * 4

        def place(name, cols, dt=F32, offset=None):
            if offset is None:
                offset = at[0]
                at[0] += (cols * 4 + 31) // 32 * 32
                assert at[0] <= end, (name, at[0], end)
            return nc.alloc_sbuf_tensor_at(name, [P, cols], dt, offset=offset), offset

        raw, _ = place("raw", 4 * UNIT)
        whi, _ = place("whi", 2 * UNIT, F32R)
        wlo, _ = place("wlo", 2 * UNIT, F32R)
        ada, _ = place("ada", 2 * 1024)
        xT, _ = place("xT", KC * S)
        hhi, o_h = place("hhi", KC * S, F32R)
        hlo, _ = place("hlo", KC * S, F32R)
        mhi, o_m = place("mhi", KC * S, F32R)
        mlo, _ = place("mlo", KC * S, F32R)
        z, _ = place("z", 32 * S, offset=o_m)
        apro, _ = place("apro", 8 * 1024, offset=o_m)
        xs, _ = place("xs", 2 * D, offset=o_h)
        rows, _ = place("rows", 11 * P, offset=o_h + 4 * 2 * D)
        wsr, _ = place("wsr", L * 512, offset=o_h + 4 * (2 * D + 11 * P))
        posi, _ = place("posi", S + 2, I32, offset=o_h + 4 * (2 * D + 11 * P + L * 512))
        lamr, _ = place("lamr", L * 4 * DA_QK, offset=o_h + 4 * (2 * D + 11 * P + L * 512 + 264))
        ang, _ = place("ang", 2 * S, offset=o_h + 4 * (2 * D + 11 * P + L * 512 + 264 + 512))
        vda, _ = place("vda", NH * S, offset=o_h)
        mq, _ = place("mq", NH * S, offset=o_h + 4 * 1536)
        mk, _ = place("mk", NH * S, offset=o_h + 4 * 3072)
        mv, _ = place("mv", NH * S, offset=o_h + 4 * 4608)
        mqr, _ = place("mqr", 3 * S, offset=o_h + 4 * 6144)
        mkr, _ = place("mkr", 3 * S, offset=o_h + 4 * 6912)
        kr, _ = place("kr", S, offset=o_h + 4 * 7680)
        sqkr, _ = place("sqkr", S, offset=o_h + 4 * 7936)
        o_s = at[0]
        sc_s, _ = place("sc_s", 2 * 2 * KEYS)
        pr, _ = place("pr", 2 * KEYS)
        pt, _ = place("pt", 2 * KEYS)
        qahi, _ = place("qahi", 6 * S, F32R, offset=o_s)
        qalo, _ = place("qalo", 6 * S, F32R, offset=o_s + 4 * 6 * S)
        yg, _ = place("yg", 2 * S, offset=o_s)
        yv, _ = place("yv", 2 * S, offset=o_s + 4 * 2 * S)
        vt, _ = place("vt", 4 * S)
        con, _ = place("con", C_N)
        cols, _ = place("cols", N_COLS)
        mod, _ = place("mod", 96 * L)
        condr, _ = place("condr", KC * 32)
        bs, _ = place("bs", L * 512)
        wt, _ = place("wt", L * 512)
        dist, _ = place("dist", KEYS)
        cos, _ = place("cos", S)
        sin, _ = place("sin", S)
        sq, _ = place("sq", 2 * 512)
        r, _ = place("r", 2 * 512)
        T, _ = place("T", 4 * S)
        ya, _ = place("ya", 256)
        stat, _ = place("stat", 2 * 16)
        sml, _ = place("sml", 64)
        rt_tmp, _ = place("rt_tmp", S)
        rtok, _ = place("rtok", R_N)

        bank = [ctx.enter_context(nc.psum_tensor(f"bank{i}", [P, 512], F32)) for i in range(8)]
        B_ADA, B_MOD, B_O, B_PT = bank[4], bank[5], bank[3], bank[2]

        def ch(t, k, n=1):
            return t[:, bass.ds(k * S, n * S)] if not isinstance(k, int) else t[:, k * S:(k + n) * S]

        ident, ones, blk = con[:, C_ID:C_ID + P], con[:, C_ONE:C_ONE + P], con[:, C_BLK:C_BLK + P]
        halves, one = con[:, C_BLK:C_BLK + P:64], con[:, C_ONE:C_ONE + 1]
        rot, tril = con[:, C_ROT:C_ROT + P], con[:, C_TRIL:C_TRIL + P]
        mask = con[:, C_MASK:C_MASK + KEYS]

        w_loaded = [sem(f"w_loaded{i}") for i in range(4)]
        ada_loaded = [sem(f"ada_loaded{i}") for i in range(8)]
        x_loaded, first_loaded, small_loaded, stored = (
            sem("x_loaded"), sem("first_loaded"), sem("small_loaded"), sem("stored"))
        unit_done, chunk0_done = sem("unit_done"), sem("chunk0_done")
        ada_used, mod_turned = sem("ada_used"), sem("mod_turned")
        sub_done, ring_full = sem("sub_done"), sem("ring_full")
        pro_full, spread_full = sem("pro_full"), sem("spread_full")
        sc_full, pt_full, o_full, fin_full = sem("sc_full"), sem("pt_full"), sem("o_full"), sem("fin_full")
        hi_ready, sq_ready, root_ready, t_high = sem("hi_ready"), sem("sq_ready"), sem("root_ready"), sem("t_high")
        ya_ready, ring_act, gelu_done, exp_done = sem("ya_ready"), sem("ring_act"), sem("gelu_done"), sem("exp_done")
        pt_ready, mh_ready, tap_ready, silu_done, a_high = (
            sem("pt_ready"), sem("mh_ready"), sem("tap_ready"), sem("silu_done"), sem("a_high"))
        o_taken = sem("o_taken")
        lam_exp, cond_silu, trig_done = sem("lam_exp"), sem("cond_silu"), sem("trig_done")
        lo_ready, acc_free, t_ready, t_low = sem("lo_ready"), sem("acc_free"), sem("t_ready"), sem("t_low")
        mod_ready, applied, ring_dve, pro_free = sem("mod_ready"), sem("applied"), sem("ring_dve"), sem("pro_free")
        cond_ready, dve_order, sc_free, max_ready = sem("cond_ready"), sem("dve_order"), sem("sc_free"), sem("max_ready")
        p_ready, mh_low, a_ready, a_low = sem("p_ready"), sem("mh_low"), sem("a_ready"), sem("a_low")
        rope_in, fin_free = sem("rope_in"), sem("fin_free")
        lam_sum, ang_ready, spread_free = sem("lam_sum"), sem("ang_ready"), sem("spread_free")


        def job(l, j):
            return l * J_LAYER + j

        def sub(l, j):
            return l * SUB_LAYER + sum(SUBS[:j])

        def dropped(l, kind):
            return U_SMALL * (l + (kind != "win"))

        def residual_final(l, which, k):
            return 2 * (l * B_LAYER + (16 if which else -8)) + k + 1

        def first_of(l, row):
            same = [x_ for x_ in phases[l] if x_[:2] == row[:2]]
            return same[0] is row

        UQ_UNITS = range(U_WIN + 3, U_WIN + 6)

        def uq_views(u, t):
            src = raw[:, (u % 4) * UNIT:(u % 4) * UNIT + 8 * 192].rearrange("p (a n) -> p a n", n=192)
            o = (u % 2) * UNIT
            return ((src[:, :, 0:P], t[:, o:o + 8 * P].rearrange("p (a n) -> p a n", n=P)),
                    (src[:, :, P:192], t[:, o + 8 * P:o + 12 * P].rearrange("p (a n) -> p a n", n=64)))

        class Order:

            def __init__(self, eng, s):
                self.eng, self.s, self.n, self.plus = eng, s, 0, 0

            def after(self, ins):
                self.n += 1
                ins.then_inc(self.s, 1)
                self.eng.wait_ge(self.s, self.plus + self.n)

        JOB_SQ = {J_QA: [(z, 18 * S, 512), (z, 20 * S, 512)], J_KVA: [(z, 22 * S, 512)],
                  J_DAQ: [(z, 2 * v_ * S, 512) for v_ in range(3)],
                  J_DAK: [(z, (NH + 2 * v_) * S, 512) for v_ in range(3)],
                  J_SGV: [(z, (28 + 2 * v_) * S, 512) for v_ in range(2)],
                  J_MK: [(mk, 2 * v_ * S, 512) for v_ in range(3)],
                  J_MQ: [x_ for v_ in range(3) for x_ in ((mq, 2 * v_ * S, 512), (mqr, v_ * S, S))],
                  J_O: [(B_O, 0, 512)] * 3}
        JOB_W = {J_N1: (P, S, D, None), J_N2: (P, S, D, None), J_QA: (P, S, 512, None), J_KVA: (P, S, 256, None),
                 J_DAQ: (P, 24, DA_QK, R_DA), J_DAK: (2 * NH, S, DA_QK, None), J_SGV: (P, 8, P, R_SG),
                 J_MK: (NH, S, 192, None), J_MQ: (P, 12, 192, R_MQ),
                 J_O: (NH, S, P, None)}

        def roots(l, j):
            (rows_, w, _, keep), g = JOB_W[j], job(l, j)
            return r[0:rows_, (g % 2) * 512:(g % 2) * 512 + w] if keep is None else rtok[:, keep:keep + w]

        block = ctx.enter_context(nc.Block())

        @block.sync
        def _(sp):
            def load_unit(u, slot, kt, width, src):
                if not isinstance(u, int) or u >= 4:
                    sp.wait_ge(lo_ready, u - 3)
                dst = raw[:, slot * UNIT:slot * UNIT + kt * width].rearrange("p (k n) -> p k n", k=kt)
                sp.dma_start(dst, src).then_inc(w_loaded[slot], 16)

            def rows_of(w, k0, kt, c0, width):
                return w[k0:k0 + kt * P, bass.ds(c0, width)].rearrange("(k p) n -> p k n", p=P)

            sp.dma_start(xs[:, 0:2 * D].rearrange("p (t d) -> p t d", t=2),
                         x.rearrange("(t p) d -> p t d", p=P)).then_inc(x_loaded, 16)
            def load(dst, src):
                sp.dma_start(dst, src).then_inc(small_loaded, 16)
                loads.append(1)

            loads = []
            for l in range(L):
                r0 = KC + G_LAYER * l

                def vector(what, src, n, c0=0, width=P):
                    at_ = gcol(l, what)
                    load(rows[at_:at_ + n, c0:c0 + width], src.rearrange("(k p) -> k p", p=width))

                for y in range(2):
                    vector("qg", da_q_gain[l], 1, 64 * y, 64)
                    vector("kg", da_k_gain[l], 1, 64 * y, 64)
                    vector("mqr", mla_q_gain[l, P:192], 1, 64 * y, 64)
                    vector("mkr", mla_k_gain[l, P:192], 1, 64 * y, 64)
                load(rows[gcol(l, "hg"):gcol(l, "hg") + NH, 0:P], da_head_gain[l])
                vector("qa", mla_q_a_gain[l], 4)
                vector("kva", mla_kv_a_gain[l], 2)
                vector("mqn", mla_q_gain[l, 0:P], 1)
                vector("mkn", mla_k_gain[l, 0:P], 1)
                load(rows[gcol(l, "sgv"):gcol(l, "sgv") + SGG, 0:P], sg_v_gain[l])
                for v in range(3):
                    load(rows[0:FFC, (3 + 4 * l + v) * P:(4 + 4 * l + v) * P],
                         ffn_conv_w[l, v].rearrange("(k p) -> k p", p=P))
                load(rows[0:FFC, (6 + 4 * l) * P:(7 + 4 * l) * P], ffn_conv_b[l].rearrange("(k p) -> k p", p=P))
                load(wsr[:, l * 512:(l + 1) * 512].rearrange("p (g s) -> p g s", g=SGG),
                     sg_w[l].rearrange("g t s -> t g s"))
                load(bs[:, l * 512:(l + 1) * 512], sg_b[l:l + 1].rearrange("a g t -> a (g t)").to_broadcast([P, 512]))
                for v, t in enumerate((da_lq1, da_lk1, da_lq2, da_lk2)):
                    a = (4 * l + v) * DA_QK
                    load(lamr[:, a:a + DA_QK], t[l:l + 1, :].to_broadcast([P, DA_QK]))
            load(posi[:, 0:S], positions.to_broadcast([P, S]))
            with nc.allow_non_contiguous_dma(reason="256 positions, one per partition"):
                load(posi[:, S:S + 2], positions.rearrange("a (t p) -> p (a t)", p=P))
            assert len(loads) == N_SMALL, len(loads)

            for l in range(L):
                for kind, p, first, n, u0, b0, g0 in phases[l]:
                    if kind == "small":
                        load_unit(u0, u0 % 4, 16, 64, rows_of(w_in[l], 0, 16, ROPE_COL, 64))
                        for v in range(2):
                            load_unit(u0 + 1 + v, (u0 + 1 + v) % 4, 2, 768, rows_of(mla_w_ukv[l], 0, 2, v * 768, 768))
                        for v in range(3):
                            load_unit(u0 + 3 + v, (u0 + 3 + v) % 4, 4, 384, rows_of(mla_w_uq[l], 0, 4, v * 384, 384))
                        continue

                    def body(i):
                        pb = sum(PASS_BLOCKS[:p])
                        for v in range(4):
                            b2, s = v // 2, v % 2
                            if kind == "win":
                                w, k0, kt, c0 = w_in[l], 8 * s * P, 8, (2 * (first + i) + b2) * 256 + 64 * (first >= 6)
                            elif kind == "wout":
                                w, k0, kt, c0 = w_out[l], 8 * s * P, 8, (2 * (first + i) + b2) * 256
                            elif kind == "up":
                                w, k0, kt, c0 = ffn_w_up[l], 8 * s * P, 8, (pb + first + i) * 256 + b2 * D_FF
                            else:
                                kt = PASS_BLOCKS[p]
                                w, k0, c0 = ffn_w_down[l], (2 * pb + s * kt) * P, (2 * (first + i) + b2) * 256
                            load_unit(u0 + 4 * i + v, (u0 + v) % 4, kt, 256, rows_of(w, k0, kt, c0, 256))

                    start = 0
                    if l == 0 and u0 == 0:
                        sp.wait_ge(ada_used, 4 * (A_PRO - 4))
                        body(0)
                        start = 1
                    with sp.Fori(start, n) as i:
                        body(i)
            for q in range(4):
                sp.wait_ge(fin_free, 2 * q + 2)
                c0, c1 = q * (D // 4), (q + 1) * (D // 4)
                sp.dma_start(out[:, c0:c1].rearrange("(t p) d -> p t d", p=P),
                             xs[:, 0:2 * D].rearrange("p (t d) -> p t d", t=2)[:, :, c0:c1]).then_inc(stored, 16)
            sp.wait_ge(stored, 16 * 4)

        @block.gpsimd
        def _(pool):
            def part_of(l, q, c0):
                return w_ada[l, 4 * q * P:(4 * q + 4) * P, bass.ds(c0, 256)].rearrange("(k p) n -> p k n", p=P)

            def slot_of(t, v):
                return t[:, v * 1024:(v + 1) * 1024].rearrange("p (k n) -> p k n", k=4)

            for g in range(A_PRO):
                for q in range(4):
                    m = 4 * g + q
                    if m >= 8:
                        pool.wait_ge(ada_used, m - 7)
                    pool.dma_start(slot_of(apro, m % 8), part_of(0, q, PRO_ORDER[g] * 256)).then_inc(ada_loaded[m % 8], 16)

            def load_group(g, lg, l, parts=range(4)):
                for q in parts:
                    pool.wait_ge(ada_used, 4 * g + q - 1)
                    pool.dma_start(slot_of(ada, q % 2), part_of(l, q, lg * 256)).then_inc(ada_loaded[q % 2], 16)

            ahead = False
            for l in range(L):
                for kind, p, first, n, u0, b0, g0 in phases[l]:
                    pb = sum(PASS_BLOCKS[:p])

                    def gated(i):
                        pair = l * (FFC // 4) + pb + first + i
                        pool.wait_ge(silu_done, pair + 1)
                        pool.wait_ge(acc_free, 2 * (b0 + 2 * i) + 4)
                        pool.tensor_tensor(yv[:, 0:512], yv[:, 0:512], yg[:, 0:512], ALU.mult).then_inc(a_ready, 1)
                        pool.wait_ge(a_ready, pair + 1)
                        o = (first + i) * 512
                        pool.tensor_copy(mhi[:, bass.ds(o, 512)], yv[:, 0:512]).then_inc(a_high, 1)
                        pool.wait_ge(a_high, pair + 1)
                        pool.tensor_tensor(mlo[:, bass.ds(o, 512)], yv[:, 0:512], mhi[:, bass.ds(o, 512)].bitcast(F32),
                                           ALU.subtract).then_inc(a_low, 1)

                    def group(i, parts=range(4)):
                        load_group(g0 + i, g0 % A_LAYER + i, g0 // A_LAYER, parts)

                    ada_row = g0 is not None
                    count = A_ATT if kind == "small" else n
                    if ada_row:
                        group(0, range(2 if ahead else 0, 4))
                    if kind == "up":
                        with pool.Fori(1, n) as i:
                            if ada_row:
                                group(i, range(3))
                            gated(i - 1)
                            if ada_row:
                                group(i, (3,))
                    elif ada_row and count > 1:
                        with pool.Fori(1, count) as i:
                            group(i)
                    ahead = False
                    if kind == "up":
                        following = phases[l][phases[l].index((kind, p, first, n, u0, b0, g0)) + 1]
                        if following[6] is not None:
                            load_group(following[6], following[6] % A_LAYER, following[6] // A_LAYER, range(2))
                            ahead = True
                        gated(n - 1)

        @block.tensor
        def _(pe):
            def mm(out_, lhsT, rhs, start, stop):
                return pe.matmul(out_, lhsT, rhs, start=start, stop=stop, skip_group_check=True)

            def three(out_, wh, wl, ah, al, start, stop):
                mm(out_, wh, ah, start, False)
                mm(out_, wh, al, False, False)
                return mm(out_, wl, ah, False, stop)

            pro = [0]

            def pro_bank():
                if pro[0] >= 4:
                    pe.wait_ge(pro_free, pro[0] - 3)
                pro[0] += 1
                return bank[(pro[0] - 1) % 4]

            pe.wait_ge(first_loaded, 16 * N_FIRST)
            b = pro_bank()
            pe.transpose(b[:, 0:KC], rows[0:KC, 0:P], ident[0:KC, 0:KC])
            for l in range(L):
                last = pe.transpose(b[:, 60 + 96 * l:156 + 96 * l], rows[0:96, (1 + l) * P:(2 + l) * P],
                                    ident[0:96, 0:96])
            last.then_inc(pro_full, 1)

            def turn_x():
                pe.wait_ge(x_loaded, 16)
                for k2 in range(KC // 2):
                    b = pro_bank()
                    for y in range(4):
                        k, t_ = 2 * k2 + y // 2, y % 2
                        last = pe.transpose(b[:, y * P:(y + 1) * P], xs[:, t_ * D + k * P:t_ * D + (k + 1) * P], ident)
                    last.then_inc(pro_full, 1)

            def turn_vectors():
                pe.wait_ge(small_loaded, 16 * N_SMALL)
                b = pro_bank()
                pe.transpose(b[:, 0:60], rows[0:60, 0:P], ident[0:60, 0:60]).then_inc(pro_full, 1)
                for l in range(L):
                    b = pro_bank()
                    for v in range(4):
                        t_ = 3 + 4 * l + v
                        last = pe.transpose(b[:, v * FFC:(v + 1) * FFC], rows[0:FFC, t_ * P:(t_ + 1) * P],
                                            ident[0:FFC, 0:FFC])
                    last.then_inc(pro_full, 1)
                for l in range(L):
                    b = pro_bank()
                    for g in range(SGG):
                        last = pe.transpose(b[:, g * P:(g + 1) * P], wsr[:, l * 512 + g * P:l * 512 + (g + 1) * P],
                                            ident)
                    last.then_inc(pro_full, 1)

            def ada_part(g, q, slot, buf, lap):
                if q == 0 and not (isinstance(g, int) and g == 0):
                    pe.wait_ge(ya_ready, g)
                pe.wait_ge(ada_loaded[slot], 16 * lap)
                for j in range(4):
                    k = 4 * q + j
                    i_ = mm(B_ADA[32 * j:32 * j + 32, 0:256], condr[:, k * 32:(k + 1) * 32],
                            buf[:, slot * 1024 + j * 256:slot * 1024 + (j + 1) * 256], q == 0, q == 3)
                i_.then_inc(ada_used, 1)

            def ada_part_later(g, q):
                ada_part(g, q, q % 2, ada, A_PRO // 2 + 2 * (g - A_PRO) + q // 2 + 1)

            def ada_turn(g):
                pe.wait_ge(ya_ready, g + 1)
                if not (isinstance(g, int) and g == 0):
                    pe.wait_ge(mod_ready, g)
                for v in range(2):
                    i_ = mm(B_MOD[:, v:v + 1], ya[:, v * P:(v + 1) * P], con[:, C_SEL:C_SEL + 1], True, True)
                i_.then_inc(mod_turned, 1)

            def ms(l, j, subs, only=None):
                g, n, total = job(l, j), 0, sum(len(x_) for x_ in subs)
                if g >= 2:
                    pe.wait_ge(root_ready, g - 1)
                for v, products in enumerate(subs):
                    if only is not None and v != only:
                        n += len(products)
                        continue
                    pe.wait_ge(sq_ready, sub(l, j) + v + 1)
                    for a_, b_, n_, (o0, o1) in products:
                        i_ = mm(bank[6 + g % 2][0:n_, o0:o1], a_, b_, n == 0, n == total - 1)
                        n += 1
                    i_.then_inc(sub_done, 1)

            def sqr(l, j, v, w0, w1):
                o = ((sub(l, j) + v) % 2) * 512
                return sq[:, o + w0:o + w1]

            def ms_all(l, j):
                n = 1 if j in (J_N1, J_N2) else 2
                ms(l, j, [[(ones, sqr(l, j, v, y * S, (y + 1) * S), P, (0, S)) for y in range(n)] for v in range(SUBS[j])])

            def ms_rows(l, j, window, step, extra=(), only=None):
                n_ = NH * step
                subs = [[(window[:, n_ - step * (c_ + 1):2 * n_ - step * (c_ + 1)],
                          sqr(l, j, c_ // 2, (c_ % 2) * S, (c_ % 2 + 1) * S), n_, (0, S)) for c_ in (2 * v, 2 * v + 1)] for v in range(3)]
                subs[-1] += extra
                ms(l, j, subs, only)

            def ms_tokens(l, j, v, width, out_, moving):
                n = JOB_SQ[j][v][2] // S
                return [(sqr(l, j, v, y * S + t * P, y * S + (t + 1) * P), moving, P, (out_(y, t), out_(y, t) + width))
                        for y in range(n) for t in range(2)]

            pe.wait_ge(cond_ready, 1)
            for g in range(A_PRO):
                for q in range(4):
                    ada_part(g, q, (4 * g + q) % 8, apro, g // 2 + 1)
                    if q == 2 and g >= 1:
                        ada_turn(g - 1)
                if g == 2:
                    turn_x()
                if g == 3:
                    ms_all(0, J_N1)
                if g == 5:
                    turn_vectors()
            ada_turn(A_PRO - 1)

            class Fill:

                def __init__(self, g):
                    self.g, self.calls = g, 0

                def __call__(self):
                    v = self.calls
                    self.calls += 1
                    if v < 10:
                        for q in range(2):
                            ada_part_later(self.g + v // 2, 2 * (v % 2) + q)
                    if v % 2 == 0 and v >= 2:
                        ada_turn(self.g + v // 2 - 1)

            def ring(l, e, b0):
                if e < 4:
                    pe.wait_ge(acc_free, 2 * b0)
                else:
                    by, count = evacuated(l, e - 4)
                    pe.wait_ge(ring_act if by == "act" else ring_dve, count)
                return bank[e % 4]

            def attention_inputs(l, u0, b0, fill):
                item = l * T_LAYER
                b = ring(l, entry("kr"), b0)
                pe.wait_ge(lo_ready, u0 + 1)
                o = (u0 % 2) * UNIT
                for k in range(KC):
                    i_ = three(b[:, 0:S], whi[:, o + k * 64:o + k * 64 + P], wlo[:, o + k * 64:o + k * 64 + P],
                               ch(hhi, k), ch(hlo, k), k == 0, k == KC - 1)
                i_.then_inc(ring_full, 1)
                fill()
                ms_all(l, J_QA)
                ms_all(l, J_KVA)
                fill()
                for v in range(3):
                    b = ring(l, entry("v", v), b0)
                    for y in range(4):
                        k, t_ = 12 + 2 * v + y // 2, y % 2
                        i_ = pe.transpose(b[:, y * P:(y + 1) * P], z[:, k * S + t_ * P:k * S + (t_ + 1) * P], ident)
                    i_.then_inc(ring_full, 1)
                ms(l, J_DAQ, [ms_tokens(l, J_DAQ, v, 2, lambda y, t, v=v: 12 * t + 2 * (2 * v + y), halves)
                              for v in range(3)])
                ms_rows(l, J_DAK, con[:, C_ROW2:C_ROW2 + 22], 2)
                fill()
                pe.wait_ge(t_low, item + T_KVA + 2)
                for v in range(2):
                    u = u0 + 1 + v
                    pe.wait_ge(lo_ready, u + 1)
                    o = (u % 2) * UNIT
                    for y in range(3):
                        b = ring(l, entry("ukv", 5 * v + y), b0)
                        for k in range(2):
                            a = o + k * 768 + y * 256
                            i_ = three(b[:, 0:S], whi[:, a:a + P], wlo[:, a:a + P], ch(qahi, 4 + k), ch(qalo, 4 + k),
                                       k == 0, k == 1)
                        i_.then_inc(ring_full, 1)
                    for t_ in range(2):
                        b = ring(l, entry("ukv", 5 * v + 3 + t_), b0)
                        for k in range(2):
                            def v_(t):
                                return t[:, o + k * 768:o + (k + 1) * 768].rearrange("p (h n) -> p h n", h=3)[:, :, P:256]
                            c0 = (4 + k) * S + t_ * P
                            i_ = three(b[:, 0:384], qahi[:, c0:c0 + P], qalo[:, c0:c0 + P], v_(whi), v_(wlo),
                                       k == 0, k == 1)
                        i_.then_inc(ring_full, 1)
                    if v == 0:
                        fill()
                pe.wait_ge(rope_in, 2 * l + 1)
                b = ring(l, entry("krot"), b0)
                mm(b[:, 0:S], rot, kr[:, 0:S], True, True).then_inc(ring_full, 1)
                pe.wait_ge(applied, job(l, J_DAK) + 1)
                for v in range(3):
                    b = ring(l, entry("dak", v), b0)
                    for y in range(4):
                        row, p0 = 4 * v + y, 64 * (y % 2)
                        i_ = mm(b[p0:p0 + 64, (y // 2) * S:(y // 2 + 1) * S],
                                ident[0:2 * NH, row:row + 1].to_broadcast([2 * NH, 64]), roots(l, J_DAK), True, True)
                    i_.then_inc(ring_full, 1)
                fill()
                ms(l, J_SGV, [ms_tokens(l, J_SGV, v, 1, lambda y, t, v=v: 4 * t + 2 * v + y, one) for v in range(2)])
                ms_rows(l, J_MK, con[:, C_ROW1:C_ROW1 + 11], 1, [(blk[:, 0:NH], sqkr[:, 0:S], NH, (0, S))])
                fill()
                pe.wait_ge(t_low, item + T_QA + 4)
                for v in range(3):
                    u = u0 + 3 + v
                    pe.wait_ge(lo_ready, u + 1)
                    o = (u % 2) * UNIT
                    for y in range(3):
                        b = ring(l, entry("uq", 3 * v + y), b0)
                        for k in range(4):
                            a = o + ((2 * k + y) * P if y < 2 else (8 + k) * P)
                            i_ = three(b[:, 0:S], whi[:, a:a + P], wlo[:, a:a + P], ch(qahi, k), ch(qalo, k),
                                       k == 0, k == 3)
                        i_.then_inc(ring_full, 1)
                    fill()
                pe.wait_ge(gelu_done, 2 * l + 2)
                for v in range(2):
                    b = ring(l, entry("vt", v), b0)
                    for y in range(4):
                        k, t_ = 28 + 2 * v + y // 2, y % 2
                        i_ = pe.transpose(b[:, y * P:(y + 1) * P], z[:, k * S + t_ * P:k * S + (t_ + 1) * P], ident)
                    i_.then_inc(ring_full, 1)
                pe.wait_ge(applied, job(l, J_MK) + 1)
                for v in range(3):
                    b = ring(l, entry("mk", v), b0)
                    for y in range(2):
                        h = 2 * v + y
                        i_ = mm(b[:, y * S:(y + 1) * S], ident[0:NH, h:h + 1].to_broadcast([NH, P]),
                                roots(l, J_MK), True, True)
                    i_.then_inc(ring_full, 1)
                fill()
                subs = []
                for v in range(3):
                    subs.append(ms_tokens(l, J_MQ, 2 * v, 1, lambda y, t, v=v: 6 * t + 2 * v + y, one))
                    subs.append(ms_tokens(l, J_MQ, 2 * v + 1, 2, lambda y, t, v=v: 6 * t + 2 * v, halves))
                ms(l, J_MQ, subs)
                pe.wait_ge(rope_in, 2 * l + 2)
                for v in range(3):
                    b = ring(l, entry("qrot", v), b0)
                    mm(b[:, 0:S], rot, ch(mqr, v), True, True).then_inc(ring_full, 1)
                fill()
                for v in range(2):
                    pe.wait_ge(ring_act, evacuated(l, entry("vt", v))[1])
                    b = ring(l, entry("sg", v), b0)
                    for y in range(4):
                        g = 2 * v + y // 2
                        i_ = mm(b[:, y * P:(y + 1) * P], vt[:, (4 * v + y) * P:(4 * v + y + 1) * P],
                                wt[:, l * 512 + g * P:l * 512 + (g + 1) * P], True, True)
                    i_.then_inc(ring_full, 1)

            def score(l, i):
                h = i % NH
                if i == 0:
                    pe.wait_ge(ring_act, (l + 1) * RING_OF["act"])
                    pe.wait_ge(ring_dve, (l + 1) * RING_OF["dve"])
                else:
                    pe.wait_ge(sc_free, 12 * l + i)
                for c0, c1, q0, nk in ((0, P, 0, P), (P, KEYS, P, S)):
                    if i < NH:
                        for y in range(2):
                            i_ = mm(bank[y][:, c0:c1], z[64 * y:64 * y + 64, h * S + q0:h * S + q0 + P],
                                    z[64 * y:64 * y + 64, (NH + h) * S:(NH + h) * S + nk], True, True)
                    else:
                        r0, c_ = 64 * (h % 2), (h // 2) * S
                        mm(bank[0][:, c0:c1], mq[:, h * S + q0:h * S + q0 + P], mk[:, h * S:h * S + nk], True, False)
                        i_ = mm(bank[0][:, c0:c1], mqr[r0:r0 + 64, c_ + q0:c_ + q0 + P],
                                mkr[r0:r0 + 64, c_:c_ + nk], False, True)
                i_.then_inc(sc_full, 1)

            def turn_probabilities(l, i):
                o = (i % 2) * KEYS
                pe.wait_ge(p_ready, 12 * l + i + 1)
                if i >= 1:
                    pe.wait_ge(pt_ready, 12 * l + i)
                for c0 in (0, P, 2 * P):
                    i_ = pe.transpose(B_PT[:, c0:c0 + P], pr[:, o + c0:o + c0 + P], ident)
                i_.then_inc(pt_full, 1)

            def values(l, i):
                h, o = i % NH, (i % 2) * KEYS
                pe.wait_ge(pt_ready, 12 * l + i + 1)
                if i % 2 == 0 and 2 <= i <= NH:
                    pe.wait_ge(o_taken, 3 * l + i // 2)
                elif i % 2 == 0 and i > NH:
                    pe.wait_ge(mh_low, l * NH + i - NH)
                v_, d0 = (vda if i < NH else mv), (i % 2) * S
                mm(B_O[:, d0:d0 + S], v_[:, h * S:h * S + P], pt[:, o:o + S], True, False)
                mm(B_O[:, d0 + P:d0 + S], v_[:, h * S + P:(h + 1) * S], pt[:, o + S:o + KEYS], False, True).then_inc(
                    o_full, 1)

            def heads(l, g):
                def spread(v):
                    pe.wait_ge(applied, job(l, J_O) + 1)
                    if v == 2:
                        pe.wait_ge(spread_free, 3 * l + 1)
                    for y in range(2):
                        h = 2 * v + y
                        i_ = mm(bank[7 - v % 2][:, y * S:(y + 1) * S], ident[0:NH, h:h + 1].to_broadcast([NH, P]),
                                roots(l, J_O), True, True)
                    i_.then_inc(spread_full, 1)

                for i in range(15):
                    if i < 12:
                        score(l, i)
                    if i in (4, 6, 8):
                        ms_rows(l, J_O, con[:, C_ROW1:C_ROW1 + 11], 1, only=(i - 4) // 2)
                    if i == 10:
                        spread(0)
                        spread(1)
                    if i == 11:
                        spread(2)
                    if 2 <= i <= 13:
                        turn_probabilities(l, i - 2)
                    if i < 2 * A_HEADS:
                        for q in range(2):
                            ada_part_later(g + i // 2, 2 * (i % 2) + q)
                    if i % 2 == 0 and i >= 2:
                        ada_turn(g + i // 2 - 1)
                    if 2 <= i <= 13:
                        values(l, i - 2)

            def unit(u, slot, b2, s, kt, rhs, waits, acc_wait, after_chunk):
                pe.wait_ge(lo_ready, u + 1)
                for c_ in range(2):
                    acc = bank[2 * b2 + c_][:, 0:S]
                    if s == 0 and acc_wait is not None:
                        pe.wait_ge(acc_free, acc_wait + c_)
                    for j in range(kt):
                        if waits is not None and c_ == 0:
                            waits(s * kt + j)
                        a = slot * UNIT + j * 256 + c_ * P
                        i_ = three(acc, whi[:, a:a + P], wlo[:, a:a + P], ch(rhs[0], s * kt + j),
                                   ch(rhs[1], s * kt + j), s == 0 and j == 0, s == 1 and j == kt - 1)
                    if c_ == 1:
                        i_.then_inc(unit_done, 1)
                    elif s == 1:
                        i_.then_inc(chunk0_done, 1)
                    after_chunk(c_)

            for l in range(L):
                item = l * T_LAYER
                if l > 0:
                    ms_all(l, J_N1)
                for row in phases[l]:
                    kind, p, first, n, u0, b0, g0 = row
                    if kind == "small":
                        attention_inputs(l, u0, b0, Fill(g0))
                        heads(l, g0 + A_FILL)
                        continue
                    begins = first_of(l, row)
                    if kind == "up" and p == 0 and begins:
                        ms_all(l, J_N2)

                    def input_ready(k):
                        if kind == "win":
                            pe.wait_ge(t_low, item + T_N1 + k + 1)
                        elif kind == "up":
                            pe.wait_ge(t_low, item + T_N2 + k + 1)
                        elif kind == "wout" and k < NH:
                            pe.wait_ge(t_low, item + T_DA + k + 1)
                        elif kind == "wout" and k < 2 * NH:
                            pe.wait_ge(mh_low, l * NH + k - NH + 1)
                        elif kind == "down" and k % 2 == 0:
                            pe.wait_ge(a_low, l * (FFC // 4) + sum(PASS_BLOCKS[:p]) + k // 2 + 1)

                    def body(i, waits):
                        for b2 in range(2):
                            acc_wait = 2 * (b0 + 2 * i + b2) - 3
                            if isinstance(acc_wait, int) and acc_wait <= 0:
                                acc_wait = None
                            for s in range(2):
                                v = 2 * b2 + s

                                def after_chunk(c_):
                                    if g0 is None:
                                        return
                                    if c_ == 0:
                                        ada_part_later(g0 + i, v)
                                    elif v == 3:
                                        ada_turn(g0 + i)

                                unit(u0 + 4 * i + v, (u0 + v) % 2, b2, s, PASS_BLOCKS[p] if kind == "down" else 8,
                                     (hhi, hlo) if kind in ("win", "up") else (mhi, mlo),
                                     waits if b2 == 0 else None, acc_wait, after_chunk)

                    start = 0
                    if begins and not (kind == "up" and p > 0):
                        body(0, input_ready)
                        start = 1
                    if start < n:
                        with pe.Fori(start, n) as i:
                            body(i, None)

            for k2 in range(KC // 2):
                pe.wait_ge(acc_free, residual_final(L, 0, 2 * k2 + 1))
                if k2 >= 2:
                    pe.wait_ge(fin_free, k2 - 1)
                for y in range(4):
                    t_, k = y // 2, 2 * k2 + y % 2
                    i_ = pe.transpose(bank[6 + k2 % 2][:, y * P:(y + 1) * P],
                                      xT[:, k * S + t_ * P:k * S + (t_ + 1) * P], ident)
                i_.then_inc(fin_full, 1)

        @block.scalar
        def _(act):
            act.dma_start(con[:, 0:C_N], consts).then_inc(first_loaded, 16)
            act.dma_start(rows[0:KC, 0:P], c.rearrange("a (k p) -> (a k) p", p=P)).then_inc(first_loaded, 16)
            for l in range(L):
                act.dma_start(rows[0:96, (1 + l) * P:(2 + l) * P],
                              b_ada[l].rearrange("(k p) -> k p", p=P)).then_inc(first_loaded, 16)

            act.wait_ge(pro_free, 1)
            act.activation(sml[:, 32:48], cols[:, 0:KC], ACT.Silu).then_inc(cond_silu, 1)

            def copy(out_, in_):
                return act.activation(out_, in_, ACT.Copy)

            def split_hi(v4, laps):
                act.wait_ge(w_loaded[v4], 16 * (laps + 1))
                o = (v4 % 2) * UNIT
                copy(whi[:, o:o + UNIT], raw[:, v4 * UNIT:(v4 + 1) * UNIT]).then_inc(hi_ready, 1)

            def split_small(l, u0, v):
                u = u0 + v
                before = (entry("kr"), entry("ukv", 4), entry("ukv", 9), entry("uq", 2), entry("uq", 5),
                          entry("uq", 8))[v - 2]
                act.wait_ge(ring_full, l * RING_N + before + 1)
                if v < 3 or v >= 6:
                    split_hi(u % 4, u // 4)
                    return
                act.wait_ge(w_loaded[u % 4], 16 * (u // 4 + 1))
                for src, dst in uq_views(u, whi):
                    i_ = copy(dst, src)
                i_.then_inc(hi_ready, 1)

            def ada_copy(g):
                act.wait_ge(ada_used, 4 * g + 4)
                if not (isinstance(g, int) and g == 0):
                    act.wait_ge(mod_turned, g)
                copy(ya[:, 0:256], B_ADA[:, 0:256]).then_inc(ya_ready, 1)

            def squares(l, j, only=None):
                for v, (t, c0, w) in enumerate(JOB_SQ[j]):
                    if only is not None and v != only:
                        continue
                    s_ = sub(l, j) + v
                    act.wait_ge(sub_done, s_ - 1)
                    if j == J_SGV:
                        act.wait_ge(gelu_done, 2 * l + 2)
                    act.activation(sq[:, (s_ % 2) * 512:(s_ % 2) * 512 + w], t[:, c0:c0 + w], ACT.Square).then_inc(
                        sq_ready, 1)

            def root(l, j):
                g, (rows_, w, n, keep) = job(l, j), JOB_W[j]
                act.wait_ge(sub_done, sub(l, j) + SUBS[j])
                if g >= 2 and keep is None:
                    act.wait_ge(applied, g - 1)
                act.activation(roots(l, j), bank[6 + g % 2][0:rows_, 0:w], ACT.Sqrt,
                               bias=con[0:rows_, C_EPS:C_EPS + 1], scale=1.0 / n).then_inc(root_ready, 1)

            def item_hi(idx, dst):
                act.wait_ge(t_ready, idx + 1)
                copy(dst, ch(T, idx % 4)).then_inc(t_high, 1)

            def trunk_squares(l, j):
                for k in range(KC):
                    s_ = sub(l, j) + k
                    if l == 0 and j == J_N1:
                        act.wait_ge(pro_free, PRO_X + k // 2 + 1)
                    else:
                        act.wait_ge(acc_free, residual_final(l, j == J_N2, k))
                    if s_ >= 2:
                        act.wait_ge(sub_done, s_ - 1)
                    act.activation(sq[:, (s_ % 2) * 512:(s_ % 2) * 512 + S], ch(xT, k), ACT.Square).then_inc(
                        sq_ready, 1)
                root(l, j)

            def trunk(l, j, t0, chunks=range(KC)):
                for k in chunks:
                    idx, shift = l * T_LAYER + t0 + k, 96 * l + 48 * (j == J_N2) + k
                    act.wait_ge(t_ready, idx + 1)
                    act.activation(ch(hhi, k), ch(T, idx % 4), ACT.Identity, bias=mod[:, shift:shift + 1]).then_inc(
                        t_high, 1)

            def attention(l, u0, b0, ga):
                item = l * T_LAYER
                act.wait_ge(acc_free, 2 * b0)
                for j in (J_QA, J_KVA, J_DAQ):
                    squares(l, j)
                    root(l, j)
                for k in range(6):
                    item_hi(item + T_QA + k, ch(qahi, k))

                def ring_bank(e):
                    act.wait_ge(ring_full, l * RING_N + e + 1)
                    return bank[e % 4]

                def ring_copy(e, dst, columns=512, view=lambda b: b):
                    b = ring_bank(e)
                    copy(dst, view(b[:, 0:columns])).then_inc(ring_act, 1)

                b = ring_bank(entry("kr"))
                copy(kr[0:64, 0:S], b[0:64, 0:S])
                act.activation(sqkr[:, 0:S], b[:, 0:S], ACT.Square)
                copy(kr[64:P, 0:S], b[0:64, 0:S]).then_inc(ring_act, 1)
                for v in range(3):
                    ring_copy(entry("v", v), vda[:, v * 512:(v + 1) * 512])
                squares(l, J_DAK)
                root(l, J_DAK)
                ada_copy(ga)
                split_small(l, u0, 2)
                act.activation(ch(z, 24, 4), ch(z, 24, 4), ACT.Gelu_apprx_tanh).then_inc(gelu_done, 1)
                act.activation(ch(z, 28, 4), ch(z, 28, 4), ACT.Gelu_apprx_tanh).then_inc(gelu_done, 1)
                for v in range(2):
                    for y in range(3):
                        ring_copy(entry("ukv", 5 * v + y), ch(mk, 3 * v + y), S)
                    for t_ in range(2):
                        dst = mv[:, 3 * v * S:3 * (v + 1) * S].rearrange("p (h t d) -> p h t d", h=3, t=2)[:, :, t_, :]
                        ring_copy(entry("ukv", 5 * v + 3 + t_), dst, 384,
                                  lambda b: b.rearrange("p (h d) -> p h d", h=3))
                    split_small(l, u0, 3 + v)
                ada_copy(ga + 1)
                for j in (J_SGV, J_MK):
                    squares(l, j)
                    root(l, j)
                ada_copy(ga + 2)
                for v in range(3):
                    ring_copy(entry("uq", 3 * v), ch(mq, 2 * v), S)
                    ring_copy(entry("uq", 3 * v + 1), ch(mq, 2 * v + 1), S)
                    ring_copy(entry("uq", 3 * v + 2), ch(mqr, v), S)
                    split_small(l, u0, 5 + v)
                ada_copy(ga + 3)
                act.wait_ge(applied, job(l, J_SGV) + 1)
                for v in range(2):
                    b = ring_bank(entry("vt", v))
                    for y in range(4):
                        a = R_SG + 4 * (y % 2) + 2 * v + y // 2
                        i_ = act.activation(vt[:, (4 * v + y) * P:(4 * v + y + 1) * P], b[:, y * P:(y + 1) * P],
                                            ACT.Copy, scale=rtok[:, a:a + 1])
                    i_.then_inc(ring_act, 1)
                squares(l, J_MQ)
                root(l, J_MQ)
                ada_copy(ga + 4)
                for g in range(SGG):
                    item_hi(item + T_SG + g, ch(mhi, 12 + g))
                for i in range(15):
                    if i % 2 == 0 and i >= 2:
                        ada_copy(ga + A_FILL + i // 2 - 1)
                    if i == 9:
                        root(l, J_O)
                    if 11 <= i <= 13:
                        for y in range(2):
                            h = 2 * (i - 11) + y
                            item_hi(item + T_DA + h, ch(mhi, h))
                    if i % 2 == 0 and i >= 10:
                        act.wait_ge(o_full, 12 * l + i - 2)
                        for y in range(2):
                            copy(ch(mhi, i - 4 + y), B_O[:, y * S:(y + 1) * S]).then_inc(mh_ready, 1)
                    if 2 <= i <= 13:
                        v = i - 2
                        act.wait_ge(pt_full, 12 * l + v + 1)
                        if v >= 2:
                            act.wait_ge(o_full, 12 * l + v - 1)
                        copy(pt[:, (v % 2) * KEYS:(v % 2 + 1) * KEYS], B_PT[:, 0:KEYS]).then_inc(pt_ready, 1)
                    if i < 12:
                        o, st = (i % 2) * 2 * KEYS, (i % 2) * 16
                        act.wait_ge(max_ready, 12 * l + i + 1)
                        for s_ in range(2 if i < NH else 1):
                            for qb, (c0, c1) in enumerate(((0, P), (P, KEYS))):
                                v = 2 * s_ + qb
                                a = sc_s[:, o + s_ * KEYS + c0:o + s_ * KEYS + c1]
                                i_ = act.activation(a, a, ACT.Exp, bias=stat[:, st + 4 + v:st + 5 + v],
                                                    accum_out=stat[:, st + 8 + v:st + 9 + v])
                        i_.then_inc(exp_done, 1)
                    if i in (3, 5, 7):
                        act.wait_ge(o_full, 12 * l + i - 1)
                        v = (i - 3) // 2
                        squares(l, J_O, v)
                        copy(ch(z, 2 * v, 2), B_O[:, 0:512]).then_inc(o_taken, 1)

            for g in range(A_PRO):
                ada_copy(g)
                if g == 2:
                    trunk_squares(0, J_N1)
                if g == 8:
                    act.wait_ge(lam_sum, 1)
                    act.activation(sml[:, 4:8], sml[:, 0:4], ACT.Exp).then_inc(lam_exp, 1)
                if g - 1 in PRO_CHUNKS:
                    trunk(0, J_N1, T_N1, range(*PRO_CHUNKS[g - 1]))
                if g == A_PRO - 2:
                    split_hi(0, 0)
                    split_hi(1, 0)
                if g == 10:
                    act.wait_ge(ang_ready, 1)
                    act.activation(sin[:, 0:S], ang[:, 0:S], ACT.Sin).then_inc(trig_done, 1)
                    act.activation(cos[:, 0:S], ang[:, S:2 * S], ACT.Sin).then_inc(trig_done, 1)
            trunk(0, J_N1, T_N1, range(*PRO_CHUNKS[A_PRO - 1]))
            for l in range(L):
                if l > 0:
                    trunk_squares(l, J_N1)
                    trunk(l, J_N1, T_N1)
                for row in phases[l]:
                    kind, p, first, n, u0, b0, g0 = row
                    if kind == "small":
                        attention(l, u0, b0, g0)
                        continue
                    if kind == "up" and p == 0 and first_of(l, row):
                        trunk_squares(l, J_N2)
                        trunk(l, J_N2, T_N2)

                    d0 = u0 - dropped(l, kind)

                    def body(i, ending=False):
                        pb = sum(PASS_BLOCKS[:p])
                        pair = l * (FFC // 4) + pb + first + i
                        for b2 in range(2):
                            for c_ in range(2):
                                v = 2 * b2 + 2 + c_
                                if not (ending and b2 == 1):
                                    act.wait_ge(unit_done, d0 + 4 * i + v - 1)
                                    split_hi((u0 + v) % 4, (u0 + v) // 4 + i)
                                if v == 4 and g0 is not None:
                                    ada_copy(g0 + i)
                                if kind not in ("win", "up"):
                                    continue
                                if c_ == 0:
                                    act.wait_ge(chunk0_done, b0 + 2 * i + b2 + 1)
                                else:
                                    act.wait_ge(unit_done, d0 + 4 * i + 2 * b2 + 2)
                                if kind == "win":
                                    copy(ch(z, (first + i) * 4 + 2 * b2 + c_), bank[2 * b2 + c_][:, 0:S]).then_inc(
                                        acc_free, 1)
                                    continue
                                if c_ == 0 and (not isinstance(pair, int) or pair >= 1):
                                    act.wait_ge(a_ready if b2 == 0 else a_low, pair)
                                cc = COL_CONV + 4 * FFC * l + 2 * (pb + first + i) + (FFC // 2) * b2 + c_
                                act.activation(ch(yv if b2 else yg, c_), bank[2 * b2 + c_][:, 0:S], ACT.Identity,
                                               bias=cols[:, bass.ds(cc + 3 * FFC, 1)],
                                               scale=cols[:, bass.ds(cc + 2 * FFC, 1)]).then_inc(tap_ready, 1)
                        if kind == "up":
                            act.wait_ge(acc_free, 2 * (b0 + 2 * i) + 2)
                            act.activation(yg[:, 0:512], yg[:, 0:512], ACT.Silu).then_inc(silu_done, 1)

                    ends = l == L - 1 and row is phases[l][-1]
                    start = 0
                    if kind == "up" and l == 0 and p == 0 and first == 0:
                        body(0)
                        start = 1
                    if n - ends > start:
                        with act.Fori(start, n - ends) as i:
                            body(i)
                    if ends:
                        body(n - 1, True)
            for k2 in range(0, KC // 2, 1):
                act.wait_ge(fin_full, k2 + 1)
                dst = xs[:, 0:2 * D].rearrange("p (t d) -> p t d", t=2)[:, :, k2 * S:(k2 + 1) * S]
                copy(dst, bank[6 + k2 % 2][:, :].rearrange("p (t d) -> p t d", t=2)).then_inc(fin_free, 1)

        @block.vector
        def _(dve):
            order = Order(dve, dve_order)
            stt, ts, tt = dve.scalar_tensor_tensor, dve.tensor_scalar, dve.tensor_tensor

            dve.wait_ge(pro_full, 1)
            dve.tensor_copy(cols[:, 0:KC], bank[0][:, 0:KC])
            dve.tensor_copy(cols[:, COL_BADA:COL_CONV], bank[0][:, 60:252]).then_inc(pro_free, 1)
            dve.wait_ge(cond_silu, 1)
            dve.tensor_copy(condr[:, 0:KC * 32].rearrange("p (k m) -> p k m", m=32),
                            sml[:, 32:48].unsqueeze(2).to_broadcast([P, KC, 32])).then_inc(cond_ready, 1)

            def turned_x():
                for k2 in range(KC // 2):
                    dve.wait_ge(pro_full, PRO_X + k2 + 1)
                    dve.tensor_copy(xT[:, k2 * 512:(k2 + 1) * 512], bank[(PRO_X + k2) % 4][:, :]).then_inc(pro_free, 1)

            def g_(l, what, i=0):
                a = gcol(l, what, i)
                return cols[:, a:a + 1]

            def vectors():
                e = PRO_VEC
                dve.wait_ge(pro_full, e + 1)
                dve.tensor_copy(cols[:, KC:COL_BADA], bank[e % 4][:, KC:COL_BADA]).then_inc(pro_free, 1)
                for l in range(L):
                    e += 1
                    dve.wait_ge(pro_full, e + 1)
                    dve.tensor_copy(cols[:, COL_CONV + 4 * FFC * l:COL_CONV + 4 * FFC * (l + 1)],
                                    bank[e % 4][:, 0:4 * FFC]).then_inc(pro_free, 1)
                for l in range(L):
                    e += 1
                    dve.wait_ge(pro_full, e + 1)
                    tt(wt[:, l * 512:(l + 1) * 512].rearrange("p (g t) -> p g t", g=SGG),
                       bank[e % 4][:, :].rearrange("p (g t) -> p g t", g=SGG),
                       tril.unsqueeze(1).to_broadcast([P, SGG, P]), ALU.mult).then_inc(pro_free, 1)
                dve.wait_ge(pro_free, PRO_VEC + 1)

            def lambdas():
                for l in range(L):
                    tt(sml[:, 50 + l:51 + l], g_(l, "qg"), g_(l, "kg"), ALU.mult)
                    order.after(tt(sml[:, 52 + l:53 + l], g_(l, "mqn"), g_(l, "mkn"), ALU.mult))
                for l in range(L):
                    a = cols[:, gcol(l, "hg"):gcol(l, "hg") + NH]
                    order.after(ts(a, a, 1.0 - LAM_INIT[l], None, ALU.mult))
                lv = lamr[:, 0:L * 4 * DA_QK].rearrange("p (a b d) -> p a b d", b=2, d=DA_QK)
                order.after(tt(lv[:, :, 0, :], lv[:, :, 0, :], lv[:, :, 1, :], ALU.mult))
                dve.tensor_reduce(sml[:, 0:4], lv[:, :, 0, :], AX_X, ALU.add).then_inc(lam_sum, 1)
                dve.wait_ge(lam_exp, 1)
                for l in range(L):
                    order.after(tt(sml[:, 8 + l:9 + l], sml[:, 5 + 2 * l:6 + 2 * l], sml[:, 4 + 2 * l:5 + 2 * l],
                                   ALU.subtract))
                    order.after(ts(sml[:, 8 + l:9 + l], sml[:, 8 + l:9 + l], -LAM_INIT[l], None, ALU.add))

            def places():
                dve.tensor_copy(sml[:, 48:50], posi[:, S:S + 2])
                order.after(dve.tensor_copy(ang[:, 0:S], posi[:, 0:S]))
                ts(dist[:, 0:P], ang[:, 0:P], sml[:, 48:49], None, ALU.subtract)
                order.after(ts(dist[:, P:KEYS], ang[:, 0:S], sml[:, 49:50], None, ALU.subtract))
                order.after(stt(dist[:, 0:KEYS], dist[:, 0:KEYS], -1.0, dist[:, 0:KEYS], ALU.mult, ALU.max))
                order.after(ts(ang[:, 0:S], ang[:, 0:S], con[:, C_INV:C_INV + 1], None, ALU.mult))
                order.after(ts(rt_tmp[:, 0:S], ang[:, 0:S], 1.0 / TURN, ROUND, ALU.mult, ALU.add))
                order.after(ts(rt_tmp[:, 0:S], rt_tmp[:, 0:S], -ROUND, None, ALU.add))
                for part in TURN_PARTS:
                    order.after(stt(ang[:, 0:S], rt_tmp[:, 0:S], -part, ang[:, 0:S], ALU.mult, ALU.add))
                order.after(ts(ang[:, 0:S], ang[:, 0:S], PI_, -PI_, ALU.min, ALU.max))
                order.after(stt(rt_tmp[:, 0:S], ang[:, 0:S], -1.0, ang[:, 0:S], ALU.mult, ALU.max))
                ts(ang[:, S:2 * S], rt_tmp[:, 0:S], -1.0, TURN / 4, ALU.mult, ALU.add).then_inc(ang_ready, 1)

            def split_lo(u, v4):
                dve.wait_ge(hi_ready, u + 1)
                o = (v4 % 2) * UNIT
                tt(wlo[:, o:o + UNIT], raw[:, v4 * UNIT:(v4 + 1) * UNIT], whi[:, o:o + UNIT].bitcast(F32),
                   ALU.subtract).then_inc(lo_ready, 1)

            def split_lo_static(u):
                if u % U_LAYER in UQ_UNITS:
                    dve.wait_ge(hi_ready, u + 1)
                    for (src, dst), (_, hi) in zip(uq_views(u, wlo), uq_views(u, whi)):
                        i_ = tt(dst, src, hi.bitcast(F32), ALU.subtract)
                    i_.then_inc(lo_ready, 1)
                    return
                split_lo(u, u % 4)

            def mod_add(g):
                dve.wait_ge(mod_turned, g + 1)
                at_ = PRO_ORDER[g] if isinstance(g, int) and g < A_PRO else g
                dst = mod[:, bass.ds(2 * at_, 2)]
                tt(dst, B_MOD[:, 0:2], cols[:, bass.ds(COL_BADA + 2 * at_, 2)], ALU.add).then_inc(mod_ready, 1)

            def t_free(idx):
                if idx >= 4:
                    dve.wait_ge(t_low, idx - 3)

            def item_lo(idx, hi, dst):
                dve.wait_ge(t_high, idx + 1)
                tt(dst, ch(T, idx % 4), hi.bitcast(F32), ALU.subtract).then_inc(t_low, 1)

            def inverse(l, j):
                dve.wait_ge(root_ready, job(l, j) + 1)
                a = roots(l, j)
                order.after(dve.reciprocal(a, a))
                return a

            def trunk_chunks(l, t0, m0, a, k0, k1):
                order.after(ts(sml[:, 16 + k0:16 + k1], mod[:, m0 + 16 + k0:m0 + 16 + k1], 1.0, None, ALU.add))
                for k in range(k0, k1 + 1):
                    idx = l * T_LAYER + t0 + k
                    if k < k1:
                        t_free(idx)
                        i_ = stt(ch(T, idx % 4), ch(xT, k), sml[:, 16 + k:17 + k], a, ALU.mult, ALU.mult)
                        i_.then_inc(t_ready, 1)
                    if k > k0:
                        dve.wait_ge(t_high, idx)
                        stt(ch(hlo, k - 1), ch(T, (idx - 1) % 4), mod[:, m0 + k - 1:m0 + k], ch(hhi, k - 1).bitcast(F32),
                            ALU.add, ALU.subtract).then_inc(t_low, 1)

            def trunk(l, j, t0, part):
                dve.wait_ge(mod_ready, A_LAYER * l + 8 * (part + 2))
                trunk_chunks(l, t0, 96 * l + 16 * part, inverse(l, j), 0, KC)
                dve.engine_nop().then_inc(applied, 1)

            def attention(l, u0, b0, ga):
                item = l * T_LAYER
                for j, t0, n, z0, what in ((J_QA, T_QA, 4, 18, "qa"), (J_KVA, T_KVA, 2, 22, "kva")):
                    a = inverse(l, j)
                    for k in range(n + 1):
                        idx = item + t0 + k
                        if k < n:
                            t_free(idx)
                            stt(ch(T, idx % 4), ch(z, z0 + k), g_(l, what, k), a, ALU.mult, ALU.mult).then_inc(t_ready, 1)
                        if k >= 1:
                            c_ = k - 1 + (4 if j == J_KVA else 0)
                            item_lo(idx - 1, ch(qahi, c_), ch(qalo, c_))
                    dve.engine_nop().then_inc(applied, 1)
                def inverse_tokens(j, scale=None):
                    a = inverse(l, j)
                    if scale is not None:
                        order.after(ts(a, a, scale, None, ALU.mult))
                    dve.engine_nop().then_inc(applied, 1)

                def inverse_rows(j):
                    inverse(l, j)
                    dve.engine_nop().then_inc(applied, 1)

                def ring_wait(e):
                    dve.wait_ge(ring_full, l * RING_N + e + 1)
                    return bank[e % 4]

                def rotate(e, t):
                    b = ring_wait(e)
                    tt(rt_tmp[:, 0:S], b[:, 0:S], sin[:, 0:S], ALU.mult)
                    order.after(tt(t, t, cos[:, 0:S], ALU.mult))
                    tt(t, t, rt_tmp[:, 0:S], ALU.add).then_inc(ring_dve, 1)
                    dve.wait_ge(ring_dve, evacuated(l, e)[1])

                split_lo_static(u0 + 2)
                mod_add(ga)
                inverse_tokens(J_DAQ, DA_SCALE)
                inverse_rows(J_DAK)
                dve.wait_ge(ring_act, evacuated(l, entry("kr"))[1])
                ts(kr[:, 0:S], kr[:, 0:S], g_(l, "mkr"), None, ALU.mult).then_inc(rope_in, 1)
                split_lo_static(u0 + 3)
                split_lo_static(u0 + 4)
                rotate(entry("krot"), kr[:, 0:S])
                for v in range(3):
                    b = ring_wait(entry("dak", v))
                    a = ch(z, NH + 2 * v, 2)
                    stt(a, a, sml[:, 50 + l:51 + l], b[:, :], ALU.mult, ALU.mult).then_inc(ring_dve, 1)
                mod_add(ga + 1)
                inverse_tokens(J_SGV)
                inverse_rows(J_MK)
                split_lo_static(u0 + 5)
                mod_add(ga + 2)
                split_lo_static(u0 + 6)
                split_lo_static(u0 + 7)
                mod_add(ga + 3)
                for v in range(3):
                    b = ring_wait(entry("mk", v))
                    for y in range(2):
                        tt(mkr[64 * y:64 * y + 64, v * S:(v + 1) * S], kr[64 * y:64 * y + 64, 0:S],
                           b[64 * y:64 * y + 64, y * S:(y + 1) * S], ALU.mult)
                    stt(ch(mk, 2 * v, 2), ch(mk, 2 * v, 2), sml[:, 52 + l:53 + l], b[:, :], ALU.mult,
                        ALU.mult).then_inc(ring_dve, 1)
                inverse_tokens(J_MQ, MLA_SCALE)
                ts(mqr[:, 0:3 * S], mqr[:, 0:3 * S], g_(l, "mqr"), None, ALU.mult).then_inc(rope_in, 1)
                dve.wait_ge(rope_in, 2 * l + 2)
                for v in range(3):
                    rotate(entry("qrot", v), ch(mqr, v))
                mod_add(ga + 4)
                for v in range(2):
                    b = ring_wait(entry("sg", v))
                    bias = bs[:, l * 512 + v * S:l * 512 + (v + 1) * S].rearrange("p (g t) -> p g t", g=2)
                    ts_ = [ch(T, (T_SG + 2 * v + y) % 4) for y in range(2)]
                    t_free(item + T_SG + 2 * v + 1)
                    for y in range(2):
                        i_ = stt(ts_[y].rearrange("p (n t) -> p n t", n=2),
                                 b[:, y * S:(y + 1) * S].rearrange("p (n t) -> p n t", n=2), g_(l, "sgv", 2 * v + y),
                                 bias[:, y, :].unsqueeze(1).to_broadcast([P, 2, P]), ALU.mult, ALU.add)
                    i_.then_inc(ring_dve, 1)
                    dve.wait_ge(ring_dve, evacuated(l, entry("sg", v))[1])
                    for y in range(2):
                        tt(ts_[y], ts_[y], ch(z, 24 + 2 * v + y), ALU.mult).then_inc(t_ready, 1)
                    for y in range(2):
                        k = 2 * v + y
                        item_lo(item + T_SG + k, ch(mhi, 12 + k), ch(mlo, 12 + k))

                def maxima(i):
                    ns, o, st = (2 if i < NH else 1), (i % 2) * 2 * KEYS, (i % 2) * 16
                    dve.wait_ge(sc_full, 12 * l + i + 1)
                    if i >= 2:
                        dve.wait_ge(p_ready, 12 * l + i - 1)
                    for s_ in range(ns):
                        for qb, (c0, c1) in enumerate(((0, P), (P, KEYS))):
                            a = R_DA + 12 * qb + 2 * i + s_ if i < NH else R_MQ + 6 * qb + i - NH
                            i_ = stt(sc_s[:, o + s_ * KEYS + c0:o + s_ * KEYS + c1], bank[s_][:, c0:c1],
                                     rtok[:, a:a + 1], mask[:, c0:c1], ALU.mult, ALU.add)
                    i_.then_inc(sc_free, 1)
                    dve.wait_ge(sc_free, 12 * l + i + 1)
                    if i < NH:
                        for s_ in range(2):
                            a = sc_s[:, o + s_ * KEYS:o + (s_ + 1) * KEYS]
                            i_ = stt(a, dist[:, 0:KEYS], -SLOPES[i], a, ALU.mult, ALU.add)
                        order.after(i_)
                    for s_ in range(ns):
                        for qb, (c0, c1) in enumerate(((0, P), (P, KEYS))):
                            v = 2 * s_ + qb
                            i_ = dve.tensor_reduce(stat[:, st + v:st + v + 1],
                                                   sc_s[:, o + s_ * KEYS + c0:o + s_ * KEYS + c1], AX_X, ALU.max)
                    order.after(i_)
                    ts(stat[:, st + 4:st + 4 + 2 * ns], stat[:, st:st + 2 * ns], -1.0, None, ALU.mult).then_inc(
                        max_ready, 1)

                def probabilities(i):
                    ns, o, st = (2 if i < NH else 1), (i % 2) * 2 * KEYS, (i % 2) * 16
                    dve.wait_ge(exp_done, 12 * l + i + 1)
                    order.after(dve.reciprocal(stat[:, st + 12:st + 12 + 2 * ns], stat[:, st + 8:st + 8 + 2 * ns]))
                    if i < NH:
                        a = stat[:, st + 14:st + 16]
                        order.after(ts(a, a, sml[:, 8 + l:9 + l], None, ALU.mult))
                    if i >= 2:
                        dve.wait_ge(pt_full, 12 * l + i - 1)
                    for s_ in reversed(range(ns)):
                        for qb, (c0, c1) in enumerate(((0, P), (P, KEYS))):
                            dst = pr[:, (i % 2) * KEYS + c0:(i % 2) * KEYS + c1]
                            e_ = sc_s[:, o + s_ * KEYS + c0:o + s_ * KEYS + c1]
                            cf = stat[:, st + 12 + 2 * s_ + qb:st + 13 + 2 * s_ + qb]
                            if s_ == ns - 1:
                                i_ = ts(dst, e_, cf, None, ALU.mult)
                            else:
                                i_ = stt(dst, e_, cf, dst, ALU.mult, ALU.add)
                        if s_ == 0:
                            i_.then_inc(p_ready, 1)
                        else:
                            order.after(i_)

                for i in range(15):
                    if i < 12:
                        maxima(i)
                    if 10 <= i <= 12:
                        v = i - 10
                        dve.wait_ge(spread_full, 3 * l + v + 1)
                        for y in range(2):
                            h = 2 * v + y
                            t_free(item + T_DA + h)
                            i_ = stt(ch(T, (T_DA + h) % 4), ch(z, h), g_(l, "hg", h),
                                     bank[7 - v % 2][:, y * S:(y + 1) * S], ALU.mult, ALU.mult)
                            i_.then_inc(t_ready, 1)
                        dve.engine_nop().then_inc(spread_free, 1)
                    if 11 <= i <= 13:
                        for h in (2 * (i - 11), 2 * (i - 11) + 1):
                            item_lo(item + T_DA + h, ch(mhi, h), ch(mlo, h))
                    if i % 2 == 0 and i >= 10:
                        dve.wait_ge(mh_ready, l * NH + i - 8)
                        for y in range(2):
                            h = i - 10 + y
                            tt(ch(mlo, NH + h), B_O[:, y * S:(y + 1) * S], ch(mhi, NH + h).bitcast(F32),
                               ALU.subtract).then_inc(mh_low, 1)
                    if 1 <= i <= 12:
                        probabilities(i - 1)
                    if i == 9:
                        inverse_rows(J_O)
                    if i % 2 == 0 and i >= 2:
                        mod_add(ga + A_FILL + i // 2 - 1)

            for g in range(A_PRO):
                mod_add(g)
                if g == 1:
                    turned_x()
                if g == 2:
                    first_inverse = inverse(0, J_N1)
                if g == 4:
                    vectors()
                if g == 7:
                    lambdas()
                if g == 9:
                    places()
                if g == min(PRO_CHUNKS):
                    dve.wait_ge(trig_done, 2)
                if g in PRO_CHUNKS:
                    dve.wait_ge(mod_ready, g + 1)
                    trunk_chunks(0, T_N1, 0, first_inverse, *PRO_CHUNKS[g])
                if g == A_PRO - 2:
                    split_lo_static(0)
                    split_lo_static(1)
            dve.engine_nop().then_inc(applied, 1)
            for l in range(L):
                if l > 0:
                    trunk(l, J_N1, T_N1, 0)
                for row in phases[l]:
                    kind, p, first, n, u0, b0, g0 = row
                    if kind == "small":
                        attention(l, u0, b0, g0)
                        continue
                    if kind == "up" and p == 0 and first_of(l, row):
                        trunk(l, J_N2, T_N2, 3)
                    if kind in ("wout", "down"):
                        dve.wait_ge(mod_ready, A_LAYER * l + (24 if kind == "wout" else 48))
                    pb = sum(PASS_BLOCKS[:p])
                    d0 = u0 - dropped(l, kind)
                    links = {"up": 4, "down": 0, "wout": 0, "win": 0}[kind]

                    def body(i, ending=False):
                        n0 = order.n
                        order.plus = links * i
                        for b2 in range(2):
                            for c_ in range(2):
                                v = 2 * b2 + 2 + c_
                                if not (ending and b2 == 1):
                                    split_lo(u0 + 4 * i + v, (u0 + v) % 4)
                                if kind == "win":
                                    continue
                                acc = bank[2 * b2 + c_]
                                if kind == "up":
                                    dve.wait_ge(tap_ready, tap0 + 4 * i + 2 * b2 + c_ + 1)
                                    y_ = ch(yv if b2 else yg, c_)
                                    cc = COL_CONV + 4 * FFC * l + 2 * (pb + first + i) + (FFC // 2) * b2 + c_
                                    order.after(stt(y_[:, 1:S], acc[:, 0:S - 1], cols[:, bass.ds(cc + FFC, 1)],
                                                    y_[:, 1:S], ALU.mult, ALU.add))
                                    stt(y_[:, 2:S], acc[:, 0:S - 2], cols[:, bass.ds(cc, 1)],
                                        y_[:, 2:S], ALU.mult, ALU.add).then_inc(acc_free, 1)
                                else:
                                    if c_ == 0:
                                        dve.wait_ge(chunk0_done, b0 + 2 * i + b2 + 1)
                                    else:
                                        dve.wait_ge(unit_done, d0 + 4 * i + 2 * b2 + 2)
                                    k = 4 * (first + i) + 2 * b2 + c_
                                    gate = 96 * l + 16 * (2 if kind == "wout" else 5) + k
                                    xa = xT[:, bass.ds(k * S, S)]
                                    stt(xa, acc[:, 0:S], mod[:, bass.ds(gate, 1)], xa, ALU.mult, ALU.add).then_inc(
                                        acc_free, 1)
                        if g0 is not None:
                            mod_add(g0 + i)
                        assert order.n - n0 == links
                        order.plus = 0
                        return n0

                    pair0 = l * (FFC // 4) + pb + first
                    tap0 = 4 * pair0
                    ends = l == L - 1 and row is phases[l][-1]
                    m = n - ends
                    if m > 0:
                        with dve.Fori(0, m) as i:
                            n0 = body(i)
                        order.n = n0 + links * m
                    if ends:
                        body(n - 1, True)


_INS = ['x', 'c', 'positions', 'w_ada', 'b_ada', 'w_in', 'da_q_gain', 'da_k_gain', 'da_lq1', 'da_lk1', 'da_lq2',
        'da_lk2', 'da_head_gain', 'mla_q_a_gain', 'mla_w_uq', 'mla_kv_a_gain', 'mla_w_ukv', 'mla_q_gain',
        'mla_k_gain', 'sg_v_gain', 'sg_w', 'sg_b', 'w_out', 'ffn_w_up', 'ffn_conv_w', 'ffn_conv_b', 'ffn_w_down']


def shape_constants():
    a = np.zeros((P, C_N), np.float32)
    p = np.arange(P)[:, None]
    f = np.arange(P)[None, :]
    a[:, C_ID:C_ID + P] = p == f
    a[:, C_ONE:C_ONE + P] = 1.0
    a[:, C_BLK:C_BLK + P] = p // 64 == f // 64
    a[:, C_ROW2 + 10] = p[:, 0] < 64
    a[:, C_ROW2 + 11] = p[:, 0] >= 64
    a[:, C_ROW1 + 5] = 1.0
    a[:, C_ROT:C_ROT + P] = np.where((f % 64 < 32) & (p == f + 32), -1.0, 0.0) + np.where(
        (f % 64 >= 32) & (p == f - 32), 1.0, 0.0)
    a[:, C_TRIL:C_TRIL + P] = p <= f
    for c0, q0, n in ((0, 0, P), (P, P, S)):
        k = np.arange(n)[None, :]
        a[:, C_MASK + c0:C_MASK + c0 + n] = np.where(k // 64 <= (q0 + p) // 64, 0.0, -1e30)
    a[::32, C_SEL] = 1.0
    a[:, C_INV] = np.float32(10000.0) ** (-(np.arange(P) % 32).astype(np.float32) / np.float32(32))
    a[:, C_EPS] = EPS
    return a


def kernel(**inputs):
    import concourse.bacc as _bacc
    from concourse.bass_utils import run_bass_kernel_spmd as _run

    nc = _bacc.Bacc("TRN2", target_bir_lowering=False, num_devices=1)
    arrays, args = {}, []
    for name in ['consts'] + _INS:
        a = shape_constants() if name == 'consts' else np.ascontiguousarray(inputs[name])
        if name == 'x':
            a = a.reshape(S, D)
        arrays[f"in_{name}_dram"] = a
        args.append(nc.dram_tensor(f"in_{name}_dram", a.shape, mybir.dt.from_np(a.dtype), kind="ExternalInput").ap())
    args.append(nc.dram_tensor("out_0_dram", (S, D), F32, kind="ExternalOutput").ap())
    bass_trunk(nc, *args)
    res = _run(nc, [arrays], core_ids=[0])
    return res.results[0]["out_0_dram"].reshape(1, S, D)
```
